# Optimizing a Trainium2 kernel written in Bass

```python
import jax, jax.numpy as jnp
from jax import lax
import numpy as np

D_MODEL = 2048
BATCH = 1
SEQ = 512
DEPTH = 1
DEC_BATCH = 8
DEC_SEQ = 1
PAST_LEN = 4096
PAGE_SIZE = 128

A_HEADS = 8
A_WIDTH = D_MODEL // 2
A_HEAD_DIM = A_WIDTH // A_HEADS
SGU_CHUNK = 128
B_HEADS = 4
B_VAL_WIDTH = D_MODEL - A_WIDTH
B_VAL_DIM = B_VAL_WIDTH // B_HEADS
B_KEY_DIM = B_VAL_DIM // 2
B_KEY_WIDTH = B_HEADS * B_KEY_DIM
GATE_RANK = 16
GATE_TAU = 16.0
GLA_CHUNK = 64
MIX_WIDTH = A_WIDTH + B_VAL_WIDTH
IN_SIZES = (2 * A_WIDTH, B_KEY_WIDTH, B_KEY_WIDTH, B_VAL_WIDTH, B_VAL_WIDTH, GATE_RANK)
IN_COLS = 2 * A_WIDTH + 2 * B_KEY_WIDTH + 2 * B_VAL_WIDTH + GATE_RANK
IN_SPLITS = [2 * A_WIDTH, 2 * A_WIDTH + B_KEY_WIDTH, 2 * A_WIDTH + 2 * B_KEY_WIDTH,
             2 * A_WIDTH + 2 * B_KEY_WIDTH + B_VAL_WIDTH, 2 * A_WIDTH + 2 * B_KEY_WIDTH + 2 * B_VAL_WIDTH]
MEM_LEN = 256
X_HEADS = 4
X_HEAD_DIM = D_MODEL // X_HEADS
N_KEYS = 128
N_EXPERTS = N_KEYS * N_KEYS
PEER_HEADS = 8
PEER_QDIM = 256
PEER_HALF = PEER_QDIM // 2
PEER_TOPK = 16
PEER_BLOCK = 256
EPS = 1e-6

kernel_name = "hybrid_sgu_gla_peer_memxattn_step"

def rmsnorm(x, g):
    xf = x.astype(jnp.float32)
    y = xf * lax.rsqrt(jnp.mean(xf * xf, axis=-1, keepdims=True) + EPS)
    return (y * g.astype(jnp.float32)).astype(x.dtype)

def spatial_gate(u, v, w_s, b_s):
    bsz, L, H, P = v.shape
    c = min(L, SGU_CHUNK)
    pad = (-L) % c
    n = (L + pad) // c
    vc = jnp.pad(v, ((0, 0), (0, pad), (0, 0), (0, 0))).reshape(bsz, n, c, H, P)
    causal = jnp.tril(jnp.ones((c, c), dtype=bool))
    w = jnp.where(causal, w_s[:, :c, :c], 0).astype(v.dtype)
    bias = b_s[:, :c].T.astype(v.dtype)[None, None, :, :, None]
    mixed = jnp.einsum('hts,bnshp->bnthp', w, vc) + bias
    mixed = mixed.reshape(bsz, n * c, H, P)[:, :L]
    return u * mixed

def gla_chunk(state, inp):
    q, k, v, lg = inp
    C = q.shape[2]
    G = jnp.cumsum(lg, axis=2)
    causal = jnp.tril(jnp.ones((C, C), dtype=bool))[:, :, None]
    diff = G[:, :, :, None, :] - G[:, :, None, :, :]
    decay = jnp.exp(jnp.where(causal, diff, -jnp.inf))
    scores = jnp.einsum('bhtd,bhsd,bhtsd->bhts', q, k, decay)
    o = jnp.einsum('bhts,bhsv->bhtv', scores, v) + jnp.einsum('bhtd,bhdv->bhtv', q * jnp.exp(G), state)
    g_last = G[:, :, -1:, :]
    k_dec = k * jnp.exp(g_last - G)
    new_state = jnp.exp(g_last[:, :, 0, :])[..., None] * state + jnp.einsum('bhsd,bhsv->bhdv', k_dec, v)
    return new_state, o

def gla_scan(state, q, k, v, lg):
    bsz, L, H, _ = q.shape
    c = min(L, GLA_CHUNK)
    pad = (-L) % c
    n = (L + pad) // c

    def chunks(a):
        a = jnp.pad(a.astype(jnp.float32), ((0, 0), (0, pad), (0, 0), (0, 0)))
        return a.reshape(bsz, n, c, H, a.shape[-1]).transpose(1, 0, 3, 2, 4)

    new_state, o = lax.scan(gla_chunk, state.astype(jnp.float32), (chunks(q), chunks(k), chunks(v), chunks(lg)))
    o = o.transpose(1, 0, 3, 2, 4).reshape(bsz, n * c, H, -1)[:, :L]
    return new_state, o

def head_group_mixer(h, gla_state, w_in, w_alpha, b_alpha, w_s, b_s, g_sgu, g_gla, w_out):
    bsz, L, _ = h.shape
    z = h @ w_in
    za, zq, zk, zv, zr, zg = jnp.split(z, IN_SPLITS, axis=-1)
    za = jax.nn.gelu(za)
    u, va = jnp.split(za, 2, axis=-1)
    u = u.reshape(bsz, L, A_HEADS, A_HEAD_DIM)
    va = rmsnorm(va.reshape(bsz, L, A_HEADS, A_HEAD_DIM), g_sgu)
    a_out = spatial_gate(u, va, w_s, b_s).reshape(bsz, L, A_WIDTH)
    start = ((L - 1) // SGU_CHUNK) * SGU_CHUNK
    chunk_v = va[:, start:]
    q = zq.reshape(bsz, L, B_HEADS, B_KEY_DIM) * (B_KEY_DIM ** -0.5)
    k = zk.reshape(bsz, L, B_HEADS, B_KEY_DIM)
    vb = zv.reshape(bsz, L, B_HEADS, B_VAL_DIM)
    lg = jax.nn.log_sigmoid((zg @ w_alpha + b_alpha).astype(jnp.float32)) / GATE_TAU
    lg = lg.reshape(bsz, L, B_HEADS, B_KEY_DIM)
    new_state, o = gla_scan(gla_state, q, k, vb, lg)
    o = rmsnorm(o, g_gla).astype(h.dtype).reshape(bsz, L, B_VAL_WIDTH)
    b_out = jax.nn.silu(zr) * o
    y = jnp.concatenate([a_out.astype(h.dtype), b_out], axis=-1) @ w_out
    return y, new_state.astype(gla_state.dtype), chunk_v

def mem_kv(mem, g_mem, w_xk, w_xv):
    bsz = mem.shape[0]
    m = rmsnorm(mem, g_mem)
    k = (m @ w_xk).reshape(bsz, MEM_LEN, X_HEADS, X_HEAD_DIM)
    v = (m @ w_xv).reshape(bsz, MEM_LEN, X_HEADS, X_HEAD_DIM)
    return k, v

def mem_attend(h, mem_k, mem_v, w_xq, w_xo):
    bsz, L, _ = h.shape
    q = (h @ w_xq).reshape(bsz, L, X_HEADS, X_HEAD_DIM)
    s = jnp.einsum('blhd,bmhd->bhlm', q, mem_k).astype(jnp.float32) * (X_HEAD_DIM ** -0.5)
    p = jax.nn.softmax(s, axis=-1).astype(mem_v.dtype)
    o = jnp.einsum('bhlm,bmhd->blhd', p, mem_v).reshape(bsz, L, D_MODEL)
    return o @ w_xo

def peer(h, w_pq, sub_keys, u_emb, v_emb):
    bsz, L, D = h.shape
    x = h.reshape(-1, D)
    T = x.shape[0]
    q = (x @ w_pq).reshape(T, PEER_HEADS, 2, PEER_HALF)
    s = jnp.einsum('thcd,hcnd->thcn', q, sub_keys).astype(jnp.float32)
    sv, si = lax.top_k(s, PEER_TOPK)
    cand = (sv[:, :, 0, :, None] + sv[:, :, 1, None, :]).reshape(T, PEER_HEADS, -1)
    cidx = (si[:, :, 0, :, None] * N_KEYS + si[:, :, 1, None, :]).reshape(T, PEER_HEADS, -1)
    top_s, pos = lax.top_k(cand, PEER_TOPK)
    idx = jnp.take_along_axis(cidx, pos, axis=-1).reshape(T, -1)
    g = jax.nn.softmax(top_s, axis=-1).reshape(T, -1).astype(h.dtype)
    tb = min(PEER_BLOCK, T)
    pad = (-T) % tb
    xb = jnp.pad(x, ((0, pad), (0, 0))).reshape(-1, tb, D)
    ib = jnp.pad(idx, ((0, pad), (0, 0))).reshape(-1, tb, idx.shape[-1])
    gb = jnp.pad(g, ((0, pad), (0, 0))).reshape(-1, tb, g.shape[-1])

    def block(args):
        xt, it, gt = args
        ue = jnp.take(u_emb, it, axis=0)
        ve = jnp.take(v_emb, it, axis=0)
        act = jax.nn.gelu(jnp.einsum('td,ted->te', xt, ue)) * gt
        return jnp.einsum('te,ted->td', act, ve)

    out = lax.map(block, (xb, ib, gb)).reshape(-1, D)[:T]
    return out.reshape(bsz, L, D)

def trunk_layer(x, gla_state, mem_k, mem_v, g_mix, w_in, w_alpha, b_alpha, w_s, b_s, g_sgu, g_gla, w_out,
                g_xq, w_xq, w_xo, g_ffn, w_pq, sub_keys, u_emb, v_emb):
    y, new_state, chunk_v = head_group_mixer(rmsnorm(x, g_mix), gla_state, w_in, w_alpha, b_alpha,
                                             w_s, b_s, g_sgu, g_gla, w_out)
    x = x + y
    x = x + mem_attend(rmsnorm(x, g_xq), mem_k, mem_v, w_xq, w_xo)
    x = x + peer(rmsnorm(x, g_ffn), w_pq, sub_keys, u_emb, v_emb)
    return x, new_state, chunk_v

def setup_inputs(seed: int = 0) -> dict:
    key = jax.random.key(seed)
    ks = jax.random.split(key, 32)

    def nrm(k, shape, scale):
        return jax.random.normal(k, shape, dtype=jnp.float32) * scale

    def gain(k, shape):
        return 1.0 + nrm(k, shape, 0.05)

    L = DEPTH
    return {
        "x_prompt": nrm(ks[0], (BATCH, SEQ, D_MODEL), 1.0),
        "x_sample": nrm(ks[1], (DEC_BATCH, DEC_SEQ, D_MODEL), 1.0),
        "mem_prompt": nrm(ks[2], (BATCH, MEM_LEN, D_MODEL), 1.0),
        "cache_mem_k": nrm(ks[3], (L, DEC_BATCH, MEM_LEN, X_HEADS, X_HEAD_DIM), 1.0),
        "cache_mem_v": nrm(ks[4], (L, DEC_BATCH, MEM_LEN, X_HEADS, X_HEAD_DIM), 1.0),
        "state_gla": nrm(ks[5], (L, DEC_BATCH, B_HEADS, B_KEY_DIM, B_VAL_DIM), 0.1),
        "g_mix": gain(ks[6], (L, D_MODEL)),
        "w_in": nrm(ks[7], (L, D_MODEL, IN_COLS), D_MODEL ** -0.5),
        "w_alpha": nrm(ks[8], (L, GATE_RANK, B_KEY_WIDTH), GATE_RANK ** -0.5),
        "b_alpha": nrm(ks[9], (L, B_KEY_WIDTH), 0.1),
        "w_s": nrm(ks[10], (L, A_HEADS, SGU_CHUNK, SGU_CHUNK), SGU_CHUNK ** -0.5),
        "b_s": gain(ks[11], (L, A_HEADS, SGU_CHUNK)),
        "g_sgu": gain(ks[12], (L, A_HEADS, A_HEAD_DIM)),
        "g_gla": gain(ks[13], (L, B_HEADS, B_VAL_DIM)),
        "w_out": nrm(ks[14], (L, MIX_WIDTH, D_MODEL), MIX_WIDTH ** -0.5),
        "g_mem": gain(ks[15], (L, D_MODEL)),
        "w_xk": nrm(ks[16], (L, D_MODEL, D_MODEL), D_MODEL ** -0.5),
        "w_xv": nrm(ks[17], (L, D_MODEL, D_MODEL), D_MODEL ** -0.5),
        "g_xq": gain(ks[18], (L, D_MODEL)),
        "w_xq": nrm(ks[19], (L, D_MODEL, D_MODEL), D_MODEL ** -0.5),
        "w_xo": nrm(ks[20], (L, D_MODEL, D_MODEL), D_MODEL ** -0.5),
        "g_ffn": gain(ks[21], (L, D_MODEL)),
        "w_pq": nrm(ks[22], (L, D_MODEL, PEER_HEADS * PEER_QDIM), D_MODEL ** -0.5),
        "sub_keys": nrm(ks[23], (L, PEER_HEADS, 2, N_KEYS, PEER_HALF), PEER_HALF ** -0.5),
        "u_emb": nrm(ks[24], (L, N_EXPERTS, D_MODEL), D_MODEL ** -0.5),
        "v_emb": nrm(ks[25], (L, N_EXPERTS, D_MODEL), 0.5),
        "g_final": gain(ks[26], (D_MODEL,)),
    }

def reference(x_prompt, x_sample, mem_prompt, cache_mem_k, cache_mem_v, state_gla, g_mix, w_in, w_alpha, b_alpha,
              w_s, b_s, g_sgu, g_gla, w_out, g_mem, w_xk, w_xv, g_xq, w_xq, w_xo, g_ffn, w_pq, sub_keys,
              u_emb, v_emb, g_final):
    xp = x_prompt
    xs = x_sample
    mk_list, mv_list, stp_list, sts_list, cvp_list, cvs_list = [], [], [], [], [], []
    for l in range(DEPTH):
        lp = (g_mix[l], w_in[l], w_alpha[l], b_alpha[l], w_s[l], b_s[l], g_sgu[l], g_gla[l], w_out[l],
              g_xq[l], w_xq[l], w_xo[l], g_ffn[l], w_pq[l], sub_keys[l], u_emb[l], v_emb[l])
        mk, mv = mem_kv(mem_prompt, g_mem[l], w_xk[l], w_xv[l])
        init_state = jnp.zeros((xp.shape[0], B_HEADS, B_KEY_DIM, B_VAL_DIM), dtype=xp.dtype)
        xp, st_p, cv_p = trunk_layer(xp, init_state, mk, mv, *lp)
        xs, st_s, cv_s = trunk_layer(xs, state_gla[l], cache_mem_k[l], cache_mem_v[l], *lp)
        mk_list.append(mk)
        mv_list.append(mv)
        stp_list.append(st_p)
        sts_list.append(st_s)
        cvp_list.append(cv_p)
        cvs_list.append(cv_s)
    y_prompt = rmsnorm(xp, g_final)
    y_sample = rmsnorm(xs, g_final)
    mem_k_prompt = jnp.stack(mk_list)
    mem_v_prompt = jnp.stack(mv_list)
    state_gla_prompt = jnp.stack(stp_list)
    state_gla_sample = jnp.stack(sts_list)
    chunk_v_prompt = jnp.stack(cvp_list)
    chunk_v_sample = jnp.stack(cvs_list)
    return (y_prompt, y_sample, mem_k_prompt, mem_v_prompt, state_gla_prompt, state_gla_sample, chunk_v_prompt, chunk_v_sample)


_drawn_inputs = setup_inputs


def setup_inputs(seed=0):
    import zlib

    import numpy as np

    out = dict(_drawn_inputs(seed))
    spreads = {}
    factors = {}
    for name, (base, spread) in spreads.items():
        noise = np.random.default_rng([zlib.crc32(name.encode()), seed]).standard_normal(out[name].shape)
        drawn = base * np.exp(spread * noise) if base else spread * noise
        out[name] = __import__('jax').numpy.asarray(drawn.astype(out[name].dtype))
    for name, factor in factors.items():
        out[name] = (out[name] * factor).astype(out[name].dtype)
    return out
```

```python
from contextlib import ExitStack

import numpy as np

import concourse.bass as bass
from concourse import mybir

F32 = mybir.dt.float32
U32 = mybir.dt.uint32
ALU = mybir.AluOpType
ACT = mybir.ActivationFunctionType
AX = mybir.AxisListType.X

P = 128
EPS = 1e-6
TAU = 16.0
SUB = 32
REF = 15
NEG = -3.0e38


class Chain:

    def __init__(self, eng, sem):
        self.eng, self.sem, self.base, self.local = eng, sem, 0, 0

    def link(self, ins):
        ins.then_inc(self.sem, 1)
        self.local += 1
        self.eng.wait_ge(self.sem, self.base + self.local)

    def enter(self, i, per):
        state = (self.base, self.local, per)
        self.base, self.local = i * per + (self.base + self.local), 0
        return state

    def leave(self, state, count):
        assert self.local == state[2], (self.local, state[2])
        self.base, self.local = state[0], state[1] + count * state[2]


def program(nc, x_prompt, x_sample, mem_prompt, cache_mem_k, cache_mem_v, state_gla, g_mix, w_in, w_alpha,
            b_alpha, w_s, b_s, g_sgu, g_gla, w_out, g_mem, w_xk, w_xv, g_xq, w_xq, w_xo, g_ffn, w_pq,
            sub_keys, u_emb, v_emb, g_final,
            y_prompt, y_sample, mem_k_out, mem_v_out, state_p_out, state_s_out, chunk_p_out, chunk_s_out):
    D = x_prompt.shape[2]
    TP = x_prompt.shape[1]
    TS = x_sample.shape[0]
    T = TP + TS
    HALF = T // 2
    KD = D // P
    NT = TP // P
    M = mem_prompt.shape[1]
    AH = w_s.shape[1]
    BH = state_gla.shape[2]
    BV = state_gla.shape[4]
    NV = BV // P
    XH = cache_mem_k.shape[3]
    XD = cache_mem_k.shape[4]
    XK = XD // P
    PH = sub_keys.shape[1]
    TOPK = 16
    E = PH * TOPK
    RANK = w_alpha.shape[1]
    NSUB = P // SUB
    KF = sum(NT * SUB * (i + 1) for i in range(NSUB))
    assert NT == 4 and KD == 16 and TS == 8 and E == P and T % 2 == 0

    with ExitStack() as ctx:
        def sb(name, shape, dt=F32):
            return ctx.enter_context(nc.sbuf_tensor(name, shape, dt))

        def sem(name):
            return ctx.enter_context(nc.semaphore(name))

        xh = sb("xh", [P, 2, KD, T])
        xT, hT = xh[:, 0], xh[:, 1]
        mT = sb("mT", [P, KD, T])
        m2 = mT[:, :, :].rearrange("p k (a t) -> p k a t", a=2)
        x2 = xh[:, 0].rearrange("p k (a t) -> p k a t", a=2)
        hflat = xh[:, 1].rearrange("p k t -> p (k t)")
        ra = sb("ra", [P, 8192])
        rowbuf = ra[:, :].rearrange("p (s d) -> p s d", s=4)
        varow = ra[:, 0:4096].rearrange("p (r c) -> p r c", r=NT)
        vrow = ra[:, 4096:8192].rearrange("p (r c) -> p r c", r=NT)
        kTm = ra[:, 0:4096].rearrange("p (k m) -> p k m", k=KD)
        vmr = ra[:, 4096:8192].rearrange("p (a d) -> p a d", a=2)
        srow = sb("srow", [TS, 2048 + 512])
        vas, vbs, kss = srow[:, 0:1024], srow[:, 1024:2048], srow[:, 2048:2560]
        rq = sb("rq", [P, 3 * BH * T])
        qT = rq[:, 0:BH * T].rearrange("p (h t) -> p h t", h=BH)
        kT = rq[:, BH * T:2 * BH * T].rearrange("p (h t) -> p h t", h=BH)
        G = rq[:, 2 * BH * T:3 * BH * T].rearrange("p (h t) -> p h t", h=BH)
        memT = mT[:, :, 0:M]
        wring = sb("wring", [P, 2, KD, P])
        stg = sb("stg", [P, 2, T])
        rstdB = sb("rstdB", [P, 2, HALF])
        sq = sb("sq", [P, 2, T])
        ident = sb("ident", [P, P])
        ones = sb("ones", [P, P])
        tri = sb("tri", [P, P])
        wsT = sb("wsT", [P, AH, P])
        bsB = sb("bsB", [P, AH, P])
        gsguB = sb("gsguB", [P, AH * P])
        NG = 4 * KD + BH + BH * NV
        gcol = sb("gcol", [P, NG])
        col_mix, col_mem, col_xq, col_ffn = (gcol[:, a * KD:(a + 1) * KD] for a in range(4))
        col_ba = gcol[:, 4 * KD:4 * KD + BH]
        col_gla = gcol[:, 4 * KD + BH:NG]
        w00B = sb("w00B", [P, AH])
        e8 = sb("e8", [P, TS, TS])
        epsT = sb("epsT", [P, 1])
        ss = sb("ss", [P, 16])
        rs = sb("rs", [P, 16])
        srs = sb("srs", [P, 16])
        wg = sb("wg", [P, KD, RANK])
        primer = sb("primer", [1, 7 * 16])
        vss = sb("vss", [P, NT + 1, AH])
        zgT = sq[0:RANK, 0, :]
        walpha = sq[0:RANK, 1, 0:BH * P]

        gates_tmp = hflat[:, 0:BH * T]
        KF0 = BH * T
        kf = hflat[:, KF0:KF0 + KF]
        qf = hflat[:, KF0 + KF:KF0 + KF + TP]
        kd = hflat[:, KF0 + KF + TP:KF0 + KF + 2 * TP]
        qd = hflat[:, KF0 + KF + 2 * TP:KF0 + KF + 3 * TP]
        factors = hflat[:, KF0:KF0 + KF + 2 * TP]
        smix = hflat[0:TS, 0:AH * P]
        stin = [hflat[:, a * 1024:(a + 1) * 1024].rearrange("p (h v) -> p h v", h=BH) for a in range(2)]
        kf_i, at = [], 0
        for i in range(NSUB):
            kf_i.append(kf[:, at:at + NT * SUB * (i + 1)].rearrange("p (r c) -> p r c", r=NT))
            at += NT * SUB * (i + 1)
        SC0 = KF0 + KF + 3 * TP
        scT = hflat[:, SC0:SC0 + TP].rearrange("p (r t) -> p r t", r=NT)
        kds = hflat[:, SC0 + TP:SC0 + 2 * TP].rearrange("p (r d) -> p r d", r=NT)
        GS0 = SC0 + 2 * TP
        gstate = hflat[:, GS0:GS0 + BV]
        on = hflat[:, GS0 + BV:GS0 + BV + NT * BV].rearrange("p (r v) -> p r v", r=NT)
        SM0 = GS0 + BV + NT * BV
        glast = hflat[:, SM0:SM0 + NT]
        gated = hflat[:, SM0 + 4:SM0 + 4 + TP].rearrange("p (r t) -> p r t", r=NT)
        SN0 = SM0 + 4 + TP
        oS = hflat[:, SN0:SN0 + 64].rearrange("p (h v b) -> p h v b", h=BH, v=NV)
        oSq = hflat[:, SN0 + 64:SN0 + 128].rearrange("p (h v b) -> p h v b", h=BH, v=NV)
        ea = hflat[:, SN0 + 128:SN0 + 160].rearrange("p (h b) -> p h b", h=BH)
        roS = hflat[:, SN0 + 160:SN0 + 192].rearrange("p (h b) -> p h b", h=BH)
        km = hflat[0:TS, KF0:KF0 + 512]
        assert SN0 + 192 <= KD * T
        pT = [rq[:, 4096 + a * 1024:4096 + (a + 1) * 1024].rearrange("p (m t) -> p m t", m=2) for a in range(2)]
        kv_ring = [rq[:, a * D:(a + 1) * D] for a in range(2)]
        qmask = [stg[0:TS, 0, 0:512], stg[0:TS, 1, 0:512], sq[0:TS, 0, 0:512], sq[0:TS, 1, 0:512]]
        wsf = wsT[:, :, :].rearrange("p h c -> p (h c)")
        sS = wsf[:, 0:64].rearrange("p (m h b) -> p m h b", m=2, h=XH)
        ssc = wsf[:, 64:72].rearrange("p (m h) -> p m h", m=2)
        pS = wsf[0:XH * TS, 128:128 + M]
        pST = wsf[:, 384:448].rearrange("p (m c) -> p m c", m=2)
        xhf = xh[:, :, :, :].rearrange("p a k t -> p (a k t)")
        urow = [xhf[:, c * D:(c + 1) * D] for c in range(4)]
        vexp = [xhf[:, (4 + c) * D:(5 + c) * D] for c in range(4)]
        skT = ra[:, 0:D].rearrange("p (n c) -> p n c", n=2 * PH)
        xrow, ystage, hrow = (ra[:, a * D:(a + 1) * D] for a in (1, 2, 3))
        skr = ra[:, 3 * D:4 * D].rearrange("p (n c) -> p n c", n=2 * PH)
        xst = [ra[:, D + a * 512:D + (a + 1) * 512] for a in range(2)]
        gffnB, gfinB = rq[:, 0:D], rq[:, D:2 * D]
        wf = wring[:, :, :, :].rearrange("p a k c -> p (a k c)")
        at = [0]

        def work(n, dt=F32):
            ap = wf[:, at[0]:at[0] + n]
            at[0] += n
            return ap if dt == F32 else ap.bitcast(dt)
        diag = [work(P) for _ in range(4)]
        idx_all, idx8, idxS = work(E, U32), work(8, U32), work(TS, U32)
        gate_all, idxf_all, gateS = work(E), work(E), work(TS)
        sc, sc2, cand, cand2 = work(2 * P), work(2 * P), work(2 * P), work(2 * P)
        onehot = work(2 * P)
        qs = work(2 * P)
        sv, si, sif = work(32), work(32, U32), work(32)
        ts, pos, posi, posj = work(TOPK), work(TOPK, U32), work(TOPK, U32), work(TOPK, U32)
        pif, pjf, pa, pb = work(TOPK), work(TOPK), work(TOPK), work(TOPK)
        ex, jota, jint = work(TOPK), work(TOPK), work(TOPK, mybir.dt.int32)
        act4, g4, w4 = work(4), work(4), work(4)
        ntop, esum, erec = work(1), work(1), work(1)
        wmask = [work(TS) for _ in range(4)]
        assert at[0] <= 2 * KD * P

        pg = [ctx.enter_context(nc.psum_tensor(f"pg{i}", [P, 2, 512], F32)) for i in range(2)]
        pt4 = ctx.enter_context(nc.psum_tensor("pt4", [P, 4, 512], F32))
        pt = [pt4[:, i] for i in range(4)]

        kT_scr = nc.dram_tensor("kT_scratch", [KD, P, M], F32, kind="Internal").ap()
        x_scr = nc.dram_tensor("x_scratch", [T, D], F32, kind="Internal").ap()

        S = {}

        def s(name):
            if name not in S:
                S[name] = sem(name)
            return S[name]

        block = ctx.enter_context(nc.Block())

        xk0, xv0, in0, out0, xq0, xo0, pq0 = 0, 16, 32, 72, 88, 104, 120
        stages = [(w_xk, xk0, 16), (w_xv, xv0, 16), (w_in, in0, 40), (w_out, out0, 16), (w_xq, xq0, 16),
                  (w_xo, xo0, 16), (w_pq, pq0, 16)]

        def pe_product(eng, i, slot, b0, moving, width):
            eng.wait_ge(s(f"w_loaded{slot}"), i * 16 + (b0 // 2 + 1) * 16)
            eng.wait_ge(s("product_read"), i * 2 + (b0 + slot + 1))
            for k in range(KD):
                if width == T:
                    for a in range(2):
                        mm = eng.matmul(pg[slot][:, a, 0:HALF], wring[:, slot, k], moving[:, k, a * HALF:(a + 1) * HALF],
                                        start=(k == 0), stop=(k == KD - 1))
                else:
                    mm = eng.matmul(pg[slot][:, 0, 0:width], wring[:, slot, k], moving[:, k, 0:width],
                                    start=(k == 0), stop=(k == KD - 1))
            mm.then_inc(s("product_done"), 1)

        def await_product(eng, i, slot, b0):
            eng.wait_ge(s("product_done"), i * 2 + (b0 + slot + 1))

        item_rows = [P, P, P, P, P, P, TS]

        @block.sync
        def _(eng):
            def load_rows(item):
                if item >= 4:
                    eng.wait_ge(s("turned"), 3 + 4 * (item - 3))
                src = (mem_prompt[0, item * P:(item + 1) * P, :] if item < 2 else
                       x_prompt[0, (item - 2) * P:(item - 1) * P, :] if item < 6 else x_sample[:, 0, :])
                eng.dma_start(rowbuf[0:item_rows[item], item % 4, :], src).then_inc(s(f"rows_loaded{item % 4}"), 16)

            def load_weights(w, b0, count, first):
                wv = w[0, :, 0:count * P].rearrange("(k p) (n c) -> n p k c", p=P, c=P)
                start = 0
                if first:
                    start = 1
                    for slot in range(2):
                        eng.dma_start(wring[:, slot], wv[slot]).then_inc(s(f"w_loaded{slot}"), 16)
                    for item in range(4, 7):
                        load_rows(item)
                with eng.Fori(start, count // 2) as i:
                    for slot in range(2):
                        eng.wait_ge(s("product_done"), i * 2 + (b0 + slot - 1))
                        eng.dma_start(wring[:, slot], wv[i * 2 + slot]).then_inc(s(f"w_loaded{slot}"), 16)

            for a, g in enumerate((g_mix, g_mem, g_xq, g_ffn)):
                eng.dma_start(stg[a * KD:(a + 1) * KD, 0, 0:P], g[0].rearrange("(k p) -> k p", p=P)).then_inc(s("gains_loaded"), 16)
            eng.dma_start(stg[4 * KD:4 * KD + BH, 0, 0:P], b_alpha[0].rearrange("(k p) -> k p", p=P)).then_inc(s("gains_loaded"), 16)
            eng.dma_start(stg[4 * KD + BH:NG, 0, 0:P], g_gla[0].rearrange("h (v p) -> (h v) p", p=P)).then_inc(s("gains_loaded"), 16)
            for item in range(4):
                load_rows(item)
            first = True
            for n, (w, b0, count) in enumerate(stages):
                load_weights(w, b0, count, first)
                first = False

            eng.sem_inc(s("y_stored"), 16)
            for r in range(NT + 1):
                n = P if r < NT else TS
                for a in range(2):
                    eng.wait_ge(s(f"x_stored{a}"), 16 * (2 * NT + 2))
                eng.wait_ge(s("y_ready"), r + 1)
                eng.dma_start(xrow[0:n], x_scr[r * P:r * P + n, :]).then_inc(s("xrow_loaded"), 16)
                eng.wait_ge(s("y_ready"), r + 2)
                dst = y_prompt[0, r * P:(r + 1) * P, :] if r < NT else y_sample[:, 0, :]
                eng.dma_start(dst, ystage[0:n]).then_inc(s("y_stored"), 16)
            eng.wait_ge(s("y_stored"), 16 * (NT + 2))

        @block.gpsimd
        def _(eng):
            def passed():
                eng.sem_inc(s("pool_passed"), 1)

            eng.dma_start(hflat[:, 0:AH * P].rearrange("p (h c) -> p h c", h=AH),
                          w_s[0].rearrange("h t s -> t h s")).then_inc(s("ws_loaded"), 16)
            eng.memset(ident[:, :], 0.0).then_inc(s("pool_set"), 1)
            eng.memset(tri[:, :], 1.0).then_inc(s("pool_set"), 1)
            eng.memset(e8[:, :, :], 0.0).then_inc(s("pool_set"), 1)
            eng.wait_ge(s("pool_set"), 3)
            eng.affine_select(out=ident[:, :], in_=ident[:, :], compare_op=ALU.not_equal, fill=1.0, base=0,
                              pattern=[[-1, P]], channel_multiplier=1).then_inc(s("masks_ready"), 1)
            eng.affine_select(out=tri[:, :], in_=tri[:, :], compare_op=ALU.is_ge, fill=0.0, base=0,
                              pattern=[[1, P]], channel_multiplier=-1).then_inc(s("masks_ready"), 1)
            eng.affine_select(out=e8[:, :, :], in_=e8[:, :, :], compare_op=ALU.not_equal, fill=1.0, base=0,
                              pattern=[[1, TS], [-1, TS]], channel_multiplier=0).then_inc(s("masks_ready"), 1)
            eng.wait_ge(s("ws_loaded"), 16)
            wsrow = hflat[:, 0:AH * P].rearrange("p (h c) -> p h c", h=AH)
            eng.affine_select(out=wsrow, in_=wsrow, compare_op=ALU.is_ge, fill=0.0, base=0,
                              pattern=[[0, AH], [-1, P]], channel_multiplier=1).then_inc(s("ws_masked"), 1)
            eng.dma_start(bsB[:, :, :].rearrange("p h c -> p (h c)"),
                          b_s[0].rearrange("h c -> (h c)").partition_broadcast(P)).then_inc(s("consts_loaded"), 16)
            eng.dma_start(gsguB[:, :], g_sgu[0].rearrange("h c -> (h c)").partition_broadcast(P)).then_inc(s("consts_loaded"), 16)
            eng.dma_start(w00B[0:TS, :], w_s[0, :, 0, 0:1].rearrange("h c -> (h c)").partition_broadcast(TS),
                          allow_slow_non_contiguous=True).then_inc(s("consts_loaded"), 16)
            eng.dma_start(wg[:, :, :], w_in[0, :, 40 * P:40 * P + RANK].rearrange("(k p) c -> p k c", p=P)).then_inc(s("wg_loaded"), 16)
            for n, name in enumerate(("kT_stored0", "kT_stored1", "memrow_stored0", "memrow_stored1", "state_stored",
                                      "sstate_stored0", "sstate_stored1")):
                eng.dma_start(primer[:, n * 16:(n + 1) * 16], g_final[0:16].partition_broadcast(1)).then_inc(s(name), 16)

            for kv, dst in enumerate((mem_k_out, mem_v_out)):
                rows = dst[0, 0].rearrange("(a m) h d -> m a (h d)", a=2).rearrange("m a (n c) -> n m a c", c=P)
                with eng.Fori(0, KD // 2) as i:
                    for slot in range(2):
                        if kv == 0:
                            eng.wait_ge(s("product_read"), i * 2 + (xk0 + slot + 3))
                            passed()
                            eng.dma_start(kT_scr[i * 2 + slot], stg[:, slot, 0:M]).then_inc(s(f"kT_stored{slot}"), 16)
                        eng.wait_ge(s("memrow_ready"), i * 2 + (kv * KD + slot + 3))
                        passed()
                        eng.dma_start(rows[i * 2 + slot], rq[:, slot * M:(slot + 1) * M].rearrange("p (a c) -> p a c", a=2)
                                      ).then_inc(s(f"memrow_stored{slot}"), 16)

            eng.wait_ge(s("sq_used"), 2 + KD)
            eng.dma_start(walpha, w_alpha[0]).then_inc(s("walpha_loaded"), 16)
            eng.wait_ge(s("va_normed"), NT + 1)
            eng.dma_start(chunk_p_out[0, 0].rearrange("t h c -> t (h c)"), varow[:, NT - 1, :]).then_inc(s("chunk_stored"), 16)
            eng.dma_start(chunk_s_out[0, :, 0].rearrange("t h c -> t (h c)"), vas).then_inc(s("chunk_stored"), 16)

            with eng.Fori(0, BH) as j:
                eng.wait_ge(s("state_ready"), j * NT + NT)
                passed()
                eng.dma_start(state_p_out[0, 0][j], hflat[:, GS0:GS0 + BV]).then_inc(s("state_stored"), 16)

            eng.wait_ge(s("head_out"), 2 + 2 * BH)
            with eng.Fori(0, TS // 2) as i:
                for a in range(2):
                    eng.wait_ge(s(f"sstate_stored{a}"), i * 16 + 16)
                    eng.wait_ge(s("os_done"), i * 2 + (a + 1))
                    passed()
                    eng.dma_start(stin[a], state_gla[0][i * 2 + a].rearrange("h d v -> d h v")).then_inc(s(f"sstate_loaded{a}"), 16)
                for a in range(2):
                    eng.wait_ge(s("sstate_read"), i * 2 + (a + 2))
                    passed()
                    eng.dma_start(state_s_out[0][i * 2 + a].rearrange("h d v -> d h v"), stin[a]).then_inc(s(f"sstate_stored{a}"), 16)

            eng.wait_ge(s("gla_sample_done"), 1)
            for slot in range(2):
                eng.wait_ge(s(f"kT_stored{slot}"), 16 * (KD // 2 + 1))
                eng.wait_ge(s(f"memrow_stored{slot}"), 16 * (KD + 1))
            eng.wait_ge(s("chunk_stored"), 32)
            eng.dma_start(kTm, kT_scr.rearrange("k p m -> p k m")).then_inc(s("attn_loaded"), 16)
            eng.dma_start(vmr, mem_v_out[0, 0].rearrange("(a m) h d -> m a (h d)", a=2)).then_inc(s("attn_loaded"), 16)
            cv = cache_mem_k[0].rearrange("b (a m) h d -> b a m (h d)", a=2)
            with eng.Fori(0, TS) as b:
                for a in range(2):
                    eng.wait_ge(s(f"cache_used{a}"), b + 1)
                    passed()
                    eng.dma_start(kv_ring[a], cv[b, a]).then_inc(s(f"cache_loaded{a}"), 16)
            cv = cache_mem_v[0].rearrange("b (a m) h d -> b a m (h d)", a=2)
            for a in range(2):
                eng.wait_ge(s(f"cache_used{a}"), TS + 1)
            with eng.Fori(0, TS) as b:
                eng.wait_ge(s("oxs_done"), b + 1)
                passed()
                for a in range(2):
                    eng.dma_start(kv_ring[a], cv[b, a]).then_inc(s(f"cache_loaded{a}"), 16)

            for n in range(4 * NT + 4):
                eng.wait_ge(s("xrow_staged"), n + 1)
                r, c = divmod(n, 4)
                rows = P if r < NT else TS
                eng.dma_start(x_scr[r * P:r * P + rows, c * 512:(c + 1) * 512],
                              xst[n % 2][0:rows]).then_inc(s(f"x_stored{n % 2}"), 16)

            for a in range(2):
                eng.wait_ge(s(f"x_stored{a}"), 16 * (2 * NT + 2))
            eng.dma_start(gffnB, g_ffn[0].partition_broadcast(P)).then_inc(s("peer_consts"), 16)
            eng.dma_start(gfinB, g_final.partition_broadcast(P)).then_inc(s("peer_consts"), 16)
            for h in range(0, 16, 4):
                eng.dma_start(skr[:, h:h + 4, :], sub_keys[0].rearrange("h c n d -> n (h c) d")[:, h:h + 4, :]).then_inc(s("keys_loaded"), 16)
            eng.wait_ge(s("product_read"), 2 + pq0 + 16)
            eng.iota(jint, pattern=[[1, TOPK]], base=0, channel_multiplier=0
                     ).then_inc(s("iota_made"), 1)
            with eng.Fori(0, NT) as r:
                eng.wait_ge(s("picks_ready"), r + 1)
                passed()
                with eng.Fori(0, E // 8) as g:
                    for half in range(2):
                        c0 = half * 4
                        eng.wait_ge(s("u_used"), r * E + g * 8 + (c0 + 1))
                        eng.wait_ge(s("v_used"), r * E + g * 8 + (c0 + 1))
                        eng.tensor_copy(idx8[:, c0:c0 + 4], idx_all[:, bass.ds(g * 8 + c0, 4)]).then_inc(s("idx_copied"), 1)
                        for c in range(4):
                            if c == 0:
                                eng.wait_ge(s("idx_copied"), r * (E // 4) + g * 2 + (half + 1))
                            eng.wait_ge(s("u_used"), r * E + g * 8 + (c0 + c + 1))
                            passed()
                            eng.indirect_dma_start(urow[c], None, u_emb[0], bass.IndirectOffsetOnAxis(ap=idx8[:, c0 + c:c0 + c + 1], axis=0)
                                                   ).then_inc(s(f"u_loaded{c}"), 16)
                            eng.wait_ge(s("v_used"), r * E + g * 8 + (c0 + c + 1))
                            passed()
                            eng.indirect_dma_start(vexp[c], None, v_emb[0], bass.IndirectOffsetOnAxis(ap=idx8[:, c0 + c:c0 + c + 1], axis=0)
                                                   ).then_inc(s(f"v_loaded{c}"), 16)
            eng.wait_ge(s("picks_ready"), NT + 1)
            for t in range(TS):
                c = t % 4
                eng.wait_ge(s("u_used"), NT * E + t + 1)
                eng.indirect_dma_start(urow[c], None, u_emb[0], bass.IndirectOffsetOnAxis(ap=idxS[:, t:t + 1], axis=0)
                                       ).then_inc(s(f"u_loaded{c}"), 16)
                eng.wait_ge(s("v_used"), NT * E + t + 1)
                eng.indirect_dma_start(vexp[c], None, v_emb[0], bass.IndirectOffsetOnAxis(ap=idxS[:, t:t + 1], axis=0)
                                       ).then_inc(s(f"v_loaded{c}"), 16)
            eng.wait_ge(s("state_stored"), 16 * (BH + 1))
            for a in range(2):
                eng.wait_ge(s(f"sstate_stored{a}"), 16 * (TS // 2 + 1))

        @block.tensor
        def _(eng):
            def turn(out, src, n):
                return eng.transpose(out, src, ident[0:n, 0:n])

            def product_loop(b0, count, moving, width, after=None):
                with eng.Fori(0, count // 2) as i:
                    for slot in range(2):
                        pe_product(eng, i, slot, b0, moving, width)
                    if after:
                        after(i)

            def norm_sum(n):
                def add(i, a, start):
                    eng.wait_ge(s("sq_ready"), i * 2 + (n * KD + a + 1))
                    for c in range(2):
                        mm = eng.matmul(pt[c][:, 0:HALF], ones[:, :], sq[:, a, c * HALF:(c + 1) * HALF],
                                        start=start, stop=True, skip_group_check=True)
                    mm.then_inc(s("sq_used"), 1)
                for a in range(2):
                    add(0, a, a == 0)
                with eng.Fori(1, KD // 2) as i:
                    for a in range(2):
                        add(i, a, False)

            eng.sem_inc(s("mem_turned"), 2)
            eng.sem_inc(s("val_turned"), 2)
            eng.sem_inc(s("sq_used"), 2)
            eng.sem_inc(s("outer_done"), 1)
            eng.sem_inc(s("os_done"), 2)
            eng.sem_inc(s("qB_done"), 1)
            eng.sem_inc(s("oxs_done"), 1)
            eng.sem_inc(s("v_used"), 4)

            unit = 0

            def turn_unit(pieces):
                nonlocal unit
                if unit >= 4:
                    eng.wait_ge(s("turn_read"), unit - 3)
                for dst, src, n in pieces:
                    mm = turn(dst, src, n)
                mm.then_inc(s("turned"), 1)
                unit += 1

            eng.wait_ge(s("masks_ready"), 1)
            eng.wait_ge(s("gains_loaded"), 96)
            turn_unit([(pt[0][:, 0:NG], stg[0:NG, 0, 0:P], NG)])
            eng.wait_ge(s("ws_masked"), 1)
            for u in range(2):
                turn_unit([(pt[unit % 4][:, a * P:(a + 1) * P], hflat[:, (4 * u + a) * P:(4 * u + a + 1) * P], P)
                           for a in range(4)])
            for item in range(7):
                if item < 2:
                    eng.wait_ge(s("mem_scaled"), item + 1)
                else:
                    eng.wait_ge(s(f"rows_loaded{item % 4}"), 16 * (item // 4 + 1))
                if item < 6:
                    for g in range(4):
                        turn_unit([(pt[unit % 4][:, a * P:(a + 1) * P],
                                    rowbuf[:, item % 4, (4 * g + a) * P:(4 * g + a + 1) * P], P) for a in range(4)])
                else:
                    turn_unit([(pt[unit % 4][:, k * TS:(k + 1) * TS], rowbuf[0:TS, item % 4, k * P:(k + 1) * P], TS)
                               for k in range(KD)])

            eng.wait_ge(s("turn_read"), unit)
            for b0 in (xk0, xv0):
                def mem_rows(i):
                    for slot in range(2):
                        eng.wait_ge(s("product_read"), i * 2 + (b0 + slot + 3))
                        eng.wait_ge(s("memrow_ready"), i * 2 + (b0 + slot + 1))
                        for a in range(2):
                            mm = turn(pt[slot][:, a * P:(a + 1) * P], stg[:, slot, a * P:(a + 1) * P], P)
                        mm.then_inc(s("mem_turned"), 1)
                product_loop(b0, 16, memT, M, mem_rows)

            eng.wait_ge(s("memrow_ready"), 2 + 2 * KD)
            norm_sum(0)
            eng.wait_ge(s("ht_ready"), KD)
            eng.wait_ge(s("wg_loaded"), 16)
            for c in range(2):
                for k in range(KD):
                    mm = eng.matmul(pt[2 + c][0:RANK, 0:HALF], wg[:, k], hT[:, k, c * HALF:(c + 1) * HALF],
                                    start=(k == 0), stop=(k == KD - 1))
            mm.then_inc(s("zg_done"), 1)
            product_loop(in0, 8, hT, T)
            eng.wait_ge(s("zg_read"), 1)

            def value_rows(first):
                def after(i):
                    for slot in range(2):
                        if first == 0:
                            eng.wait_ge(s("val_staged"), i * 2 + (slot + 1))
                        else:
                            eng.wait_ge(s("product_read"), i * 2 + (in0 + 24 + slot + 3))
                        eng.wait_ge(s("val_read"), i * 2 + (first + slot + 1))
                        for r in range(NT):
                            turn(pt[slot][:, r * P:(r + 1) * P], stg[:, slot, r * P:(r + 1) * P], P)
                        turn(pt[2 + slot][0:TS, 0:P], stg[:, slot, TP:T], P).then_inc(s("val_turned"), 1)
                return after
            eng.wait_ge(s("norm_root"), 1)
            product_loop(in0 + 8, 8, hT, T, value_rows(0))
            product_loop(in0 + 16, 8, hT, T)
            product_loop(in0 + 24, 8, hT, T, value_rows(8))
            product_loop(in0 + 32, 8, hT, T)

            eng.wait_ge(s("val_read"), 2 + 16)
            eng.wait_ge(s("walpha_loaded"), 16)
            for j in range(BH):
                eng.wait_ge(s("product_read"), 2 + out0)
                if j >= 2:
                    eng.wait_ge(s("gate_read"), j - 1)
                for c in range(2):
                    mm = eng.matmul(pg[j % 2][:, c, 0:HALF], walpha[:, j * P:(j + 1) * P],
                                    zgT[:, c * HALF:(c + 1) * HALF], start=True, stop=True)
                mm.then_inc(s("gate_done"), 1)

            for h in range(AH):
                if h < NT:
                    eng.wait_ge(s("va_normed"), NT + 1)
                else:
                    eng.wait_ge(s("sgu_read"), h - 3)
                for r in range(NT):
                    mm = eng.matmul(pt[h % 4][:, r * P:(r + 1) * P], varow[:, r, h * P:(h + 1) * P], wsT[:, h],
                                    start=True, stop=True)
                mm.then_inc(s("sgu_done"), 1)
            eng.wait_ge(s("sgu_read"), AH)
            eng.wait_ge(s("sgu_sample"), 1)
            for h in range(AH):
                mm = turn(pt[0][:, h * TS:(h + 1) * TS], smix[:, h * P:(h + 1) * P], TS)
            mm.then_inc(s("sgu_done"), 1)

            eng.wait_ge(s("sgu_read"), AH + 1)
            eng.wait_ge(s("gate_read"), BH)
            with eng.Fori(0, BH) as j:
                eng.wait_ge(s("factors_ready"), j * 7 + 7)
                eng.wait_ge(s("head_out"), j * 2 + 2)
                for r in range(NT):
                    mm = turn(pt[0][:, r * P:(r + 1) * P], kd[:, r * P:(r + 1) * P], P)
                mm.then_inc(s("kd_turned"), 1)
                for r in range(NT):
                    for a in range(NSUB):
                        mm = eng.matmul(pt[1][0:SUB * (a + 1), r * P + a * SUB:r * P + (a + 1) * SUB],
                                        kf_i[a][:, r, :], qf[:, r * P + a * SUB:r * P + (a + 1) * SUB],
                                        start=True, stop=True)
                mm.then_inc(s("scores_done"), 1)
                eng.wait_ge(s("scores_masked"), j * NSUB + NSUB)
                eng.wait_ge(s("kds_ready"), j + 1)
                for r in range(NT):
                    v = vrow[:, r, bass.ds(j * BV, BV)]
                    if r >= 2:
                        eng.wait_ge(s("state_ready"), j * NT + (r - 1))
                    eng.matmul(pg[0][:, r % 2, 0:BV], kds[:, r, :], v, start=True, stop=True).then_inc(s("state_part"), 1)
                    out = pt[2 + r // 2][:, (r % 2) * BV:(r % 2 + 1) * BV]
                    mm = eng.matmul(out, scT[:, r, :], v, start=True, stop=(r == 0))
                    if r >= 1:
                        eng.wait_ge(s("state_ready"), j * NT + r)
                        mm = eng.matmul(out, qd[:, r * P:(r + 1) * P], gstate, start=False, stop=True)
                        if r < NT - 1:
                            mm.then_inc(s("state_used"), 1)
                mm.then_inc(s("o_done"), 1)
                eng.wait_ge(s("o_normed"), j * NT + NT)
                for v in range(NV):
                    for r in range(NT):
                        mm = turn(pg[1][:, v, r * P:(r + 1) * P], on[:, r, v * P:(v + 1) * P], P)
                mm.then_inc(s("o_turned"), 1)

            eng.wait_ge(s("head_out"), 2 + 2 * BH)
            for j in range(BH):
                mm = turn(pt[0][0:TS, j * P:(j + 1) * P], kT[:, j, TP:T], P)
            mm.then_inc(s("ks_turned"), 1)
            with eng.Fori(0, TS // 2) as i:
                for a in range(2):
                    eng.wait_ge(s("km_ready"), i * 2 + (a + 1))
                    eng.wait_ge(s("sstate_read"), i * 2 + (a + 1))
                    for j in range(BH):
                        mm = eng.matmul(pg[j // 2][:, 0, (j % 2) * BV:(j % 2 + 1) * BV], km[:, j * P:(j + 1) * P],
                                        vbs[:, j * BV:(j + 1) * BV], start=True, stop=True)
                    mm.then_inc(s("outer_done"), 1)
                    eng.wait_ge(s("sstate_read"), i * 2 + (a + 2))
                    eng.wait_ge(s("os_read"), i * 2 + (a + 1))
                    st = stin[a]
                    for j in range(BH):
                        for v in range(NV):
                            mm = eng.matmul(pt[3][:, j * NV + v:j * NV + v + 1], st[:, j, v * P:(v + 1) * P],
                                            qT[:, j, bass.ds(i * 2 + (TP + a), 1)], start=True, stop=True)
                    mm.then_inc(s("os_done"), 1)
            eng.wait_ge(s("os_squared"), 1)
            for v in range(NV):
                mm = eng.matmul(pt[0][:, 0:BH * TS], ones[:, :], oSq[:, :, v, :], start=(v == 0), stop=(v == NV - 1))
            mm.then_inc(s("os_summed"), 1)

            eng.wait_ge(s("gla_sample_done"), 1)
            product_loop(out0, 16, mT, T)
            eng.wait_ge(s("product_read"), 2 + xq0)
            norm_sum(1)
            eng.wait_ge(s("ht_ready"), 2 * KD)
            product_loop(xq0, 16, hT, T)
            eng.wait_ge(s("product_read"), 2 + xo0)
            eng.wait_ge(s("attn_loaded"), 32)
            eng.wait_ge(s("norm_root"), 2)

            units = [(h, r) for h in range(XH) for r in range(NT)]

            def scores(u):
                h, r = units[u]
                if u >= 2:
                    eng.wait_ge(s("p_exp"), u - 1)
                for k in range(XK):
                    mm = eng.matmul(pt[u % 2][:, 0:M], mT[:, h * XK + k, r * P:(r + 1) * P], kTm[:, h * XK + k, :],
                                    start=(k == 0), stop=(k == XK - 1))
                mm.then_inc(s("xscores_done"), 1)

            def turn_p(u):
                eng.wait_ge(s("p_ready"), u + 1)
                if u >= 2:
                    eng.wait_ge(s("pT_ready"), u - 1)
                for a in range(2):
                    mm = turn(pt[2 + u % 2][:, a * P:(a + 1) * P], stg[:, u % 2, a * P:(a + 1) * P], P)
                mm.then_inc(s("p_turned"), 1)

            def values(h):
                eng.wait_ge(s("pT_ready"), NT * (h + 1))
                for k in range(XK):
                    n = h * XK + k
                    if n >= 4:
                        eng.wait_ge(s("xo_read"), n - 3)
                    bank = pg[(n % 4) // 2][:, n % 2, :]
                    for a in range(2):
                        mm = eng.matmul(bank, vmr[:, a, n * P:(n + 1) * P], pT[h % 2][:, a, :], start=(a == 0), stop=(a == 1))
                    mm.then_inc(s("xo_done"), 1)

            for u in range(len(units) + 1):
                if u < len(units):
                    scores(u)
                if u >= 1:
                    turn_p(u - 1)
                if u >= 2 and (u - 2) % NT == NT - 1:
                    values((u - 2) // NT)
            values(XH - 1)

            eng.wait_ge(s("pT_ready"), len(units))
            for k in range(KD):
                mm = turn(pt[k // 4][0:TS, (k % 4) * P:(k % 4 + 1) * P], mT[:, k, TP:T], P)
            mm.then_inc(s("qs_turned"), 1)
            with eng.Fori(0, TS) as b:
                eng.wait_ge(s("qmask_ready"), b + 1)
                for c in range(4):
                    mm = eng.matmul(pt[c][:, :], ones[0:TS, :], qmask[c], start=True, stop=True)
                mm.then_inc(s("qB_done"), 1)
            eng.wait_ge(s("ss_ready"), TS)
            for a in range(2):
                mm = turn(pt[0][0:XH * TS, a * P:(a + 1) * P], wsf[:, a * 32:(a + 1) * 32], P)
            mm.then_inc(s("ss_turned"), 1)
            eng.wait_ge(s("pS_ready"), 1)
            for a in range(2):
                mm = turn(pt[1][:, a * 32:(a + 1) * 32], pS[:, a * P:(a + 1) * P], XH * TS)
            mm.then_inc(s("pS_turned"), 1)
            eng.wait_ge(s("pST_ready"), 1)
            with eng.Fori(0, TS) as b:
                for a in range(2):
                    eng.wait_ge(s(f"cache_loaded{a}"), b * 16 + 16 * (TS + 1))
                eng.wait_ge(s("oxs_read"), b + 1)
                for n in range(KD):
                    for a in range(2):
                        mm = eng.matmul(pt[2][:, n:n + 1], kv_ring[a][:, n * P:(n + 1) * P],
                                        pST[:, a, bass.ds(b + (n // XK) * TS, 1)], start=(a == 0), stop=(a == 1))
                mm.then_inc(s("oxs_done"), 1)
            eng.wait_ge(s("oxs_read"), TS + 1)
            eng.wait_ge(s("xo_read"), KD)
            product_loop(xo0, 16, hT, T)
            eng.wait_ge(s("product_read"), 2 + pq0)
            norm_sum(2)
            for n in range(4 * NT + 4):
                r, c = divmod(n, 4)
                if n >= 2:
                    eng.wait_ge(s("xrow_staged"), n - 1)
                for a in range(4):
                    k = 4 * c + a
                    src = xT[:, k, r * P:(r + 1) * P] if r < NT else xT[:, k, TP:T]
                    mm = turn(pt[2 + n % 2][0:(P if r < NT else TS), a * P:(a + 1) * P], src, P)
                mm.then_inc(s("xrow_turned"), 1)
            eng.wait_ge(s("xrow_staged"), 4 * NT + 4)
            for n in range(4):
                eng.wait_ge(s("keys_loaded"), 64)
                if n >= 2:
                    eng.wait_ge(s("keys_read"), n - 1)
                for a in range(4):
                    mm = turn(pt[2 + n % 2][:, a * P:(a + 1) * P], skr[:, 4 * n + a, :], P)
                mm.then_inc(s("keys_turned"), 1)
            eng.wait_ge(s("ht_ready"), 3 * KD)
            product_loop(pq0, 16, hT, T)
            eng.wait_ge(s("product_read"), 2 + pq0 + 16)
            eng.wait_ge(s("keys_read"), 4)

            def acc(c):
                return pg[c // 2][:, c % 2, :]

            def select(n, r):
                with eng.Fori(0, PH) as h:
                    eng.wait_ge(s("qs_ready"), r * PH + h + 1)
                    eng.wait_ge(s("sc_copied"), r * PH + h + 1)
                    for c in range(2):
                        mm = eng.matmul(pt[0][0:n, c * P:(c + 1) * P], qs[:, c * P:c * P + n], skT[:, h * 2 + c, :],
                                        start=True, stop=True)
                    mm.then_inc(s("sc_done"), 1)

            with eng.Fori(0, NT) as r:
                select(P, r)
                eng.wait_ge(s("xrow_loaded"), r * 16 + 16)
                eng.wait_ge(s("y_ready"), r + 1)
                for c in range(4):
                    eng.matmul(acc(c), ident[:, :], xrow[:, c * 512:(c + 1) * 512], start=True, stop=True
                               ).then_inc(s("acc_started"), 1)
                with eng.Fori(0, E // 4) as g:
                    for c in range(4):
                        eng.wait_ge(s("diag_ready"), r * E + g * 4 + (c + 1))
                        eng.wait_ge(s(f"v_loaded{c}"), (r * (E // 4) + g) * 16 + 16)
                        for d in range(4):
                            mm = eng.matmul(acc(d), diag[c], vexp[c][:, d * 512:(d + 1) * 512], start=False, stop=True,
                                            skip_group_check=True)
                        mm.then_inc(s("v_used"), 1)
            select(TS, NT)
            eng.wait_ge(s("picks_made"), 1)
            turn(pt[1][:, 0:TS], idxf_all[0:TS, :], TS)
            turn(pt[1][:, TS:2 * TS], gate_all[0:TS, :], TS).then_inc(s("picks_turned"), 1)
            eng.wait_ge(s("xrow_loaded"), (NT + 1) * 16)
            eng.wait_ge(s("y_ready"), NT + 1)
            eng.wait_ge(s("picks_ready"), NT + 1)
            for c in range(4):
                eng.matmul(acc(c)[0:TS], ident[0:TS, 0:TS], xrow[0:TS, c * 512:(c + 1) * 512], start=True, stop=True
                           ).then_inc(s("acc_started"), 1)
            for t in range(TS):
                eng.wait_ge(s("hmask_ready"), t + 1)
                for c in range(4):
                    mm = eng.matmul(pt[c][:, :], ones[0:TS, :], ystage[0:TS, c * 512:(c + 1) * 512], start=True, stop=True)
                mm.then_inc(s("hB_done"), 1)
                c = t % 4
                eng.wait_ge(s("diag_ready"), NT * E + t + 1)
                eng.wait_ge(s(f"v_loaded{c}"), (NT * E // 4 + t // 4 + 1) * 16)
                for d in range(4):
                    mm = eng.matmul(acc(d)[0:TS], wmask[c], vexp[c][:, d * 512:(d + 1) * 512], start=False, stop=True,
                                    skip_group_check=True)
                mm.then_inc(s("v_used"), 1)

        @block.vector
        def _(eng):
            ch = Chain(eng, s("dve_chain"))
            for name, n in (("product_read", 2), ("head_out", 2), ("sstate_read", 1), ("cache_used0", 1),
                            ("cache_used1", 1), ("u_used", 4), ("y_ready", 1), ("head_selected", 1)):
                eng.sem_inc(s(name), n)
            eng.memset(ones[:, :], 1.0).then_inc(s("ones_ready"), 1)
            eng.memset(epsT[:, :], EPS).then_inc(s("ones_ready"), 1)
            eng.memset(vss[:, :, :], 1.0).then_inc(s("ones_ready"), 1)
            eng.wait_ge(s("ones_ready"), 3)

            for item in range(2):
                eng.wait_ge(s("mem_root"), item + 1)
                ch.link(eng.reciprocal(rs[:, item:item + 1], ss[:, item:item + 1]))
                eng.tensor_scalar(rowbuf[:, item, :], rowbuf[:, item, :], rs[:, item:item + 1], None, ALU.mult
                                  ).then_inc(s("mem_scaled"), 1)
            unit = 0

            def take(ins_of):
                nonlocal unit
                eng.wait_ge(s("turned"), unit + 1)
                ins_of(pt[unit % 4]).then_inc(s("turn_read"), 1)
                unit += 1

            take(lambda t: eng.tensor_copy(gcol[:, :], t[:, 0:NG]))
            for u in range(2):
                take(lambda t: eng.tensor_copy(wsT[:, 4 * u:4 * u + 4, :], t.rearrange("p (h c) -> p h c", h=4)))
            eng.wait_ge(s("turn_read"), 1)
            for item in range(2):
                for g in range(4):
                    take(lambda t: eng.tensor_tensor(
                        memT[:, 4 * g:4 * g + 4, item * P:(item + 1) * P], t.rearrange("p (k c) -> p k c", k=4),
                        col_mem[:, 4 * g:4 * g + 4].unsqueeze(2).broadcast_to([P, 4, P]), ALU.mult))
            for r in range(NT):
                for g in range(4):
                    take(lambda t: eng.tensor_copy(xT[:, 4 * g:4 * g + 4, r * P:(r + 1) * P],
                                                   t.rearrange("p (k c) -> p k c", k=4)))
            take(lambda t: eng.tensor_copy(xT[:, :, TP:T], t[:, 0:P].rearrange("p (k c) -> p k c", k=KD)))

            for kv, b0 in enumerate((xk0, xv0)):
                if kv:
                    for slot in range(2):
                        eng.wait_ge(s(f"kT_stored{slot}"), 16 * (KD // 2 + 1))
                with eng.Fori(0, KD // 2) as i:
                    for slot in range(2):
                        await_product(eng, i, slot, b0)
                        eng.wait_ge(s("mem_turned"), i * 2 + (b0 + slot + 1))
                        if not kv:
                            eng.wait_ge(s(f"kT_stored{slot}"), i * 16 + 16)
                        eng.tensor_copy(stg[:, slot, 0:M], pg[slot][:, 0, 0:M]).then_inc(s("product_read"), 1)

            def norm_operand(n, col):
                with eng.Fori(0, KD // 2) as i:
                    for a in range(2):
                        eng.tensor_scalar(hT[:, i * 2 + a, :], xT[:, i * 2 + a, :], col[:, bass.ds(i * 2 + a, 1)], None,
                                          ALU.mult).then_inc(s("ht_ready"), 1)
                eng.wait_ge(s("norm_root"), n + 1)
                ch.link(eng.reciprocal(rstdB[:, :, :], rstdB[:, :, :]))

            def read_loop(b0, count, ins_of, before=None):
                with eng.Fori(0, count // 2) as i:
                    for slot in range(2):
                        await_product(eng, i, slot, b0)
                        if before:
                            before(i, slot)
                        ins_of(i * 2 + slot, slot).then_inc(s("product_read"), 1)

            def halves(ap):
                return ap.rearrange("p (a t) -> p a t", a=2)

            eng.wait_ge(s("turn_read"), unit)
            norm_operand(0, col_mix)
            eng.wait_ge(s("zg_done"), 1)
            eng.tensor_tensor(halves(zgT), pt4[0:RANK, 2:4, 0:HALF], rstdB[0:RANK], ALU.mult).then_inc(s("zg_read"), 1)
            prod = [pg[a][:, :, 0:HALF] for a in range(2)]
            read_loop(in0, 8, lambda n, a: eng.tensor_tensor(m2[:, n], prod[a], rstdB[:, :, :], ALU.mult))
            eng.wait_ge(s("mem_turned"), 2 + 2 * KD)
            read_loop(in0 + 8, 8, lambda n, a: eng.tensor_tensor(halves(stg[:, a, :]), prod[a], rstdB[:, :, :], ALU.mult),
                      lambda i, a: eng.wait_ge(s("val_turned"), i * 2 + (a + 1)))
            for slot in range(2):
                eng.wait_ge(s(f"memrow_stored{slot}"), 16 * (KD + 1))
            read_loop(in0 + 16, 4, lambda n, a: eng.scalar_tensor_tensor(
                halves(qT[:, n, :]), prod[a], float(P) ** -0.5, rstdB[:, :, :], ALU.mult, ALU.mult))
            read_loop(in0 + 20, 4, lambda n, a: eng.tensor_tensor(halves(kT[:, n, :]), prod[a], rstdB[:, :, :], ALU.mult))
            read_loop(in0 + 24, 8, lambda n, a: eng.tensor_tensor(halves(stg[:, a, :]), prod[a], rstdB[:, :, :], ALU.mult),
                      lambda i, a: eng.wait_ge(s("val_turned"), i * 2 + (8 + a + 1)))
            read_loop(in0 + 32, 8, lambda n, a: eng.tensor_tensor(m2[:, n + 8], prod[a], rstdB[:, :, :], ALU.mult))

            for j in range(BH):
                eng.wait_ge(s("gate_done"), j + 1)
                eng.tensor_scalar(halves(G[:, j, :]), prod[j % 2], col_ba[:, j:j + 1], None, ALU.add
                                  ).then_inc(s("gate_read"), 1)

            sqtmp = hflat[:, KF0:KF0 + AH * P]
            eng.wait_ge(s("val_read"), 2 + 16)
            eng.wait_ge(s("consts_loaded"), 48)

            def va_rows(r):
                return (varow[:, r, :], P) if r < NT else (vas, TS)
            for r in range(NT + 1):
                v, n = va_rows(r)
                ch.link(eng.tensor_tensor(sqtmp[0:n], v, v, ALU.mult))
                eng.tensor_reduce(vss[0:n, r, :], sqtmp[0:n].rearrange("p (h c) -> p h c", h=AH), AX, ALU.add
                                  ).then_inc(s("va_squared"), 1)
                eng.wait_ge(s("va_squared"), r + 1)
            eng.wait_ge(s("va_root"), 1)
            ch.link(eng.reciprocal(vss[:, :, :], vss[:, :, :]))
            for r in range(NT + 1):
                v, n = va_rows(r)
                v3 = v.rearrange("p (h c) -> p h c", h=AH)
                ch.link(eng.tensor_tensor(v3, v3, vss[0:n, r, :].unsqueeze(2).broadcast_to([n, AH, P]), ALU.mult))
                eng.tensor_tensor(v, v, gsguB[0:n], ALU.mult).then_inc(s("va_normed"), 1)

            for h in range(AH):
                eng.wait_ge(s("sgu_done"), h + 1)
                eng.tensor_tensor(gated, pt[h % 4].rearrange("p (r t) -> p r t", r=NT),
                                  bsB[:, h, :].unsqueeze(1).broadcast_to([P, NT, P]), ALU.add).then_inc(s("sgu_read"), 1)
                eng.wait_ge(s("sgu_read"), h + 1)
                if h == 0:
                    eng.wait_ge(s("u_acted"), 8)
                ch.link(eng.tensor_tensor(mT[:, h, 0:TP].rearrange("p (r t) -> p r t", r=NT),
                                          mT[:, h, 0:TP].rearrange("p (r t) -> p r t", r=NT), gated, ALU.mult))

            Gf = rq[:, 2 * BH * T:3 * BH * T]
            eng.wait_ge(s("gate_ln"), 3)
            ch.link(eng.tensor_scalar(Gf, Gf, 0.0, None, ALU.min))
            ch.link(eng.tensor_tensor(Gf, Gf, gates_tmp, ALU.subtract))
            ch.link(eng.tensor_scalar(gates_tmp, Gf, 1.0 / TAU, None, ALU.mult))
            lg = gates_tmp.rearrange("p (h t) -> p h t", h=BH)
            for j in range(BH):
                for r in range(NT):
                    eng.tensor_tensor_scan(G[:, j, r * P:(r + 1) * P], ones[:, :], lg[:, j, r * P:(r + 1) * P], 0.0,
                                           ALU.mult, ALU.add)
            ch.link(eng.tensor_copy(G[:, :, TP:T], lg[:, :, TP:T]))
            s3 = smix.rearrange("p (h c) -> p h c", h=AH)
            ch.link(eng.tensor_tensor(s3, vas.rearrange("p (h c) -> p h c", h=AH),
                                      w00B[0:TS].unsqueeze(2).broadcast_to([TS, AH, P]), ALU.mult))
            eng.tensor_tensor(s3, s3, bsB[0:TS, :, 0:1].broadcast_to([TS, AH, P]), ALU.add).then_inc(s("sgu_sample"), 1)
            eng.memset(scT, 0.0)
            eng.wait_ge(s("sgu_done"), AH + 1)
            eng.tensor_tensor(mT[:, 0:AH, TP:T], mT[:, 0:AH, TP:T], pt[0][:, 0:AH * TS].rearrange("p (h c) -> p h c", h=AH),
                              ALU.mult).then_inc(s("sgu_read"), 1)

            eng.wait_ge(s("r_acted"), 8)
            with eng.Fori(0, BH) as j:
                st = ch.enter(j, 1)
                Gr = G[:, j, 0:TP].rearrange("p (r t) -> p r t", r=NT)
                kr = kT[:, j, 0:TP].rearrange("p (r t) -> p r t", r=NT)
                Gs = G[:, j, 0:TP].rearrange("p (a t) -> p a t", t=SUB)
                eng.tensor_tensor(qf.rearrange("p (a t) -> p a t", t=SUB), Gs,
                                  Gs[:, :, REF:REF + 1].broadcast_to([P, NT * NSUB, SUB]), ALU.subtract
                                  ).then_inc(s("diffs_ready"), 1)
                for a in range(NSUB):
                    n = SUB * (a + 1)
                    eng.tensor_tensor(kf_i[a], Gr[:, :, a * SUB + REF:a * SUB + REF + 1].broadcast_to([P, NT, n]),
                                      Gr[:, :, 0:n], ALU.subtract).then_inc(s("diffs_ready"), 1)
                kd3 = kd.rearrange("p (r t) -> p r t", r=NT)
                eng.tensor_tensor(kd3, Gr[:, :, P - 1:P].broadcast_to([P, NT, P]), Gr, ALU.subtract
                                  ).then_inc(s("diffs_ready"), 1)
                eng.wait_ge(s("exps_ready"), j * 3 + 3)
                eng.tensor_tensor(qf, qf, qT[:, j, 0:TP], ALU.mult).then_inc(s("factors_ready"), 1)
                for a in range(NSUB):
                    eng.tensor_tensor(kf_i[a], kf_i[a], kr[:, :, 0:SUB * (a + 1)], ALU.mult).then_inc(s("factors_ready"), 1)
                eng.tensor_tensor(kd, kd, kT[:, j, 0:TP], ALU.mult).then_inc(s("factors_ready"), 1)
                eng.tensor_tensor(qd, qd, qT[:, j, 0:TP], ALU.mult).then_inc(s("factors_ready"), 1)
                eng.wait_ge(s("scores_done"), j + 1)
                for a in range(NSUB):
                    n, c = SUB * (a + 1), a * SUB
                    eng.tensor_tensor(scT[0:n, :, c:c + SUB], pt[1][0:n].rearrange("p (r t) -> p r t", r=NT)[:, :, c:c + SUB],
                                      tri[0:n, c:c + SUB].unsqueeze(1).broadcast_to([n, NT, SUB]), ALU.mult
                                      ).then_inc(s("scores_masked"), 1)
                eng.wait_ge(s("state_stored"), j * 16 + 16)
                for r in range(NT):
                    eng.wait_ge(s("state_part"), j * NT + (r + 1))
                    part = pg[0][:, r % 2, 0:BV]
                    if r == 0:
                        eng.tensor_copy(gstate, part).then_inc(s("state_ready"), 1)
                        continue
                    if r < NT - 1:
                        eng.wait_ge(s("state_used"), j * (NT - 2) + r)
                    else:
                        eng.wait_ge(s("o_done"), j + 1)
                    eng.wait_ge(s("state_ready"), j * NT + r)
                    eng.scalar_tensor_tensor(gstate, gstate, glast[:, r:r + 1], part, ALU.mult, ALU.add
                                             ).then_inc(s("state_ready"), 1)
                eng.wait_ge(s("o_root"), j + 1)
                ch.link(eng.reciprocal(rs[:, 0:NT], ss[:, 0:NT]))
                for r in range(NT):
                    eng.tensor_scalar(on[:, r, :], pt[2 + r // 2][:, (r % 2) * BV:(r % 2 + 1) * BV], rs[:, r:r + 1], None,
                                      ALU.mult).then_inc(s("o_normed"), 1)
                eng.wait_ge(s("o_turned"), j + 1)
                for v in range(NV):
                    m = mT[:, j * NV + (AH + v), 0:TP]
                    eng.scalar_tensor_tensor(m, pg[1][:, v, :], col_gla[:, bass.ds(j * NV + v, 1)], m, ALU.mult, ALU.mult
                                             ).then_inc(s("head_out"), 1)
            ch.leave(st, BH)

            eng.wait_ge(s("ks_ready"), 2)
            with eng.Fori(0, TS // 2) as i:
                for a in range(2):
                    eng.wait_ge(s("outer_done"), i * 2 + (a + 1))
                    eng.tensor_scalar(km, kss, ident[0:TS, bass.ds(i * 2 + a, 1)], None, ALU.mult).then_inc(s("km_ready"), 1)
                    eng.wait_ge(s("outer_done"), i * 2 + (a + 2))
                    eng.wait_ge(s(f"sstate_loaded{a}"), i * 16 + 16)
                    for h in range(BH):
                        ins = eng.scalar_tensor_tensor(stin[a][:, h, :], stin[a][:, h, :], ea[:, h, bass.ds(i * 2 + a, 1)],
                                                       pg[h // 2][:, 0, (h % 2) * BV:(h % 2 + 1) * BV], ALU.mult, ALU.add)
                    ins.then_inc(s("sstate_read"), 1)
            eng.wait_ge(s("os_root"), 1)
            ch.link(eng.reciprocal(roS, roS))
            for v in range(NV):
                ch.link(eng.tensor_tensor(oS[:, :, v, :], oS[:, :, v, :], roS, ALU.mult))
            for h in range(BH):
                for v in range(NV):
                    m = mT[:, AH + h * NV + v, TP:T]
                    ins = eng.scalar_tensor_tensor(m, oS[:, h, v, :], col_gla[:, h * NV + v:h * NV + v + 1], m, ALU.mult, ALU.mult)
            ins.then_inc(s("gla_sample_done"), 1)

            read_loop(out0, 16, lambda n, a: eng.tensor_tensor(x2[:, n], x2[:, n], prod[a], ALU.add))
            for a in range(2):
                eng.wait_ge(s(f"sstate_stored{a}"), 16 * (TS // 2 + 1))
            eng.wait_ge(s("state_stored"), 16 * (BH + 1))
            eng.wait_ge(s("product_read"), 2 + xq0)
            norm_operand(1, col_xq)
            read_loop(xq0, 16, lambda n, a: eng.scalar_tensor_tensor(
                m2[:, n], prod[a], float(XD) ** -0.5, rstdB[:, :, :], ALU.mult, ALU.mult))

            for u in range(XH * NT):
                a = u % 2
                eng.wait_ge(s("xscores_done"), u + 1)
                ch.link(eng.tensor_reduce(ss[:, 4 + a:5 + a], pt[a][:, 0:M], AX, ALU.max))
                eng.tensor_scalar(ss[:, 6 + a:7 + a], ss[:, 4 + a:5 + a], -1.0, None, ALU.mult).then_inc(s("p_max"), 1)
                eng.wait_ge(s("p_exp"), u + 1)
                ch.link(eng.reciprocal(rs[:, 4 + a:5 + a], ss[:, 8 + a:9 + a]))
                eng.tensor_scalar(stg[:, a, 0:M], stg[:, a, 0:M], rs[:, 4 + a:5 + a], None, ALU.mult).then_inc(s("p_ready"), 1)

            eng.wait_ge(s("qs_copied"), 1)
            eng.wait_ge(s("p_turned"), XH * NT)
            with eng.Fori(0, TS) as b:
                st = ch.enter(b, 0)
                eng.wait_ge(s("qB_done"), b + 1)
                for c in range(4):
                    ins = eng.tensor_scalar(qmask[c], srow[0:TS, c * 512:(c + 1) * 512], ident[0:TS, bass.ds(b, 1)], None,
                                            ALU.mult)
                ins.then_inc(s("qmask_ready"), 1)
                eng.wait_ge(s("qB_done"), b + 2)
                for a in range(2):
                    eng.wait_ge(s(f"cache_loaded{a}"), b * 16 + 16)
                    for h in range(XH):
                        keys = kv_ring[a][:, h * XD:(h + 1) * XD]
                        ins = eng.tensor_tensor_reduce(keys, keys, pt[h], 1.0, 0.0, ALU.mult, ALU.add, ssc[:, a, h:h + 1])
                    ins.then_inc(s(f"cache_used{a}"), 1)
                for a in range(2):
                    eng.wait_ge(s(f"cache_used{a}"), b + 2)
                eng.tensor_copy(sS[:, :, :, b], ssc).then_inc(s("ss_ready"), 1)
            ch.leave(st, TS)
            NS = XH * TS
            eng.wait_ge(s("ss_turned"), 1)
            ch.link(eng.tensor_reduce(ss[0:NS, 4:5], pt[0][0:NS, 0:M], AX, ALU.max))
            eng.tensor_scalar(ss[0:NS, 6:7], ss[0:NS, 4:5], -1.0, None, ALU.mult).then_inc(s("p_max"), 1)
            eng.wait_ge(s("pS_exp"), 1)
            ch.link(eng.reciprocal(rs[0:NS, 4:5], ss[0:NS, 8:9]))
            eng.tensor_scalar(pS, pS, rs[0:NS, 4:5], None, ALU.mult).then_inc(s("pS_ready"), 1)

            read_loop(xo0, 16, lambda n, a: eng.tensor_tensor(x2[:, n], x2[:, n], prod[a], ALU.add))
            eng.wait_ge(s("product_read"), 2 + pq0)
            norm_operand(2, col_ffn)
            read_loop(pq0, 16, lambda n, a: eng.tensor_tensor(m2[:, n], prod[a], rstdB[:, :, :], ALU.mult))

            eng.wait_ge(s("iota_made"), 1)
            eng.wait_ge(s("product_read"), 2 + pq0 + 16)
            ch.link(eng.tensor_copy(jota, jint))
            eng.wait_ge(s("peer_consts"), 32)

            def passed():
                eng.sem_inc(s("dve_passed"), 1)

            def top16(n, vals, idx, table, rest):
                passed()
                ch.link(eng.max(vals[0:n, 0:8], table[0:n]))
                passed()
                eng.max_index(idx[0:n, 0:8], vals[0:n, 0:8], table[0:n])
                ch.link(eng.match_replace(rest[0:n], vals[0:n, 0:8], table[0:n], NEG))
                passed()
                ch.link(eng.max(vals[0:n, 8:16], rest[0:n]))
                passed()
                ch.link(eng.max_index(idx[0:n, 8:16], vals[0:n, 8:16], rest[0:n]))

            def select_head(n, r, h):
                eng.wait_ge(s("sc_copied"), r * PH + h + 2)
                for c in range(2):
                    top16(n, sv[:, c * 16:c * 16 + 16], si[:, c * 16:c * 16 + 16], sc[:, c * P:(c + 1) * P], sc2[:, c * P:(c + 1) * P])
                shape = [n, TOPK, TOPK]
                c3, o3 = (x[0:n].rearrange("p (i j) -> p i j", i=TOPK) for x in (cand, onehot))
                eng.tensor_copy(sif[0:n], si[0:n])
                ch.link(eng.tensor_tensor(c3, sv[0:n, 0:16].unsqueeze(2).broadcast_to(shape),
                                          sv[0:n, 16:32].unsqueeze(1).broadcast_to(shape), ALU.add))
                top16(n, ts, pos, cand, cand2)
                eng.tensor_scalar(ntop[0:n], ts[0:n, 0:1], -1.0, None, ALU.mult).then_inc(s("top_ready"), 1)
                eng.tensor_scalar(posi[0:n], pos[0:n], 4, None, ALU.logical_shift_right)
                ch.link(eng.tensor_scalar(posj[0:n], pos[0:n], 15, None, ALU.bitwise_and))
                eng.tensor_copy(pif[0:n], posi[0:n])
                ch.link(eng.tensor_copy(pjf[0:n], posj[0:n]))
                for c, (pf, out) in enumerate(((pif, pa), (pjf, pb))):
                    ch.link(eng.tensor_tensor(o3, jota[0:n].unsqueeze(1).broadcast_to(shape),
                                              pf[0:n].unsqueeze(2).broadcast_to(shape), ALU.is_equal))
                    ch.link(eng.tensor_tensor(o3, o3, sif[0:n, c * 16:c * 16 + 16].unsqueeze(1).broadcast_to(shape), ALU.mult))
                    ch.link(eng.tensor_reduce(out[0:n], o3, AX, ALU.add))
                at = bass.ds(h * TOPK, TOPK)
                ch.link(eng.scalar_tensor_tensor(pa[0:n], pa[0:n], float(P), pb[0:n], ALU.mult, ALU.add))
                if n == P:
                    eng.tensor_copy(idx_all[:, at], pa)
                else:
                    eng.tensor_copy(idxf_all[0:n, at], pa[0:n])
                eng.wait_ge(s("top_exp"), r * PH + h + 1)
                ch.link(eng.reciprocal(erec[0:n], esum[0:n]))
                eng.tensor_scalar(gate_all[0:n, at], ex[0:n], erec[0:n], None, ALU.mult).then_inc(s("head_selected"), 1)

            def norm_rows(n, r):
                eng.wait_ge(s("xrow_root"), r + 1)
                ch.link(eng.reciprocal(rs[0:n, 0:1], ss[0:n, 0:1]))
                eng.scalar_tensor_tensor(hrow[0:n], xrow[0:n], rs[0:n, 0:1], gffnB[0:n], ALU.mult, ALU.mult
                                         ).then_inc(s("hrow_ready"), 1)
                eng.wait_ge(s("hrow_ready"), r + 1)
                passed()

            def finish(n, r):
                eng.wait_ge(s("y_root"), r + 1)
                ch.link(eng.reciprocal(rs[0:n, 0:1], ss[0:n, 3:4]))
                eng.wait_ge(s("y_stored"), r * 16 + 16)
                for a in range(2):
                    ins = eng.scalar_tensor_tensor(ystage[0:n, a * 1024:(a + 1) * 1024].rearrange("p (c d) -> p c d", c=2),
                                                   pg[a][0:n], rs[0:n, 0:1],
                                                   gfinB[0:n, a * 1024:(a + 1) * 1024].rearrange("p (c d) -> p c d", c=2),
                                                   ALU.mult, ALU.mult)
                ins.then_inc(s("y_ready"), 1)

            SEL = 23
            with eng.Fori(0, NT) as r:
                sr = ch.enter(r, SEL * PH + 4)
                with eng.Fori(0, PH) as h:
                    sh = ch.enter(h, SEL)
                    select_head(P, r, h)
                ch.leave(sh, PH)
                eng.wait_ge(s("head_selected"), r * PH + PH + 1)
                eng.sem_inc(s("picks_ready"), 1)
                norm_rows(P, r)
                with eng.Fori(0, E // 4) as g:
                    for c in range(4):
                        eng.wait_ge(s(f"u_loaded{c}"), (r * (E // 4) + g) * 16 + 16)
                        eng.wait_ge(s("act_read"), r * E + g * 4 + (c + 1))
                        eng.tensor_tensor_reduce(urow[c], urow[c], hrow, 1.0, 0.0, ALU.mult, ALU.add, act4[:, c:c + 1]
                                                 ).then_inc(s("u_used"), 1)
                eng.wait_ge(s("y_squared"), r + 1)
                ch.link(eng.tensor_tensor(ss[:, 3:4], ss[:, 1:2], ss[:, 2:3], ALU.add))
                ch.link(eng.tensor_scalar(ss[:, 3:4], ss[:, 3:4], 1.0, None, ALU.mult))
                eng.sem_inc(s("y_summed"), 1)
                finish(P, r)
            ch.leave(sr, NT)

            with eng.Fori(0, PH) as h:
                sh = ch.enter(h, SEL)
                select_head(TS, NT, h)
            ch.leave(sh, PH)
            eng.wait_ge(s("head_selected"), NT * PH + PH + 1)
            eng.sem_inc(s("picks_made"), 1)
            eng.wait_ge(s("picks_turned"), 1)
            eng.tensor_copy(idxS, pt[1][:, 0:TS])
            eng.tensor_copy(gateS, pt[1][:, TS:2 * TS]).then_inc(s("picks_ready"), 1)
            norm_rows(TS, NT)
            eng.wait_ge(s("y_stored"), 16 * (NT + 1))
            for t in range(TS):
                c = t % 4
                if t >= 1:
                    eng.wait_ge(s("hB_done"), t)
                eng.tensor_scalar(ystage[0:TS], hrow[0:TS], ident[0:TS, t:t + 1], None, ALU.mult).then_inc(s("hmask_ready"), 1)
                eng.wait_ge(s("hB_done"), t + 1)
                eng.wait_ge(s(f"u_loaded{c}"), (NT * E // 4 + t // 4 + 1) * 16)
                eng.wait_ge(s("act_read"), NT * E + t + 1)
                eng.tensor_tensor_reduce(urow[c], urow[c], pt4[:, :, :].rearrange("p a d -> p (a d)"), 1.0, 0.0, ALU.mult,
                                         ALU.add, act4[:, c:c + 1]).then_inc(s("u_used"), 1)
            eng.wait_ge(s("y_squared"), NT + 1)
            ch.link(eng.tensor_tensor(ss[0:TS, 3:4], ss[0:TS, 1:2], ss[0:TS, 2:3], ALU.add))
            eng.sem_inc(s("y_summed"), 1)
            finish(TS, NT)

        @block.scalar
        def _(eng):
            ch = Chain(eng, s("act_chain"))
            act = eng.activation
            for name, n in (("memrow_ready", 2), ("val_read", 2), ("os_read", 1), ("oxs_read", 1), ("sc_copied", 1), ("act_read", 4)):
                eng.sem_inc(s(name), n)
            eng.wait_ge(s("ones_ready"), 3)
            for item in range(2):
                eng.wait_ge(s(f"rows_loaded{item}"), 16)
                ch.link(act(hflat[:, 2048:4096], rowbuf[:, item, :], ACT.Square, accum_out=ss[:, item:item + 1]))
                act(ss[:, item:item + 1], ss[:, item:item + 1], ACT.Sqrt, bias=epsT[:, :], scale=1.0 / D).then_inc(s("mem_root"), 1)

            for b0 in (xk0, xv0):
                with eng.Fori(0, KD // 2) as i:
                    for slot in range(2):
                        eng.wait_ge(s("mem_turned"), i * 2 + (b0 + slot + 3))
                        eng.wait_ge(s(f"memrow_stored{slot}"), i * 16 + (b0 // 2 + 1) * 16)
                        eng.copy(rq[:, slot * M:(slot + 1) * M], pt[slot][:, 0:M]).then_inc(s("memrow_ready"), 1)

            def norm_squares(n):
                with eng.Fori(0, KD // 2) as i:
                    for a in range(2):
                        eng.wait_ge(s("sq_used"), i * 2 + (n * KD + a + 1))
                        act(sq[:, a, :], xT[:, i * 2 + a, :], ACT.Square).then_inc(s("sq_ready"), 1)
                eng.wait_ge(s("sq_used"), 2 + (n + 1) * KD)
                act(rstdB[:, :, :], pt4[:, 0:2, 0:HALF], ACT.Sqrt, bias=epsT[:, :], scale=1.0 / D).then_inc(s("norm_root"), 1)

            eng.wait_ge(s("turn_read"), 28)
            norm_squares(0)
            with eng.Fori(0, 4) as i:
                for a in range(2):
                    eng.wait_ge(s("product_read"), i * 2 + (in0 + a + 3))
                    act(mT[:, i * 2 + a, :], mT[:, i * 2 + a, :], ACT.Gelu_apprx_tanh).then_inc(s("u_acted"), 1)

            def value_rows(i, a, first, rows, srows):
                eng.wait_ge(s("val_turned"), i * 2 + (first + a + 3))
                at = bass.ds((i * 2 + a) * P, P)
                eng.copy(rows[:, :, at], pt[a].rearrange("p (r c) -> p r c", r=NT))
                eng.copy(srows[:, at], pt[2 + a][0:TS, 0:P]).then_inc(s("val_read"), 1)

            with eng.Fori(0, 4) as i:
                for a in range(2):
                    eng.wait_ge(s("product_read"), i * 2 + (in0 + 8 + a + 3))
                    act(stg[:, a, :], stg[:, a, :], ACT.Gelu_apprx_tanh).then_inc(s("val_staged"), 1)
                for a in range(2):
                    value_rows(i, a, 0, varow, vas)
            with eng.Fori(0, 4) as i:
                for a in range(2):
                    value_rows(i, a, 8, vrow, vbs)
            with eng.Fori(0, 4) as i:
                for a in range(2):
                    eng.wait_ge(s("product_read"), i * 2 + (in0 + 32 + a + 3))
                    m = mT[:, i * 2 + (AH + a), :]
                    act(m, m, ACT.Silu).then_inc(s("r_acted"), 1)
            eng.wait_ge(s("va_squared"), NT + 1)
            act(vss[:, :, :], vss[:, :, :], ACT.Sqrt, bias=epsT[:, :], scale=1.0 / P).then_inc(s("va_root"), 1)
            eng.wait_ge(s("gate_read"), BH)
            act(gates_tmp, rq[:, 2 * BH * T:3 * BH * T], ACT.Abs).then_inc(s("gate_ln"), 1)
            eng.wait_ge(s("gate_ln"), 1)
            act(gates_tmp, gates_tmp, ACT.Exp, scale=-1.0).then_inc(s("gate_ln"), 1)
            eng.wait_ge(s("gate_ln"), 2)
            act(gates_tmp, gates_tmp, ACT.Ln, bias=1.0).then_inc(s("gate_ln"), 1)

            with eng.Fori(0, BH) as j:
                st = ch.enter(j, 1)
                eng.wait_ge(s("diffs_ready"), j * 6 + 6)
                act(factors, factors, ACT.Exp).then_inc(s("exps_ready"), 1)
                act(qd, G[:, j, 0:TP], ACT.Exp).then_inc(s("exps_ready"), 1)
                act(glast, G[:, j, 0:TP].rearrange("p (r t) -> p r t", r=NT)[:, :, P - 1], ACT.Exp).then_inc(s("exps_ready"), 1)
                eng.wait_ge(s("kd_turned"), j + 1)
                eng.copy(kds, pt[0].rearrange("p (r d) -> p r d", r=NT)).then_inc(s("kds_ready"), 1)
                eng.wait_ge(s("o_done"), j + 1)
                for r in range(NT):
                    ins = act(on[:, r, :], pt[2 + r // 2][:, (r % 2) * BV:(r % 2 + 1) * BV], ACT.Square,
                              accum_out=ss[:, r:r + 1])
                ch.link(ins)
                act(ss[:, 0:NT], ss[:, 0:NT], ACT.Sqrt, bias=epsT[:, :], scale=1.0 / BV).then_inc(s("o_root"), 1)
            ch.leave(st, BH)

            act(ea, G[:, :, TP:T], ACT.Exp).then_inc(s("ks_ready"), 1)
            eng.wait_ge(s("ks_turned"), 1)
            eng.copy(kss, pt[0][0:TS, 0:BH * P]).then_inc(s("ks_ready"), 1)
            with eng.Fori(0, TS) as b:
                eng.wait_ge(s("os_done"), b + 3)
                eng.copy(oS[:, :, :, b], pt[3][:, 0:BH * NV].rearrange("p (h v) -> p h v", h=BH)).then_inc(s("os_read"), 1)
            eng.wait_ge(s("os_read"), TS + 1)
            act(oSq, oS, ACT.Square).then_inc(s("os_squared"), 1)
            eng.wait_ge(s("os_summed"), 1)
            act(roS, pt[0][:, 0:BH * TS].rearrange("p (h b) -> p h b", h=BH), ACT.Sqrt, bias=epsT[:, :], scale=1.0 / BV
                ).then_inc(s("os_root"), 1)

            eng.wait_ge(s("product_read"), 2 + xq0)
            norm_squares(1)

            def p_exp(u):
                a = u % 2
                eng.wait_ge(s("p_max"), u + 1)
                if u >= 2:
                    eng.wait_ge(s("p_turned"), u - 1)
                act(stg[:, a, 0:M], pt[a][:, 0:M], ACT.Exp, bias=ss[:, 6 + a:7 + a], accum_out=ss[:, 8 + a:9 + a]
                    ).then_inc(s("p_exp"), 1)

            def p_rows(u):
                h, r = divmod(u, NT)
                eng.wait_ge(s("p_turned"), u + 1)
                if h >= 2 and r == 0:
                    eng.wait_ge(s("xo_done"), XK * (h - 1))
                eng.copy(pT[h % 2][:, :, r * P:(r + 1) * P], pt[2 + u % 2][:, 0:2 * P].rearrange("p (m t) -> p m t", m=2)
                         ).then_inc(s("pT_ready"), 1)

            def out_rows(h):
                for k in range(XK):
                    n = h * XK + k
                    eng.wait_ge(s("xo_done"), n + 1)
                    eng.copy(hT[:, n, 0:TP], pg[(n % 4) // 2][:, n % 2, :]).then_inc(s("xo_read"), 1)

            for u in range(XH * NT + 1):
                if u < XH * NT:
                    p_exp(u)
                if u >= 1:
                    p_rows(u - 1)
                if u >= 2 and (u - 2) % NT == NT - 1:
                    out_rows((u - 2) // NT)
            out_rows(XH - 1)

            eng.wait_ge(s("qs_turned"), 1)
            eng.copy(srow[0:TS, 0:D].rearrange("p (a d) -> p a d", a=4), pt4[0:TS]).then_inc(s("qs_copied"), 1)
            NS = XH * TS
            eng.wait_ge(s("p_max"), XH * NT + 1)
            act(pS, pt[0][0:NS, 0:M], ACT.Exp, bias=ss[0:NS, 6:7], accum_out=ss[0:NS, 8:9]).then_inc(s("pS_exp"), 1)
            eng.wait_ge(s("pS_turned"), 1)
            eng.copy(pST, pt[1][:, 0:2 * NS].rearrange("p (m c) -> p m c", m=2)).then_inc(s("pST_ready"), 1)
            with eng.Fori(0, TS) as b:
                eng.wait_ge(s("oxs_done"), b + 2)
                eng.copy(hT[:, :, bass.ds(b + TP, 1)], pt[2][:, 0:KD].unsqueeze(2)).then_inc(s("oxs_read"), 1)

            eng.wait_ge(s("product_read"), 2 + pq0)
            norm_squares(2)
            for n in range(4 * NT + 4):
                rows = P if n // 4 < NT else TS
                eng.wait_ge(s("xrow_turned"), n + 1)
                if n >= 2:
                    eng.wait_ge(s(f"x_stored{n % 2}"), 16 * (n // 2))
                eng.copy(xst[n % 2][0:rows], pt[2 + n % 2][0:rows]).then_inc(s("xrow_staged"), 1)
            for n in range(4):
                eng.wait_ge(s("keys_turned"), n + 1)
                eng.copy(skT[:, 4 * n:4 * n + 4, :], pt[2 + n % 2].rearrange("p (n c) -> p n c", n=4)).then_inc(s("keys_read"), 1)

            eng.wait_ge(s("product_read"), 2 + pq0 + 16)

            def select_head(n, r, h, cols):
                eng.copy(qs.rearrange("p (c t) -> p c t", c=2)[:, :, 0:n], cols).then_inc(s("qs_ready"), 1)
                eng.wait_ge(s("sc_done"), r * PH + h + 1)
                eng.wait_ge(s("head_selected"), r * PH + h + 1)
                eng.copy(sc[0:n], pt[0][0:n, 0:2 * P]).then_inc(s("sc_copied"), 1)
                eng.wait_ge(s("top_ready"), r * PH + h + 1)
                act(ex[0:n], ts[0:n], ACT.Exp, bias=ntop[0:n], accum_out=esum[0:n]).then_inc(s("top_exp"), 1)

            def row_root(n, r):
                eng.wait_ge(s("xrow_loaded"), r * 16 + 16)
                ch.link(act(hrow[0:n], xrow[0:n], ACT.Square, accum_out=ss[0:n, 0:1]))
                act(ss[0:n, 0:1], ss[0:n, 0:1], ACT.Sqrt, bias=epsT[0:n], scale=1.0 / D).then_inc(s("xrow_root"), 1)

            def y_root(n, r):
                eng.wait_ge(s("v_used"), r * E + (E + 4) if n == P else NT * E + TS + 4)
                for a in range(2):
                    ins = act(hrow[0:n, a * 1024:(a + 1) * 1024].rearrange("p (c d) -> p c d", c=2), pg[a][0:n], ACT.Square,
                              accum_out=ss[0:n, 1 + a:2 + a])
                ins.then_inc(s("y_squared"), 1)
                eng.wait_ge(s("y_summed"), r + 1)
                act(ss[0:n, 3:4], ss[0:n, 3:4], ACT.Sqrt, bias=epsT[0:n], scale=1.0 / D).then_inc(s("y_root"), 1)

            with eng.Fori(0, NT) as r:
                sr = ch.enter(r, 1 + 2 * E)
                with eng.Fori(0, PH) as h:
                    select_head(P, r, h, mT[:, bass.ds(h * 2, 2), bass.ds(r * P, P)])
                row_root(P, r)
                with eng.Fori(0, E // 4) as g:
                    sg = ch.enter(g, 8)
                    for c in range(4):
                        eng.wait_ge(s("u_used"), r * E + g * 4 + (c + 5))
                        act(g4[:, c:c + 1], act4[:, c:c + 1], ACT.Gelu_apprx_tanh).then_inc(s("act_read"), 1)
                        eng.wait_ge(s("act_read"), r * E + g * 4 + (c + 5))
                        ch.link(act(w4[:, c:c + 1], gate_all[:, bass.ds(g * 4 + c, 1)], ACT.Copy, scale=g4[:, c:c + 1]))
                        eng.wait_ge(s("v_used"), r * E + g * 4 + (c + 1))
                        ch.link(act(diag[c], ident[:, :], ACT.Copy, scale=w4[:, c:c + 1]))
                        eng.sem_inc(s("diag_ready"), 1)
                ch.leave(sg, E // 4)
                y_root(P, r)
            ch.leave(sr, NT)
            with eng.Fori(0, PH) as h:
                select_head(TS, NT, h, mT[:, bass.ds(h * 2, 2), TP:T])
            row_root(TS, NT)
            eng.wait_ge(s("picks_ready"), NT + 1)
            for t in range(TS):
                c = t % 4
                eng.wait_ge(s("u_used"), NT * E + t + 5)
                act(g4[:, c:c + 1], act4[:, c:c + 1], ACT.Gelu_apprx_tanh).then_inc(s("act_read"), 1)
                eng.wait_ge(s("act_read"), NT * E + t + 5)
                ch.link(act(w4[:, c:c + 1], gateS[:, t:t + 1], ACT.Copy, scale=g4[:, c:c + 1]))
                eng.wait_ge(s("v_used"), NT * E + t + 1)
                act(wmask[c], e8[:, t, :], ACT.Copy, scale=w4[:, c:c + 1]).then_inc(s("diag_ready"), 1)
            y_root(TS, NT)


_INS = ["x_prompt", "x_sample", "mem_prompt", "cache_mem_k", "cache_mem_v", "state_gla", "g_mix", "w_in", "w_alpha",
        "b_alpha", "w_s", "b_s", "g_sgu", "g_gla", "w_out", "g_mem", "w_xk", "w_xv", "g_xq", "w_xq", "w_xo", "g_ffn",
        "w_pq", "sub_keys", "u_emb", "v_emb", "g_final"]
_OUTS = [(1, 512, 2048), (8, 1, 2048), (1, 1, 256, 4, 512), (1, 1, 256, 4, 512), (1, 1, 4, 128, 256),
         (1, 8, 4, 128, 256), (1, 1, 128, 8, 128), (1, 8, 1, 8, 128)]


def kernel(**inputs):
    import concourse.bacc as _bacc
    from concourse.bass_utils import run_bass_kernel_spmd as _run

    nc = _bacc.Bacc("TRN2", target_bir_lowering=False, num_devices=1)
    arrays, args = {}, []
    for name in _INS:
        a = np.ascontiguousarray(inputs[name])
        arrays[f"in_{name}_dram"] = a
        args.append(nc.dram_tensor(f"in_{name}_dram", a.shape, mybir.dt.from_np(a.dtype), kind="ExternalInput").ap())
    for i, shape in enumerate(_OUTS):
        args.append(nc.dram_tensor(f"out_{i}_dram", shape, F32, kind="ExternalOutput").ap())
    program(nc, *args)
    r = _run(nc, [arrays], core_ids=[0])
    return tuple(r.results[0][f"out_{i}_dram"] for i in range(len(_OUTS)))
```

```python
from contextlib import ExitStack

import numpy as np

import concourse.bass as bass
from concourse import mybir

F32 = mybir.dt.float32
U32 = mybir.dt.uint32
ALU = mybir.AluOpType
ACT = mybir.ActivationFunctionType
AX = mybir.AxisListType.X

P = 128
EPS = 1e-6
TAU = 16.0
SUB = 32
REF = 15
NEG = -3.0e38


class Chain:

    def __init__(self, eng, sem):
        self.eng, self.sem, self.base, self.local = eng, sem, 0, 0

    def link(self, ins):
        ins.then_inc(self.sem, 1)
        self.local += 1
        self.eng.wait_ge(self.sem, self.base + self.local)

    def enter(self, i, per):
        state = (self.base, self.local, per)
        self.base, self.local = i * per + (self.base + self.local), 0
        return state

    def leave(self, state, count):
        assert self.local == state[2], (self.local, state[2])
        self.base, self.local = state[0], state[1] + count * state[2]


def program(nc, x_prompt, x_sample, mem_prompt, cache_mem_k, cache_mem_v, state_gla, g_mix, w_in, w_alpha,
            b_alpha, w_s, b_s, g_sgu, g_gla, w_out, g_mem, w_xk, w_xv, g_xq, w_xq, w_xo, g_ffn, w_pq,
            sub_keys, u_emb, v_emb, g_final,
            y_prompt, y_sample, mem_k_out, mem_v_out, state_p_out, state_s_out, chunk_p_out, chunk_s_out):
    D = x_prompt.shape[2]
    TP = x_prompt.shape[1]
    TS = x_sample.shape[0]
    T = TP + TS
    HALF = T // 2
    KD = D // P
    NT = TP // P
    M = mem_prompt.shape[1]
    AH = w_s.shape[1]
    BH = state_gla.shape[2]
    BV = state_gla.shape[4]
    NV = BV // P
    XH = cache_mem_k.shape[3]
    XD = cache_mem_k.shape[4]
    XK = XD // P
    PH = sub_keys.shape[1]
    TOPK = 16
    E = PH * TOPK
    RANK = w_alpha.shape[1]
    NSUB = P // SUB
    KF = sum(NT * SUB * (i + 1) for i in range(NSUB))
    assert NT == 4 and KD == 16 and TS == 8 and E == P and T % 2 == 0

    with ExitStack() as ctx:
        def sb(name, shape, dt=F32):
            return ctx.enter_context(nc.sbuf_tensor(name, shape, dt))

        def sem(name):
            return ctx.enter_context(nc.semaphore(name))

        xh = sb("xh", [P, 2, KD, T])
        xT, hT = xh[:, 0], xh[:, 1]
        mflat = sb("mT", [P, KD * T + (NT + 1) * P - T])
        mT = mflat[:, 0:KD * T].rearrange("p (k t) -> p k t", k=KD)
        m2 = mT[:, :, :].rearrange("p k (a t) -> p k a t", a=2)
        x2 = xh[:, 0].rearrange("p k (a t) -> p k a t", a=2)
        hflat = xh[:, 1].rearrange("p k t -> p (k t)")
        ra = sb("ra", [P, 8192])
        rowbuf = ra[:, :].rearrange("p (s d) -> p s d", s=4)
        varow = ra[:, 0:4096].rearrange("p (r c) -> p r c", r=NT)
        vrow = ra[:, 4096:8192].rearrange("p (r c) -> p r c", r=NT)
        kTm = ra[:, 0:4096].rearrange("p (k m) -> p k m", k=KD)
        vmr = ra[:, 4096:8192].rearrange("p (a d) -> p a d", a=2)
        srow = sb("srow", [TS, 2048 + 512])
        vas, vbs, kss = srow[:, 0:1024], srow[:, 1024:2048], srow[:, 2048:2560]
        rq = sb("rq", [P, 3 * BH * T])
        qT = rq[:, 0:BH * T].rearrange("p (h t) -> p h t", h=BH)
        kT = rq[:, BH * T:2 * BH * T].rearrange("p (h t) -> p h t", h=BH)
        G = rq[:, 2 * BH * T:3 * BH * T].rearrange("p (h t) -> p h t", h=BH)
        memT = mT[:, :, 0:M]
        wring = sb("wring", [P, 2, KD, P])
        stg = sb("stg", [P, 2, T])
        rstdB = sb("rstdB", [P, 2, HALF])
        sq = sb("sq", [P, 2, T])
        ident = sb("ident", [P, P])
        ones = sb("ones", [P, P])
        tri = sb("tri", [P, P])
        wsT = sb("wsT", [P, AH, P])
        bsB = sb("bsB", [P, AH, P])
        gsguB = sb("gsguB", [P, AH * P])
        NG = 4 * KD + BH + BH * NV
        gcol = sb("gcol", [P, NG])
        col_mix, col_mem, col_xq, col_ffn = (gcol[:, a * KD:(a + 1) * KD] for a in range(4))
        col_ba = gcol[:, 4 * KD:4 * KD + BH]
        col_gla = gcol[:, 4 * KD + BH:NG]
        w00B = sb("w00B", [P, AH])
        e8 = sb("e8", [P, TS, TS])
        epsT = sb("epsT", [P, 1])
        ss = sb("ss", [P, 16])
        rs = sb("rs", [P, 16])
        srs = sb("srs", [P, 16])
        wg = sb("wg", [P, KD, RANK])
        primer = sb("primer", [1, 7 * 16])
        vss = sb("vss", [P, NT + 1, AH])
        zgT = sq[0:RANK, 0, :]
        walpha = sq[0:RANK, 1, 0:BH * P]

        gates_tmp = hflat[:, 0:BH * T]
        KF0 = BH * T
        kf = hflat[:, KF0:KF0 + KF]
        qf = hflat[:, KF0 + KF:KF0 + KF + TP]
        kd = hflat[:, KF0 + KF + TP:KF0 + KF + 2 * TP]
        qd = hflat[:, KF0 + KF + 2 * TP:KF0 + KF + 3 * TP]
        factors = hflat[:, KF0:KF0 + KF + 2 * TP]
        smix = hflat[0:TS, 0:AH * P]
        stin = [hflat[:, a * 1024:(a + 1) * 1024].rearrange("p (h v) -> p h v", h=BH) for a in range(2)]
        kf_i, at = [], 0
        for i in range(NSUB):
            kf_i.append(kf[:, at:at + NT * SUB * (i + 1)].rearrange("p (r c) -> p r c", r=NT))
            at += NT * SUB * (i + 1)
        SC0 = KF0 + KF + 3 * TP
        scT = hflat[:, SC0:SC0 + TP].rearrange("p (r t) -> p r t", r=NT)
        kds = hflat[:, SC0 + TP:SC0 + 2 * TP].rearrange("p (r d) -> p r d", r=NT)
        GS0 = SC0 + 2 * TP
        gstate = hflat[:, GS0:GS0 + BV]
        on = hflat[:, GS0 + BV:GS0 + BV + NT * BV].rearrange("p (r v) -> p r v", r=NT)
        SM0 = GS0 + BV + NT * BV
        glast = hflat[:, SM0:SM0 + NT]
        gated = hflat[:, SM0 + 4:SM0 + 4 + TP].rearrange("p (r t) -> p r t", r=NT)
        SN0 = SM0 + 4 + TP
        oS = hflat[:, SN0:SN0 + 64].rearrange("p (h v b) -> p h v b", h=BH, v=NV)
        oSq = hflat[:, SN0 + 64:SN0 + 128].rearrange("p (h v b) -> p h v b", h=BH, v=NV)
        ea = hflat[:, SN0 + 128:SN0 + 160].rearrange("p (h b) -> p h b", h=BH)
        roS = hflat[:, SN0 + 160:SN0 + 192].rearrange("p (h b) -> p h b", h=BH)
        km = hflat[0:TS, KF0:KF0 + 512]
        assert SN0 + 192 <= KD * T
        pT = [rq[:, 4096 + a * 1024:4096 + (a + 1) * 1024].rearrange("p (m t) -> p m t", m=2) for a in range(2)]
        k_ring = [rq[:, a * D:(a + 1) * D] for a in range(2)]
        v_ring = [ra[:, a * D:(a + 1) * D] for a in range(4)]
        wsf = wsT[:, :, :].rearrange("p h c -> p (h c)")
        sS = wsf[:, 0:64].rearrange("p (m h b) -> p m h b", m=2, h=XH)
        pS = wsf[0:XH * TS, 128:128 + M]
        pST = wsf[:, 384:448]
        pM = wsf[:, 512:1024].rearrange("p (m h b c) -> p m h b c", m=2, h=XH, b=TS)
        xhf = xh[:, :, :, :].rearrange("p a k t -> p (a k t)")
        urow = [xhf[:, c * D:(c + 1) * D] for c in range(4)]
        vexp = [xhf[:, (4 + c) * D:(5 + c) * D] for c in range(4)]
        skT = ra[:, 0:D].rearrange("p (n c) -> p n c", n=2 * PH)
        xrow, ystage = ra[:, D:2 * D], ra[:, 2 * D:3 * D]
        hrow = [ra[:, 3 * D:4 * D], rq[:, 2 * D:3 * D]]
        skr = ra[:, 3 * D:4 * D].rearrange("p (n c) -> p n c", n=2 * PH)
        xst = [ra[:, D + a * 512:D + (a + 1) * 512] for a in range(2)]
        gffnB, gfinB = rq[:, 0:D], rq[:, D:2 * D]
        pools = [[gsguB[:, :], AH * P], [bsB[:, :, :].rearrange("p h c -> p (h c)"), AH * P], [wsf, AH * P],
                 [stg[:, :, :].rearrange("p a t -> p (a t)"), 2 * T]]

        def work(n, dt=F32):
            pool = next(p for p in pools if p[1] >= n)
            pool[1] -= n
            ap = pool[0][:, pool[1]:pool[1] + n]
            return ap if dt == F32 else ap.bitcast(dt)
        diag = [work(P) for _ in range(4)]
        idx_all, gate_all = [work(E, U32) for _ in range(2)], [work(E) for _ in range(2)]
        idx8, idxS = work(8, U32), work(TS, U32)
        idxf, gateS = work(E), work(TS)
        sc, sc2, cand, cand2 = work(2 * P), work(2 * P), work(2 * P), work(2 * P)
        onehot = work(2 * P)
        qs = work(2 * P)
        sv, si, sif = work(32), work(32, U32), work(32)
        ts, pos, posi, posj = work(TOPK), work(TOPK, U32), work(TOPK, U32), work(TOPK, U32)
        pif, pjf, pa, pb = work(TOPK), work(TOPK), work(TOPK), work(TOPK)
        ex, jota, jint = work(TOPK), work(TOPK), work(TOPK, mybir.dt.int32)
        act4, g4, w4 = work(4), work(4), work(4)
        ntop, esum, erec = work(1), work(1), work(1)
        wmask = [work(TS) for _ in range(4)]

        pg = [ctx.enter_context(nc.psum_tensor(f"pg{i}", [P, 2, 512], F32)) for i in range(2)]
        pt4 = ctx.enter_context(nc.psum_tensor("pt4", [P, 4, 512], F32))
        pt = [pt4[:, i] for i in range(4)]

        def query_bank(b, h):
            return pt[h] if b % 2 == 0 else pg[h // 2][:, h % 2, :]

        kT_scr = nc.dram_tensor("kT_scratch", [KD, P, M], F32, kind="Internal").ap()
        x_scr = nc.dram_tensor("x_scratch", [T, D], F32, kind="Internal").ap()

        S = {}

        def s(name):
            if name not in S:
                S[name] = sem(name)
            return S[name]

        block = ctx.enter_context(nc.Block())

        xk0, xv0, in0, out0, xq0, xo0, pq0 = 0, 16, 32, 72, 88, 104, 120
        stages = [(w_xk, xk0, 16), (w_xv, xv0, 16), (w_in, in0, 40), (w_out, out0, 16), (w_xq, xq0, 16),
                  (w_xo, xo0, 16), (w_pq, pq0, 16)]

        def pe_product(eng, i, slot, b0, moving, width):
            eng.wait_ge(s(f"w_loaded{slot}"), i * 16 + (b0 // 2 + 1) * 16)
            eng.wait_ge(s("product_read"), i * 2 + (b0 + slot + 1))
            for k in range(KD):
                if width == T:
                    for a in range(2):
                        mm = eng.matmul(pg[slot][:, a, 0:HALF], wring[:, slot, k], moving[:, k, a * HALF:(a + 1) * HALF],
                                        start=(k == 0), stop=(k == KD - 1))
                else:
                    mm = eng.matmul(pg[slot][:, 0, 0:width], wring[:, slot, k], moving[:, k, 0:width],
                                    start=(k == 0), stop=(k == KD - 1))
            mm.then_inc(s("product_done"), 1)

        def await_product(eng, i, slot, b0):
            eng.wait_ge(s("product_done"), i * 2 + (b0 + slot + 1))

        item_rows = [P, P, P, P, P, P, TS]

        @block.sync
        def _(eng):
            def load_rows(item):
                if item >= 4:
                    eng.wait_ge(s("turned"), 3 + 4 * (item - 3))
                src = (mem_prompt[0, item * P:(item + 1) * P, :] if item < 2 else
                       x_prompt[0, (item - 2) * P:(item - 1) * P, :] if item < 6 else x_sample[:, 0, :])
                eng.dma_start(rowbuf[0:item_rows[item], item % 4, :], src).then_inc(s(f"rows_loaded{item % 4}"), 16)

            def load_weights(w, b0, count, first):
                wv = w[0, :, 0:count * P].rearrange("(k p) (n c) -> n p k c", p=P, c=P)
                start = 0
                if first:
                    start = 1
                    for slot in range(2):
                        eng.dma_start(wring[:, slot], wv[slot]).then_inc(s(f"w_loaded{slot}"), 16)
                    for item in range(4, 7):
                        load_rows(item)
                with eng.Fori(start, count // 2) as i:
                    for slot in range(2):
                        eng.wait_ge(s("product_done"), i * 2 + (b0 + slot - 1))
                        eng.dma_start(wring[:, slot], wv[i * 2 + slot]).then_inc(s(f"w_loaded{slot}"), 16)

            for a, g in enumerate((g_mix, g_mem, g_xq, g_ffn)):
                eng.dma_start(stg[a * KD:(a + 1) * KD, 0, 0:P], g[0].rearrange("(k p) -> k p", p=P)).then_inc(s("gains_loaded"), 16)
            eng.dma_start(stg[4 * KD:4 * KD + BH, 0, 0:P], b_alpha[0].rearrange("(k p) -> k p", p=P)).then_inc(s("gains_loaded"), 16)
            eng.dma_start(stg[4 * KD + BH:NG, 0, 0:P], g_gla[0].rearrange("h (v p) -> (h v) p", p=P)).then_inc(s("gains_loaded"), 16)
            for item in range(4):
                load_rows(item)
            first = True
            for n, (w, b0, count) in enumerate(stages):
                load_weights(w, b0, count, first)
                first = False

            eng.sem_inc(s("y_stored"), 16)
            def load_xrow(r):
                n = P if r < NT else TS
                eng.dma_start(xrow[0:n], x_scr[r * P:r * P + n, :]).then_inc(s("xrow_loaded"), 16)

            for a in range(2):
                eng.wait_ge(s(f"x_stored{a}"), 16 * (2 * NT + 2))
            load_xrow(0)
            for r in range(NT + 1):
                if r < NT:
                    eng.wait_ge(s("acc_started"), 4 * (r + 1))
                    eng.wait_ge(s("hrow_ready"), r + 1)
                    load_xrow(r + 1)
                eng.wait_ge(s("y_ready"), r + 2)
                dst = y_prompt[0, r * P:(r + 1) * P, :] if r < NT else y_sample[:, 0, :]
                eng.dma_start(dst, ystage[0:(P if r < NT else TS)]).then_inc(s("y_stored"), 16)
            eng.wait_ge(s("y_stored"), 16 * (NT + 2))

        @block.gpsimd
        def _(eng):
            def passed():
                eng.sem_inc(s("pool_passed"), 1)

            eng.dma_start(hflat[:, 0:AH * P].rearrange("p (h c) -> p h c", h=AH),
                          w_s[0].rearrange("h t s -> t h s")).then_inc(s("ws_loaded"), 16)
            eng.memset(ident[:, :], 0.0).then_inc(s("pool_set"), 1)
            eng.memset(tri[:, :], 1.0).then_inc(s("pool_set"), 1)
            eng.memset(e8[:, :, :], 0.0).then_inc(s("pool_set"), 1)
            eng.memset(mflat[:, KD * T:], 0.0)
            eng.wait_ge(s("pool_set"), 3)
            eng.affine_select(out=ident[:, :], in_=ident[:, :], compare_op=ALU.not_equal, fill=1.0, base=0,
                              pattern=[[-1, P]], channel_multiplier=1).then_inc(s("masks_ready"), 1)
            eng.affine_select(out=tri[:, :], in_=tri[:, :], compare_op=ALU.is_ge, fill=0.0, base=0,
                              pattern=[[1, P]], channel_multiplier=-1).then_inc(s("masks_ready"), 1)
            eng.affine_select(out=e8[:, :, :], in_=e8[:, :, :], compare_op=ALU.not_equal, fill=1.0, base=0,
                              pattern=[[1, TS], [-1, TS]], channel_multiplier=0).then_inc(s("masks_ready"), 1)
            eng.wait_ge(s("ws_loaded"), 16)
            wsrow = hflat[:, 0:AH * P].rearrange("p (h c) -> p h c", h=AH)
            eng.affine_select(out=wsrow, in_=wsrow, compare_op=ALU.is_ge, fill=0.0, base=0,
                              pattern=[[0, AH], [-1, P]], channel_multiplier=1).then_inc(s("ws_masked"), 1)
            eng.dma_start(bsB[:, :, :].rearrange("p h c -> p (h c)"),
                          b_s[0].rearrange("h c -> (h c)").partition_broadcast(P)).then_inc(s("consts_loaded"), 16)
            eng.dma_start(gsguB[:, :], g_sgu[0].rearrange("h c -> (h c)").partition_broadcast(P)).then_inc(s("consts_loaded"), 16)
            eng.dma_start(w00B[0:TS, :], w_s[0, :, 0, 0:1].rearrange("h c -> (h c)").partition_broadcast(TS),
                          allow_slow_non_contiguous=True).then_inc(s("consts_loaded"), 16)
            eng.dma_start(wg[:, :, :], w_in[0, :, 40 * P:40 * P + RANK].rearrange("(k p) c -> p k c", p=P)).then_inc(s("wg_loaded"), 16)
            for n, name in enumerate(("kT_stored0", "kT_stored1", "memrow_stored0", "memrow_stored1", "state_stored",
                                      "sstate_stored0", "sstate_stored1")):
                eng.dma_start(primer[:, n * 16:(n + 1) * 16], g_final[0:16].partition_broadcast(1)).then_inc(s(name), 16)

            for kv, dst in enumerate((mem_k_out, mem_v_out)):
                rows = dst[0, 0].rearrange("(a m) h d -> m a (h d)", a=2).rearrange("m a (n c) -> n m a c", c=P)
                with eng.Fori(0, KD // 2) as i:
                    for slot in range(2):
                        if kv == 0:
                            eng.wait_ge(s("product_read"), i * 2 + (xk0 + slot + 3))
                            passed()
                            eng.dma_start(kT_scr[i * 2 + slot], stg[:, slot, 0:M]).then_inc(s(f"kT_stored{slot}"), 16)
                        eng.wait_ge(s("memrow_ready"), i * 2 + (kv * KD + slot + 3))
                        passed()
                        eng.dma_start(rows[i * 2 + slot], rq[:, slot * M:(slot + 1) * M].rearrange("p (a c) -> p a c", a=2)
                                      ).then_inc(s(f"memrow_stored{slot}"), 16)

            eng.wait_ge(s("sq_used"), 2 + KD)
            eng.dma_start(walpha, w_alpha[0]).then_inc(s("walpha_loaded"), 16)
            eng.wait_ge(s("va_normed"), NT + 1)
            eng.dma_start(chunk_p_out[0, 0].rearrange("t h c -> t (h c)"), varow[:, NT - 1, :]).then_inc(s("chunk_stored"), 16)
            eng.dma_start(chunk_s_out[0, :, 0].rearrange("t h c -> t (h c)"), vas).then_inc(s("chunk_stored"), 16)

            with eng.Fori(0, BH) as j:
                eng.wait_ge(s("state_ready"), j * NT + NT)
                passed()
                eng.dma_start(state_p_out[0, 0][j], hflat[:, GS0:GS0 + BV]).then_inc(s("state_stored"), 16)

            eng.wait_ge(s("head_out"), 2 + 2 * BH)
            with eng.Fori(0, TS // 2) as i:
                for a in range(2):
                    eng.wait_ge(s(f"sstate_stored{a}"), i * 16 + 16)
                    eng.wait_ge(s("os_done"), i * 2 + (a + 1))
                    passed()
                    eng.dma_start(stin[a], state_gla[0][i * 2 + a].rearrange("h d v -> d h v")).then_inc(s(f"sstate_loaded{a}"), 16)
                for a in range(2):
                    eng.wait_ge(s("sstate_read"), i * 2 + (a + 2))
                    passed()
                    eng.dma_start(state_s_out[0][i * 2 + a].rearrange("h d v -> d h v"), stin[a]).then_inc(s(f"sstate_stored{a}"), 16)

            eng.wait_ge(s("gla_sample_done"), 1)
            for slot in range(2):
                eng.wait_ge(s(f"kT_stored{slot}"), 16 * (KD // 2 + 1))
                eng.wait_ge(s(f"memrow_stored{slot}"), 16 * (KD + 1))
            eng.wait_ge(s("chunk_stored"), 32)
            eng.dma_start(kTm, kT_scr.rearrange("k p m -> p k m")).then_inc(s("attn_loaded"), 16)
            eng.dma_start(vmr, mem_v_out[0, 0].rearrange("(a m) h d -> m a (h d)", a=2)).then_inc(s("attn_loaded"), 16)
            cv = cache_mem_k[0].rearrange("b (a m) h d -> b a m (h d)", a=2)
            with eng.Fori(0, TS) as b:
                for a in range(2):
                    eng.wait_ge(s(f"cache_used{a}"), b + 1)
                    passed()
                    eng.dma_start(k_ring[a], cv[b, a]).then_inc(s(f"cache_loaded{a}"), 16)
            cv = cache_mem_v[0].rearrange("b (a m) h d -> b a m (h d)", a=2)
            eng.wait_ge(s("xo_done"), KD)
            for b in range(TS):
                for a in range(2):
                    n = b * 2 + a
                    if n >= 4:
                        eng.wait_ge(s("vcache_used"), n - 3)
                    eng.dma_start(v_ring[n % 4], cv[b, a]).then_inc(s(f"vcache_loaded{n % 4}"), 16)

            for n in range(4 * NT + 4):
                eng.wait_ge(s("xrow_staged"), n + 1)
                r, c = divmod(n, 4)
                rows = P if r < NT else TS
                eng.dma_start(x_scr[r * P:r * P + rows, c * 512:(c + 1) * 512],
                              xst[n % 2][0:rows]).then_inc(s(f"x_stored{n % 2}"), 16)

            for a in range(2):
                eng.wait_ge(s(f"x_stored{a}"), 16 * (2 * NT + 2))
            eng.dma_start(gffnB, g_ffn[0].partition_broadcast(P)).then_inc(s("peer_consts"), 16)
            eng.dma_start(gfinB, g_final.partition_broadcast(P)).then_inc(s("peer_consts"), 16)
            for h in range(0, 16, 4):
                eng.dma_start(skr[:, h:h + 4, :], sub_keys[0].rearrange("h c n d -> n (h c) d")[:, h:h + 4, :]).then_inc(s("keys_loaded"), 16)
            eng.iota(jint, pattern=[[1, TOPK]], base=0, channel_multiplier=0
                     ).then_inc(s("iota_made"), 1)
            def gather_tile(r, p):
                eng.wait_ge(s("head_selected"), r * PH + (PH + 1))
                passed()
                with eng.Fori(0, E // 8) as g:
                    for half in range(2):
                        c0 = half * 4
                        eng.wait_ge(s("u_used"), r * E + g * 8 + (c0 + 1))
                        eng.wait_ge(s("v_used"), r * E + g * 8 + (c0 + 1))
                        eng.tensor_copy(idx8[:, c0:c0 + 4], idx_all[p][:, bass.ds(g * 8 + c0, 4)]).then_inc(s("idx_copied"), 1)
                        for c in range(4):
                            if c == 0:
                                eng.wait_ge(s("idx_copied"), r * (E // 4) + g * 2 + (half + 1))
                            eng.wait_ge(s("u_used"), r * E + g * 8 + (c0 + c + 1))
                            passed()
                            eng.indirect_dma_start(urow[c], None, u_emb[0], bass.IndirectOffsetOnAxis(ap=idx8[:, c0 + c:c0 + c + 1], axis=0)
                                                   ).then_inc(s(f"u_loaded{c}"), 16)
                            eng.wait_ge(s("v_used"), r * E + g * 8 + (c0 + c + 1))
                            passed()
                            eng.indirect_dma_start(vexp[c], None, v_emb[0], bass.IndirectOffsetOnAxis(ap=idx8[:, c0 + c:c0 + c + 1], axis=0)
                                                   ).then_inc(s(f"v_loaded{c}"), 16)

            eng.wait_ge(s("product_read"), 2 + pq0 + 16)
            with eng.Fori(0, NT // 2) as i:
                for p in range(2):
                    gather_tile(i * 2 + p, p)
            eng.wait_ge(s("picks_ready"), 1)
            for t in range(TS):
                c = t % 4
                eng.wait_ge(s("u_used"), NT * E + t + 1)
                eng.indirect_dma_start(urow[c], None, u_emb[0], bass.IndirectOffsetOnAxis(ap=idxS[:, t:t + 1], axis=0)
                                       ).then_inc(s(f"u_loaded{c}"), 16)
                eng.wait_ge(s("v_used"), NT * E + t + 1)
                eng.indirect_dma_start(vexp[c], None, v_emb[0], bass.IndirectOffsetOnAxis(ap=idxS[:, t:t + 1], axis=0)
                                       ).then_inc(s(f"v_loaded{c}"), 16)
            eng.wait_ge(s("state_stored"), 16 * (BH + 1))
            for a in range(2):
                eng.wait_ge(s(f"sstate_stored{a}"), 16 * (TS // 2 + 1))

        @block.tensor
        def _(eng):
            def turn(out, src, n):
                return eng.transpose(out, src, ident[0:n, 0:n])

            def product_loop(b0, count, moving, width, after=None):
                with eng.Fori(0, count // 2) as i:
                    for slot in range(2):
                        pe_product(eng, i, slot, b0, moving, width)
                    if after:
                        after(i)

            def norm_sum(n):
                def add(i, a, start):
                    eng.wait_ge(s("sq_ready"), i * 2 + (n * KD + a + 1))
                    for c in range(2):
                        mm = eng.matmul(pt[c][:, 0:HALF], ones[:, :], sq[:, a, c * HALF:(c + 1) * HALF],
                                        start=start, stop=True, skip_group_check=True)
                    mm.then_inc(s("sq_used"), 1)
                for a in range(2):
                    add(0, a, a == 0)
                with eng.Fori(1, KD // 2) as i:
                    for a in range(2):
                        add(i, a, False)

            eng.sem_inc(s("mem_turned"), 2)
            eng.sem_inc(s("val_turned"), 2)
            eng.sem_inc(s("sq_used"), 2)
            eng.sem_inc(s("outer_done"), 1)
            eng.sem_inc(s("os_done"), 2)
            eng.sem_inc(s("v_used"), 4)

            unit = 0

            def turn_unit(pieces):
                nonlocal unit
                if unit >= 4:
                    eng.wait_ge(s("turn_read"), unit - 3)
                for dst, src, n in pieces:
                    mm = turn(dst, src, n)
                mm.then_inc(s("turned"), 1)
                unit += 1

            eng.wait_ge(s("masks_ready"), 1)
            eng.wait_ge(s("gains_loaded"), 96)
            turn_unit([(pt[0][:, 0:NG], stg[0:NG, 0, 0:P], NG)])
            eng.wait_ge(s("ws_masked"), 1)
            for u in range(2):
                turn_unit([(pt[unit % 4][:, a * P:(a + 1) * P], hflat[:, (4 * u + a) * P:(4 * u + a + 1) * P], P)
                           for a in range(4)])
            for item in range(7):
                if item < 2:
                    eng.wait_ge(s("mem_scaled"), item + 1)
                else:
                    eng.wait_ge(s(f"rows_loaded{item % 4}"), 16 * (item // 4 + 1))
                if item < 6:
                    for g in range(4):
                        turn_unit([(pt[unit % 4][:, a * P:(a + 1) * P],
                                    rowbuf[:, item % 4, (4 * g + a) * P:(4 * g + a + 1) * P], P) for a in range(4)])
                else:
                    turn_unit([(pt[unit % 4][:, k * TS:(k + 1) * TS], rowbuf[0:TS, item % 4, k * P:(k + 1) * P], TS)
                               for k in range(KD)])

            eng.wait_ge(s("turn_read"), unit)
            for b0 in (xk0, xv0):
                def mem_rows(i):
                    for slot in range(2):
                        eng.wait_ge(s("product_read"), i * 2 + (b0 + slot + 3))
                        eng.wait_ge(s("memrow_ready"), i * 2 + (b0 + slot + 1))
                        for a in range(2):
                            mm = turn(pt[slot][:, a * P:(a + 1) * P], stg[:, slot, a * P:(a + 1) * P], P)
                        mm.then_inc(s("mem_turned"), 1)
                product_loop(b0, 16, memT, M, mem_rows)

            eng.wait_ge(s("memrow_ready"), 2 + 2 * KD)
            norm_sum(0)
            eng.wait_ge(s("ht_ready"), KD)
            eng.wait_ge(s("wg_loaded"), 16)
            for c in range(2):
                for k in range(KD):
                    mm = eng.matmul(pt[2 + c][0:RANK, 0:HALF], wg[:, k], hT[:, k, c * HALF:(c + 1) * HALF],
                                    start=(k == 0), stop=(k == KD - 1))
            mm.then_inc(s("zg_done"), 1)
            product_loop(in0, 8, hT, T)
            eng.wait_ge(s("zg_read"), 1)

            def value_rows(first):
                def after(i):
                    for slot in range(2):
                        if first == 0:
                            eng.wait_ge(s("val_staged"), i * 2 + (slot + 1))
                        else:
                            eng.wait_ge(s("product_read"), i * 2 + (in0 + 24 + slot + 3))
                        eng.wait_ge(s("val_read"), i * 2 + (first + slot + 1))
                        for r in range(NT):
                            turn(pt[slot][:, r * P:(r + 1) * P], stg[:, slot, r * P:(r + 1) * P], P)
                        turn(pt[2 + slot][0:TS, 0:P], stg[:, slot, TP:T], P).then_inc(s("val_turned"), 1)
                return after
            eng.wait_ge(s("norm_root"), 1)
            product_loop(in0 + 8, 8, hT, T, value_rows(0))
            product_loop(in0 + 16, 8, hT, T)
            product_loop(in0 + 24, 8, hT, T, value_rows(8))
            product_loop(in0 + 32, 8, hT, T)

            eng.wait_ge(s("val_read"), 2 + 16)
            eng.wait_ge(s("walpha_loaded"), 16)
            for j in range(BH):
                eng.wait_ge(s("product_read"), 2 + out0)
                if j >= 2:
                    eng.wait_ge(s("gate_read"), j - 1)
                for c in range(2):
                    mm = eng.matmul(pg[j % 2][:, c, 0:HALF], walpha[:, j * P:(j + 1) * P],
                                    zgT[:, c * HALF:(c + 1) * HALF], start=True, stop=True)
                mm.then_inc(s("gate_done"), 1)

            for h in range(AH):
                if h < NT:
                    eng.wait_ge(s("va_normed"), NT + 1)
                else:
                    eng.wait_ge(s("sgu_read"), h - 3)
                for r in range(NT):
                    mm = eng.matmul(pt[h % 4][:, r * P:(r + 1) * P], varow[:, r, h * P:(h + 1) * P], wsT[:, h],
                                    start=True, stop=True)
                mm.then_inc(s("sgu_done"), 1)
            eng.wait_ge(s("sgu_read"), AH)
            eng.wait_ge(s("sgu_sample"), 1)
            for h in range(AH):
                mm = turn(pt[0][:, h * TS:(h + 1) * TS], smix[:, h * P:(h + 1) * P], TS)
            mm.then_inc(s("sgu_done"), 1)

            eng.wait_ge(s("sgu_read"), AH + 1)
            eng.wait_ge(s("gate_read"), BH)
            with eng.Fori(0, BH) as j:
                eng.wait_ge(s("factors_ready"), j * 7 + 7)
                eng.wait_ge(s("head_out"), j * 2 + 2)
                for r in range(NT):
                    mm = turn(pt[0][:, r * P:(r + 1) * P], kd[:, r * P:(r + 1) * P], P)
                mm.then_inc(s("kd_turned"), 1)
                for r in range(NT):
                    for a in range(NSUB):
                        mm = eng.matmul(pt[1][0:SUB * (a + 1), r * P + a * SUB:r * P + (a + 1) * SUB],
                                        kf_i[a][:, r, :], qf[:, r * P + a * SUB:r * P + (a + 1) * SUB],
                                        start=True, stop=True)
                mm.then_inc(s("scores_done"), 1)
                eng.wait_ge(s("scores_masked"), j * NSUB + NSUB)
                eng.wait_ge(s("kds_ready"), j + 1)
                for r in range(NT):
                    v = vrow[:, r, bass.ds(j * BV, BV)]
                    if r >= 2:
                        eng.wait_ge(s("state_ready"), j * NT + (r - 1))
                    eng.matmul(pg[0][:, r % 2, 0:BV], kds[:, r, :], v, start=True, stop=True).then_inc(s("state_part"), 1)
                    out = pt[2 + r // 2][:, (r % 2) * BV:(r % 2 + 1) * BV]
                    mm = eng.matmul(out, scT[:, r, :], v, start=True, stop=(r == 0))
                    if r >= 1:
                        eng.wait_ge(s("state_ready"), j * NT + r)
                        mm = eng.matmul(out, qd[:, r * P:(r + 1) * P], gstate, start=False, stop=True)
                        if r < NT - 1:
                            mm.then_inc(s("state_used"), 1)
                mm.then_inc(s("o_done"), 1)
                eng.wait_ge(s("o_normed"), j * NT + NT)
                for v in range(NV):
                    for r in range(NT):
                        mm = turn(pg[1][:, v, r * P:(r + 1) * P], on[:, r, v * P:(v + 1) * P], P)
                mm.then_inc(s("o_turned"), 1)

            eng.wait_ge(s("head_out"), 2 + 2 * BH)
            for j in range(BH):
                mm = turn(pt[0][0:TS, j * P:(j + 1) * P], kT[:, j, TP:T], P)
            mm.then_inc(s("ks_turned"), 1)
            with eng.Fori(0, TS // 2) as i:
                for a in range(2):
                    eng.wait_ge(s("km_ready"), i * 2 + (a + 1))
                    eng.wait_ge(s("sstate_read"), i * 2 + (a + 1))
                    for j in range(BH):
                        mm = eng.matmul(pg[j // 2][:, 0, (j % 2) * BV:(j % 2 + 1) * BV], km[:, j * P:(j + 1) * P],
                                        vbs[:, j * BV:(j + 1) * BV], start=True, stop=True)
                    mm.then_inc(s("outer_done"), 1)
                    eng.wait_ge(s("sstate_read"), i * 2 + (a + 2))
                    eng.wait_ge(s("os_read"), i * 2 + (a + 1))
                    st = stin[a]
                    for j in range(BH):
                        for v in range(NV):
                            mm = eng.matmul(pt[3][:, j * NV + v:j * NV + v + 1], st[:, j, v * P:(v + 1) * P],
                                            qT[:, j, bass.ds(i * 2 + (TP + a), 1)], start=True, stop=True)
                    mm.then_inc(s("os_done"), 1)
            eng.wait_ge(s("os_squared"), 1)
            for v in range(NV):
                mm = eng.matmul(pt[0][:, 0:BH * TS], ones[:, :], oSq[:, :, v, :], start=(v == 0), stop=(v == NV - 1))
            mm.then_inc(s("os_summed"), 1)

            eng.wait_ge(s("gla_sample_done"), 1)
            product_loop(out0, 16, mT, T)
            eng.wait_ge(s("product_read"), 2 + xq0)
            norm_sum(1)
            eng.wait_ge(s("ht_ready"), 2 * KD)
            product_loop(xq0, 16, hT, T)
            eng.wait_ge(s("product_read"), 2 + xo0)
            eng.wait_ge(s("attn_loaded"), 32)
            eng.wait_ge(s("norm_root"), 2)

            units = [(h, r) for h in range(XH) for r in range(NT)]

            def scores(u):
                h, r = units[u]
                if u >= 2:
                    eng.wait_ge(s("p_exp"), u - 1)
                for k in range(XK):
                    mm = eng.matmul(pt[u % 2][:, 0:M], mT[:, h * XK + k, r * P:(r + 1) * P], kTm[:, h * XK + k, :],
                                    start=(k == 0), stop=(k == XK - 1))
                mm.then_inc(s("xscores_done"), 1)

            def turn_p(u):
                eng.wait_ge(s("p_ready"), u + 1)
                if u >= 2:
                    eng.wait_ge(s("pT_ready"), u - 1)
                for a in range(2):
                    mm = turn(pt[2 + u % 2][:, a * P:(a + 1) * P], stg[:, u % 2, a * P:(a + 1) * P], P)
                mm.then_inc(s("p_turned"), 1)

            def values(h):
                eng.wait_ge(s("pT_ready"), NT * (h + 1))
                for k in range(XK):
                    n = h * XK + k
                    if n >= 4:
                        eng.wait_ge(s("xo_read"), n - 3)
                    bank = pg[(n % 4) // 2][:, n % 2, :]
                    for a in range(2):
                        mm = eng.matmul(bank, vmr[:, a, n * P:(n + 1) * P], pT[h % 2][:, a, :], start=(a == 0), stop=(a == 1))
                    mm.then_inc(s("xo_done"), 1)

            for u in range(len(units) + 1):
                if u < len(units):
                    scores(u)
                if u >= 1:
                    turn_p(u - 1)
                if u >= 2 and (u - 2) % NT == NT - 1:
                    values((u - 2) // NT)
            values(XH - 1)

            eng.wait_ge(s("pT_ready"), len(units))
            for k in range(KD):
                mm = turn(pt[k // 4][0:TS, (k % 4) * P:(k % 4 + 1) * P], mT[:, k, TP:T], P)
            mm.then_inc(s("qs_turned"), 1)
            eng.wait_ge(s("qs_copied"), 1)
            eng.wait_ge(s("xo_read"), KD)
            for b in range(TS):
                if b >= 2:
                    eng.wait_ge(s("cache_used1"), b)
                for c in range(XH):
                    mm = eng.matmul(query_bank(b, c), ident[0:TS, b:b + 1].broadcast_to([TS, P]),
                                    srow[0:TS, c * XD:(c + 1) * XD], start=True, stop=True)
                mm.then_inc(s("qB_done"), 1)
            eng.wait_ge(s("cache_used1"), TS + 1)
            for a in range(2):
                mm = turn(pt[0][0:XH * TS, a * P:(a + 1) * P], wsf[:, a * 32:(a + 1) * 32], P)
            mm.then_inc(s("ss_turned"), 1)
            eng.wait_ge(s("pS_ready"), 1)
            for a in range(2):
                mm = turn(pt[1][:, a * 32:(a + 1) * 32], pS[:, a * P:(a + 1) * P], XH * TS)
            mm.then_inc(s("pS_turned"), 1)
            eng.wait_ge(s("pM_ready"), 1)
            for b in range(TS):
                for a in range(2):
                    n = b * 2 + a
                    eng.wait_ge(s(f"vcache_loaded{n % 4}"), 16 * (n // 4 + 1))
                    for h in range(XH):
                        mm = eng.matmul(pg[h // 2][0:TS, h % 2, :], pM[:, a, h, b, :], v_ring[n % 4][:, h * XD:(h + 1) * XD],
                                        start=(n == 0), stop=(n == 2 * TS - 1), skip_group_check=True)
                    mm.then_inc(s("vcache_used"), 1)
            eng.wait_ge(s("oxs_copied"), 1)
            for k in range(KD):
                mm = turn(pt[2][:, k * TS:(k + 1) * TS], srow[0:TS, k * P:(k + 1) * P], TS)
            mm.then_inc(s("oxs_turned"), 1)
            eng.wait_ge(s("oxs_read"), 1)
            product_loop(xo0, 16, hT, T)
            eng.wait_ge(s("product_read"), 2 + pq0)
            norm_sum(2)
            for n in range(4 * NT + 4):
                r, c = divmod(n, 4)
                if n >= 2:
                    eng.wait_ge(s("xrow_staged"), n - 1)
                for a in range(4):
                    k = 4 * c + a
                    src = xT[:, k, r * P:(r + 1) * P] if r < NT else xT[:, k, TP:T]
                    mm = turn(pt[2 + n % 2][0:(P if r < NT else TS), a * P:(a + 1) * P], src, P)
                mm.then_inc(s("xrow_turned"), 1)
            eng.wait_ge(s("xrow_staged"), 4 * NT + 4)
            for n in range(4):
                eng.wait_ge(s("keys_loaded"), 64)
                if n >= 2:
                    eng.wait_ge(s("keys_read"), n - 1)
                for a in range(4):
                    mm = turn(pt[2 + n % 2][:, a * P:(a + 1) * P], skr[:, 4 * n + a, :], P)
                mm.then_inc(s("keys_turned"), 1)
            eng.wait_ge(s("ht_ready"), 3 * KD)
            eng.wait_ge(s("keys_read"), 4)

            def key_scores(r, h):
                eng.wait_ge(s("qs_ready"), r * PH + h + 1)
                eng.wait_ge(s("sc_copied"), r * PH + h + 1)
                for c in range(2):
                    mm = eng.matmul(pt[0][:, c * P:(c + 1) * P], qs[:, c * P:(c + 1) * P], skT[:, h * 2 + c, :],
                                    start=True, stop=True)
                mm.then_inc(s("sc_done"), 1)

            for slot in range(2):
                pe_product(eng, 0, slot, pq0, hT, T)
            with eng.Fori(0, PH - 1) as h:
                pe_product(eng, h + 1, 0, pq0, hT, T)
                key_scores(0, h)
                pe_product(eng, h + 1, 1, pq0, hT, T)
            key_scores(0, PH - 1)
            eng.wait_ge(s("product_read"), 2 + pq0 + 16)

            def acc(c):
                return pg[c // 2][:, c % 2, :]

            def tile_sum(r):
                eng.wait_ge(s("xrow_loaded"), r * 16 + 16)
                eng.wait_ge(s("y_ready"), r + 1)
                for c in range(4):
                    eng.matmul(acc(c), ident[:, :], xrow[:, c * 512:(c + 1) * 512], start=True, stop=True
                               ).then_inc(s("acc_started"), 1)
                with eng.Fori(0, PH) as h:
                    key_scores(r + 1, h)
                    with eng.Fori(0, TOPK // 4) as g:
                        for c in range(4):
                            eng.wait_ge(s("diag_ready"), r * E + h * TOPK + g * 4 + (c + 1))
                            eng.wait_ge(s(f"v_loaded{c}"), (r * (E // 4) + h * (TOPK // 4) + g) * 16 + 16)
                            for d in range(4):
                                mm = eng.matmul(acc(d), diag[c], vexp[c][:, d * 512:(d + 1) * 512], start=False, stop=True,
                                                skip_group_check=True)
                            mm.then_inc(s("v_used"), 1)

            with eng.Fori(0, NT // 2) as i:
                for p in range(2):
                    tile_sum(i * 2 + p)
            eng.wait_ge(s("picks_made"), 1)
            turn(pt[1][:, 0:TS], idxf[0:TS, :], TS)
            turn(pt[1][:, TS:2 * TS], gate_all[0][0:TS, :], TS).then_inc(s("picks_turned"), 1)
            eng.wait_ge(s("xrow_loaded"), (NT + 1) * 16)
            eng.wait_ge(s("y_ready"), NT + 1)
            eng.wait_ge(s("picks_ready"), 1)
            for c in range(4):
                eng.matmul(acc(c)[0:TS], ident[0:TS, 0:TS], xrow[0:TS, c * 512:(c + 1) * 512], start=True, stop=True
                           ).then_inc(s("acc_started"), 1)

            def spread(t):
                eng.wait_ge(s("u_used"), NT * E + t + 4)
                for c in range(4):
                    mm = eng.matmul(pt[c][:, :], ident[0:TS, t:t + 1].broadcast_to([TS, P]),
                                    hrow[0][0:TS, c * 512:(c + 1) * 512], start=True, stop=True)
                mm.then_inc(s("hB_done"), 1)

            spread(0)
            for t in range(TS):
                if t + 1 < TS:
                    spread(t + 1)
                c = t % 4
                eng.wait_ge(s("diag_ready"), NT * E + t + 1)
                eng.wait_ge(s(f"v_loaded{c}"), (NT * E // 4 + t // 4 + 1) * 16)
                for d in range(4):
                    mm = eng.matmul(acc(d)[0:TS], wmask[c], vexp[c][:, d * 512:(d + 1) * 512], start=False, stop=True,
                                    skip_group_check=True)
                mm.then_inc(s("v_used"), 1)

        @block.vector
        def _(eng):
            ch = Chain(eng, s("dve_chain"))
            for name, n in (("product_read", 2), ("head_out", 2), ("sstate_read", 1), ("cache_used0", 1),
                            ("cache_used1", 1), ("u_used", 4), ("y_ready", 1), ("head_selected", 1)):
                eng.sem_inc(s(name), n)
            eng.memset(ones[:, :], 1.0).then_inc(s("ones_ready"), 1)
            eng.memset(epsT[:, :], EPS).then_inc(s("ones_ready"), 1)
            eng.memset(vss[:, :, :], 1.0).then_inc(s("ones_ready"), 1)
            eng.wait_ge(s("ones_ready"), 3)

            for item in range(2):
                eng.wait_ge(s("mem_root"), item + 1)
                ch.link(eng.reciprocal(rs[:, item:item + 1], ss[:, item:item + 1]))
                eng.tensor_scalar(rowbuf[:, item, :], rowbuf[:, item, :], rs[:, item:item + 1], None, ALU.mult
                                  ).then_inc(s("mem_scaled"), 1)
            unit = 0

            def take(ins_of):
                nonlocal unit
                eng.wait_ge(s("turned"), unit + 1)
                ins_of(pt[unit % 4]).then_inc(s("turn_read"), 1)
                unit += 1

            take(lambda t: eng.tensor_copy(gcol[:, :], t[:, 0:NG]))
            for u in range(2):
                take(lambda t: eng.tensor_copy(wsT[:, 4 * u:4 * u + 4, :], t.rearrange("p (h c) -> p h c", h=4)))
            eng.wait_ge(s("turn_read"), 1)
            for item in range(2):
                for g in range(4):
                    take(lambda t: eng.tensor_tensor(
                        memT[:, 4 * g:4 * g + 4, item * P:(item + 1) * P], t.rearrange("p (k c) -> p k c", k=4),
                        col_mem[:, 4 * g:4 * g + 4].unsqueeze(2).broadcast_to([P, 4, P]), ALU.mult))
            for r in range(NT):
                for g in range(4):
                    take(lambda t: eng.tensor_copy(xT[:, 4 * g:4 * g + 4, r * P:(r + 1) * P],
                                                   t.rearrange("p (k c) -> p k c", k=4)))
            take(lambda t: eng.tensor_copy(xT[:, :, TP:T], t[:, 0:P].rearrange("p (k c) -> p k c", k=KD)))

            for kv, b0 in enumerate((xk0, xv0)):
                if kv:
                    for slot in range(2):
                        eng.wait_ge(s(f"kT_stored{slot}"), 16 * (KD // 2 + 1))
                with eng.Fori(0, KD // 2) as i:
                    for slot in range(2):
                        await_product(eng, i, slot, b0)
                        eng.wait_ge(s("mem_turned"), i * 2 + (b0 + slot + 1))
                        if not kv:
                            eng.wait_ge(s(f"kT_stored{slot}"), i * 16 + 16)
                        eng.tensor_copy(stg[:, slot, 0:M], pg[slot][:, 0, 0:M]).then_inc(s("product_read"), 1)

            def norm_operand(n, col):
                with eng.Fori(0, KD // 2) as i:
                    for a in range(2):
                        eng.tensor_scalar(hT[:, i * 2 + a, :], xT[:, i * 2 + a, :], col[:, bass.ds(i * 2 + a, 1)], None,
                                          ALU.mult).then_inc(s("ht_ready"), 1)
                eng.wait_ge(s("norm_root"), n + 1)
                ch.link(eng.reciprocal(rstdB[:, :, :], rstdB[:, :, :]))

            def read_loop(b0, count, ins_of, before=None):
                with eng.Fori(0, count // 2) as i:
                    for slot in range(2):
                        await_product(eng, i, slot, b0)
                        if before:
                            before(i, slot)
                        ins_of(i * 2 + slot, slot).then_inc(s("product_read"), 1)

            def halves(ap):
                return ap.rearrange("p (a t) -> p a t", a=2)

            eng.wait_ge(s("turn_read"), unit)
            norm_operand(0, col_mix)
            eng.wait_ge(s("zg_done"), 1)
            eng.tensor_tensor(halves(zgT), pt4[0:RANK, 2:4, 0:HALF], rstdB[0:RANK], ALU.mult).then_inc(s("zg_read"), 1)
            prod = [pg[a][:, :, 0:HALF] for a in range(2)]
            read_loop(in0, 8, lambda n, a: eng.tensor_tensor(m2[:, n], prod[a], rstdB[:, :, :], ALU.mult))
            eng.wait_ge(s("mem_turned"), 2 + 2 * KD)
            read_loop(in0 + 8, 8, lambda n, a: eng.tensor_tensor(halves(stg[:, a, :]), prod[a], rstdB[:, :, :], ALU.mult),
                      lambda i, a: eng.wait_ge(s("val_turned"), i * 2 + (a + 1)))
            for slot in range(2):
                eng.wait_ge(s(f"memrow_stored{slot}"), 16 * (KD + 1))
            read_loop(in0 + 16, 4, lambda n, a: eng.scalar_tensor_tensor(
                halves(qT[:, n, :]), prod[a], float(P) ** -0.5, rstdB[:, :, :], ALU.mult, ALU.mult))
            read_loop(in0 + 20, 4, lambda n, a: eng.tensor_tensor(halves(kT[:, n, :]), prod[a], rstdB[:, :, :], ALU.mult))
            read_loop(in0 + 24, 8, lambda n, a: eng.tensor_tensor(halves(stg[:, a, :]), prod[a], rstdB[:, :, :], ALU.mult),
                      lambda i, a: eng.wait_ge(s("val_turned"), i * 2 + (8 + a + 1)))
            read_loop(in0 + 32, 8, lambda n, a: eng.tensor_tensor(m2[:, n + 8], prod[a], rstdB[:, :, :], ALU.mult))

            for j in range(BH):
                eng.wait_ge(s("gate_done"), j + 1)
                eng.tensor_scalar(halves(G[:, j, :]), prod[j % 2], col_ba[:, j:j + 1], None, ALU.add
                                  ).then_inc(s("gate_read"), 1)

            sqtmp = hflat[:, KF0:KF0 + AH * P]
            eng.wait_ge(s("val_read"), 2 + 16)
            eng.wait_ge(s("consts_loaded"), 48)

            def va_rows(r):
                return (varow[:, r, :], P) if r < NT else (vas, TS)
            for r in range(NT + 1):
                v, n = va_rows(r)
                ch.link(eng.tensor_tensor(sqtmp[0:n], v, v, ALU.mult))
                eng.tensor_reduce(vss[0:n, r, :], sqtmp[0:n].rearrange("p (h c) -> p h c", h=AH), AX, ALU.add
                                  ).then_inc(s("va_squared"), 1)
                eng.wait_ge(s("va_squared"), r + 1)
            eng.wait_ge(s("va_root"), 1)
            ch.link(eng.reciprocal(vss[:, :, :], vss[:, :, :]))
            for r in range(NT + 1):
                v, n = va_rows(r)
                v3 = v.rearrange("p (h c) -> p h c", h=AH)
                ch.link(eng.tensor_tensor(v3, v3, vss[0:n, r, :].unsqueeze(2).broadcast_to([n, AH, P]), ALU.mult))
                eng.tensor_tensor(v, v, gsguB[0:n], ALU.mult).then_inc(s("va_normed"), 1)

            for h in range(AH):
                eng.wait_ge(s("sgu_done"), h + 1)
                eng.tensor_tensor(gated, pt[h % 4].rearrange("p (r t) -> p r t", r=NT),
                                  bsB[:, h, :].unsqueeze(1).broadcast_to([P, NT, P]), ALU.add).then_inc(s("sgu_read"), 1)
                eng.wait_ge(s("sgu_read"), h + 1)
                if h == 0:
                    eng.wait_ge(s("u_acted"), 8)
                ch.link(eng.tensor_tensor(mT[:, h, 0:TP].rearrange("p (r t) -> p r t", r=NT),
                                          mT[:, h, 0:TP].rearrange("p (r t) -> p r t", r=NT), gated, ALU.mult))

            Gf = rq[:, 2 * BH * T:3 * BH * T]
            eng.wait_ge(s("gate_ln"), 3)
            ch.link(eng.tensor_scalar(Gf, Gf, 0.0, None, ALU.min))
            ch.link(eng.tensor_tensor(Gf, Gf, gates_tmp, ALU.subtract))
            ch.link(eng.tensor_scalar(gates_tmp, Gf, 1.0 / TAU, None, ALU.mult))
            lg = gates_tmp.rearrange("p (h t) -> p h t", h=BH)
            for j in range(BH):
                for r in range(NT):
                    eng.tensor_tensor_scan(G[:, j, r * P:(r + 1) * P], ones[:, :], lg[:, j, r * P:(r + 1) * P], 0.0,
                                           ALU.mult, ALU.add)
            ch.link(eng.tensor_copy(G[:, :, TP:T], lg[:, :, TP:T]))
            s3 = smix.rearrange("p (h c) -> p h c", h=AH)
            ch.link(eng.tensor_tensor(s3, vas.rearrange("p (h c) -> p h c", h=AH),
                                      w00B[0:TS].unsqueeze(2).broadcast_to([TS, AH, P]), ALU.mult))
            eng.tensor_tensor(s3, s3, bsB[0:TS, :, 0:1].broadcast_to([TS, AH, P]), ALU.add).then_inc(s("sgu_sample"), 1)
            eng.memset(scT, 0.0)
            eng.wait_ge(s("sgu_done"), AH + 1)
            eng.tensor_tensor(mT[:, 0:AH, TP:T], mT[:, 0:AH, TP:T], pt[0][:, 0:AH * TS].rearrange("p (h c) -> p h c", h=AH),
                              ALU.mult).then_inc(s("sgu_read"), 1)

            eng.wait_ge(s("r_acted"), 8)
            with eng.Fori(0, BH) as j:
                st = ch.enter(j, 1)
                Gr = G[:, j, 0:TP].rearrange("p (r t) -> p r t", r=NT)
                kr = kT[:, j, 0:TP].rearrange("p (r t) -> p r t", r=NT)
                Gs = G[:, j, 0:TP].rearrange("p (a t) -> p a t", t=SUB)
                eng.tensor_tensor(qf.rearrange("p (a t) -> p a t", t=SUB), Gs,
                                  Gs[:, :, REF:REF + 1].broadcast_to([P, NT * NSUB, SUB]), ALU.subtract
                                  ).then_inc(s("diffs_ready"), 1)
                for a in range(NSUB):
                    n = SUB * (a + 1)
                    eng.tensor_tensor(kf_i[a], Gr[:, :, a * SUB + REF:a * SUB + REF + 1].broadcast_to([P, NT, n]),
                                      Gr[:, :, 0:n], ALU.subtract).then_inc(s("diffs_ready"), 1)
                kd3 = kd.rearrange("p (r t) -> p r t", r=NT)
                eng.tensor_tensor(kd3, Gr[:, :, P - 1:P].broadcast_to([P, NT, P]), Gr, ALU.subtract
                                  ).then_inc(s("diffs_ready"), 1)
                eng.wait_ge(s("exps_ready"), j * 3 + 3)
                eng.tensor_tensor(qf, qf, qT[:, j, 0:TP], ALU.mult).then_inc(s("factors_ready"), 1)
                for a in range(NSUB):
                    eng.tensor_tensor(kf_i[a], kf_i[a], kr[:, :, 0:SUB * (a + 1)], ALU.mult).then_inc(s("factors_ready"), 1)
                eng.tensor_tensor(kd, kd, kT[:, j, 0:TP], ALU.mult).then_inc(s("factors_ready"), 1)
                eng.tensor_tensor(qd, qd, qT[:, j, 0:TP], ALU.mult).then_inc(s("factors_ready"), 1)
                eng.wait_ge(s("scores_done"), j + 1)
                for a in range(NSUB):
                    n, c = SUB * (a + 1), a * SUB
                    eng.tensor_tensor(scT[0:n, :, c:c + SUB], pt[1][0:n].rearrange("p (r t) -> p r t", r=NT)[:, :, c:c + SUB],
                                      tri[0:n, c:c + SUB].unsqueeze(1).broadcast_to([n, NT, SUB]), ALU.mult
                                      ).then_inc(s("scores_masked"), 1)
                eng.wait_ge(s("state_stored"), j * 16 + 16)
                for r in range(NT):
                    eng.wait_ge(s("state_part"), j * NT + (r + 1))
                    part = pg[0][:, r % 2, 0:BV]
                    if r == 0:
                        eng.tensor_copy(gstate, part).then_inc(s("state_ready"), 1)
                        continue
                    if r < NT - 1:
                        eng.wait_ge(s("state_used"), j * (NT - 2) + r)
                    else:
                        eng.wait_ge(s("o_done"), j + 1)
                    eng.wait_ge(s("state_ready"), j * NT + r)
                    eng.scalar_tensor_tensor(gstate, gstate, glast[:, r:r + 1], part, ALU.mult, ALU.add
                                             ).then_inc(s("state_ready"), 1)
                eng.wait_ge(s("o_root"), j + 1)
                ch.link(eng.reciprocal(rs[:, 0:NT], ss[:, 0:NT]))
                for r in range(NT):
                    eng.tensor_scalar(on[:, r, :], pt[2 + r // 2][:, (r % 2) * BV:(r % 2 + 1) * BV], rs[:, r:r + 1], None,
                                      ALU.mult).then_inc(s("o_normed"), 1)
                eng.wait_ge(s("o_turned"), j + 1)
                for v in range(NV):
                    m = mT[:, j * NV + (AH + v), 0:TP]
                    eng.scalar_tensor_tensor(m, pg[1][:, v, :], col_gla[:, bass.ds(j * NV + v, 1)], m, ALU.mult, ALU.mult
                                             ).then_inc(s("head_out"), 1)
            ch.leave(st, BH)

            eng.wait_ge(s("ks_ready"), 2)
            with eng.Fori(0, TS // 2) as i:
                for a in range(2):
                    eng.wait_ge(s("outer_done"), i * 2 + (a + 1))
                    eng.tensor_scalar(km, kss, ident[0:TS, bass.ds(i * 2 + a, 1)], None, ALU.mult).then_inc(s("km_ready"), 1)
                    eng.wait_ge(s("outer_done"), i * 2 + (a + 2))
                    eng.wait_ge(s(f"sstate_loaded{a}"), i * 16 + 16)
                    for h in range(BH):
                        ins = eng.scalar_tensor_tensor(stin[a][:, h, :], stin[a][:, h, :], ea[:, h, bass.ds(i * 2 + a, 1)],
                                                       pg[h // 2][:, 0, (h % 2) * BV:(h % 2 + 1) * BV], ALU.mult, ALU.add)
                    ins.then_inc(s("sstate_read"), 1)
            eng.wait_ge(s("os_root"), 1)
            ch.link(eng.reciprocal(roS, roS))
            for v in range(NV):
                ch.link(eng.tensor_tensor(oS[:, :, v, :], oS[:, :, v, :], roS, ALU.mult))
            for h in range(BH):
                for v in range(NV):
                    m = mT[:, AH + h * NV + v, TP:T]
                    ins = eng.scalar_tensor_tensor(m, oS[:, h, v, :], col_gla[:, h * NV + v:h * NV + v + 1], m, ALU.mult, ALU.mult)
            ins.then_inc(s("gla_sample_done"), 1)

            read_loop(out0, 16, lambda n, a: eng.tensor_tensor(x2[:, n], x2[:, n], prod[a], ALU.add))
            for a in range(2):
                eng.wait_ge(s(f"sstate_stored{a}"), 16 * (TS // 2 + 1))
            eng.wait_ge(s("state_stored"), 16 * (BH + 1))
            eng.wait_ge(s("product_read"), 2 + xq0)
            norm_operand(1, col_xq)
            read_loop(xq0, 16, lambda n, a: eng.scalar_tensor_tensor(
                m2[:, n], prod[a], float(XD) ** -0.5, rstdB[:, :, :], ALU.mult, ALU.mult))

            for u in range(XH * NT):
                a = u % 2
                eng.wait_ge(s("xscores_done"), u + 1)
                ch.link(eng.tensor_reduce(ss[:, 4 + a:5 + a], pt[a][:, 0:M], AX, ALU.max))
                eng.tensor_scalar(ss[:, 6 + a:7 + a], ss[:, 4 + a:5 + a], -1.0, None, ALU.mult).then_inc(s("p_max"), 1)
                eng.wait_ge(s("p_exp"), u + 1)
                ch.link(eng.reciprocal(rs[:, 4 + a:5 + a], ss[:, 8 + a:9 + a]))
                eng.tensor_scalar(stg[:, a, 0:M], stg[:, a, 0:M], rs[:, 4 + a:5 + a], None, ALU.mult).then_inc(s("p_ready"), 1)

            for b in range(TS):
                eng.wait_ge(s("qB_done"), b + 1)
                for a in range(2):
                    eng.wait_ge(s(f"cache_loaded{a}"), b * 16 + 16)
                    for h in range(XH):
                        keys = k_ring[a][:, h * XD:(h + 1) * XD]
                        ins = eng.tensor_tensor_reduce(keys, keys, query_bank(b, h), 1.0, 0.0, ALU.mult, ALU.add,
                                                       sS[:, a, h, b:b + 1])
                    ins.then_inc(s(f"cache_used{a}"), 1)
            NS = XH * TS
            eng.wait_ge(s("ss_turned"), 1)
            ch.link(eng.tensor_reduce(ss[0:NS, 4:5], pt[0][0:NS, 0:M], AX, ALU.max))
            eng.tensor_scalar(ss[0:NS, 6:7], ss[0:NS, 4:5], -1.0, None, ALU.mult).then_inc(s("p_max"), 1)
            eng.wait_ge(s("pS_exp"), 1)
            ch.link(eng.reciprocal(rs[0:NS, 4:5], ss[0:NS, 8:9]))
            eng.tensor_scalar(pS, pS, rs[0:NS, 4:5], None, ALU.mult).then_inc(s("pS_ready"), 1)
            eng.wait_ge(s("pST_ready"), 1)
            eng.tensor_tensor(pM.rearrange("p m h b c -> p (m h) b c"),
                              pST.rearrange("p (n b) -> p n b", b=TS).unsqueeze(3).broadcast_to([P, 2 * XH, TS, TS]),
                              e8[:, :, :].unsqueeze(1).broadcast_to([P, 2 * XH, TS, TS]), ALU.mult).then_inc(s("pM_ready"), 1)

            read_loop(xo0, 16, lambda n, a: eng.tensor_tensor(x2[:, n], x2[:, n], prod[a], ALU.add))
            eng.wait_ge(s("product_read"), 2 + pq0)
            norm_operand(2, col_ffn)

            eng.wait_ge(s("iota_made"), 1)
            ch.link(eng.tensor_copy(jota, jint))

            def passed():
                eng.sem_inc(s("dve_passed"), 1)

            def top16(vals, idx, table, rest):
                passed()
                ch.link(eng.max(vals[:, 0:8], table))
                passed()
                eng.max_index(idx[:, 0:8], vals[:, 0:8], table)
                ch.link(eng.match_replace(rest, vals[:, 0:8], table, NEG))
                passed()
                ch.link(eng.max(vals[:, 8:16], rest))
                passed()
                ch.link(eng.max_index(idx[:, 8:16], vals[:, 8:16], rest))

            c3, o3 = (x.rearrange("p (i j) -> p i j", i=TOPK) for x in (cand, onehot))
            pairs = [P, TOPK, TOPK]

            def top_half(r, h, c):
                eng.wait_ge(s("sc_copied"), r * PH + h + 2)
                top16(sv[:, c * 16:c * 16 + 16], si[:, c * 16:c * 16 + 16], sc[:, c * P:(c + 1) * P], sc2[:, c * P:(c + 1) * P])

            def top_pairs():
                eng.tensor_copy(sif, si)
                ch.link(eng.tensor_tensor(c3, sv[:, 0:16].unsqueeze(2).broadcast_to(pairs),
                                          sv[:, 16:32].unsqueeze(1).broadcast_to(pairs), ALU.add))
                top16(ts, pos, cand, cand2)
                eng.tensor_scalar(ntop, ts[:, 0:1], -1.0, None, ALU.mult).then_inc(s("top_ready"), 1)

            def keep_picks(r, h, p):
                eng.tensor_scalar(posi, pos, 4, None, ALU.logical_shift_right)
                ch.link(eng.tensor_scalar(posj, pos, 15, None, ALU.bitwise_and))
                eng.tensor_copy(pif, posi)
                ch.link(eng.tensor_copy(pjf, posj))
                for c, (pf, out) in enumerate(((pif, pa), (pjf, pb))):
                    ch.link(eng.tensor_tensor(o3, jota.unsqueeze(1).broadcast_to(pairs),
                                              pf.unsqueeze(2).broadcast_to(pairs), ALU.is_equal))
                    ch.link(eng.tensor_tensor(o3, o3, sif[:, c * 16:c * 16 + 16].unsqueeze(1).broadcast_to(pairs), ALU.mult))
                    ch.link(eng.tensor_reduce(out, o3, AX, ALU.add))
                at = bass.ds(h * TOPK, TOPK)
                ch.link(eng.scalar_tensor_tensor(pa, pa, float(P), pb, ALU.mult, ALU.add))
                eng.tensor_copy(idx_all[p][:, at], pa)
                eng.wait_ge(s("top_exp"), r * PH + h + 1)
                ch.link(eng.reciprocal(erec, esum))
                eng.tensor_scalar(gate_all[p][:, at], ex, erec, None, ALU.mult).then_inc(s("head_selected"), 1)

            def select_head(r, h, p):
                for c in range(2):
                    top_half(r, h, c)
                top_pairs()
                keep_picks(r, h, p)

            def norm_rows(r, p):
                eng.wait_ge(s("xrow_root"), r + 1)
                ch.link(eng.reciprocal(rs[:, 0:1], ss[:, 0:1]))
                eng.scalar_tensor_tensor(hrow[p], xrow, rs[:, 0:1], gffnB, ALU.mult, ALU.mult).then_inc(s("hrow_ready"), 1)
                eng.wait_ge(s("hrow_ready"), r + 1)
                passed()

            def finish(n, r):
                eng.wait_ge(s("y_root"), r + 1)
                ch.link(eng.reciprocal(rs[0:n, 1:2], ss[0:n, 3:4]))
                eng.wait_ge(s("y_stored"), r * 16 + 16)
                for a in range(2):
                    ins = eng.scalar_tensor_tensor(ystage[0:n, a * 1024:(a + 1) * 1024].rearrange("p (c d) -> p c d", c=2),
                                                   pg[a][0:n], rs[0:n, 1:2],
                                                   gfinB[0:n, a * 1024:(a + 1) * 1024].rearrange("p (c d) -> p c d", c=2),
                                                   ALU.mult, ALU.mult)
                ins.then_inc(s("y_ready"), 1)

            SEL = 23

            def query_block(i, slot):
                await_product(eng, i, slot, pq0)
                eng.tensor_tensor(m2[:, i * 2 + slot], prod[slot], rstdB[:, :, :], ALU.mult).then_inc(s("product_read"), 1)

            for slot in range(2):
                query_block(0, slot)
            with eng.Fori(0, PH - 1) as h:
                sh = ch.enter(h, SEL)
                query_block(h + 1, 0)
                select_head(0, h, 0)
                query_block(h + 1, 1)
            ch.leave(sh, PH - 1)
            select_head(0, PH - 1, 0)
            eng.wait_ge(s("peer_consts"), 32)
            norm_rows(0, 0)

            def tile(r, p):
                with eng.Fori(0, PH) as h:
                    sh = ch.enter(h, SEL)
                    for g in range(TOPK // 4):
                        for c in range(4):
                            eng.wait_ge(s(f"u_loaded{c}"), (r * (E // 4) + h * (TOPK // 4)) * 16 + (g * 16 + 16))
                            eng.wait_ge(s("act_read"), r * E + h * TOPK + (g * 4 + c + 1))
                            eng.tensor_tensor_reduce(urow[c], urow[c], hrow[p], 1.0, 0.0, ALU.mult, ALU.add, act4[:, c:c + 1]
                                                     ).then_inc(s("u_used"), 1)
                        if g < 2:
                            top_half(r + 1, h, g)
                        elif g == 2:
                            top_pairs()
                        else:
                            keep_picks(r + 1, h, 1 - p)
                ch.leave(sh, PH)
                norm_rows(r + 1, 1 - p)
                eng.wait_ge(s("y_squared"), r + 1)
                ch.link(eng.tensor_tensor(ss[:, 3:4], ss[:, 1:2], ss[:, 2:3], ALU.add))
                eng.sem_inc(s("y_summed"), 1)
                finish(P, r)

            with eng.Fori(0, NT // 2) as i:
                sr = ch.enter(i, 2 * (SEL * PH + 3))
                for p in range(2):
                    tile(i * 2 + p, p)
            ch.leave(sr, NT // 2)

            ch.link(eng.tensor_copy(idxf, idx_all[0]))
            eng.sem_inc(s("picks_made"), 1)
            eng.wait_ge(s("picks_turned"), 1)
            eng.tensor_copy(idxS, pt[1][:, 0:TS])
            eng.tensor_copy(gateS, pt[1][:, TS:2 * TS]).then_inc(s("picks_ready"), 1)
            for t in range(TS):
                c = t % 4
                eng.wait_ge(s("hB_done"), t + 1)
                eng.wait_ge(s(f"u_loaded{c}"), (NT * E // 4 + t // 4 + 1) * 16)
                eng.wait_ge(s("act_read"), NT * E + t + 1)
                eng.tensor_tensor_reduce(urow[c], urow[c], pt4[:, :, :].rearrange("p a d -> p (a d)"), 1.0, 0.0, ALU.mult,
                                         ALU.add, act4[:, c:c + 1]).then_inc(s("u_used"), 1)
            eng.wait_ge(s("y_squared"), NT + 1)
            ch.link(eng.tensor_tensor(ss[0:TS, 3:4], ss[0:TS, 1:2], ss[0:TS, 2:3], ALU.add))
            eng.sem_inc(s("y_summed"), 1)
            finish(TS, NT)

        @block.scalar
        def _(eng):
            ch = Chain(eng, s("act_chain"))
            act = eng.activation
            for name, n in (("memrow_ready", 2), ("val_read", 2), ("os_read", 1), ("sc_copied", 1), ("act_read", 4)):
                eng.sem_inc(s(name), n)
            eng.wait_ge(s("ones_ready"), 3)
            for item in range(2):
                eng.wait_ge(s(f"rows_loaded{item}"), 16)
                ch.link(act(hflat[:, 2048:4096], rowbuf[:, item, :], ACT.Square, accum_out=ss[:, item:item + 1]))
                act(ss[:, item:item + 1], ss[:, item:item + 1], ACT.Sqrt, bias=epsT[:, :], scale=1.0 / D).then_inc(s("mem_root"), 1)

            for b0 in (xk0, xv0):
                with eng.Fori(0, KD // 2) as i:
                    for slot in range(2):
                        eng.wait_ge(s("mem_turned"), i * 2 + (b0 + slot + 3))
                        eng.wait_ge(s(f"memrow_stored{slot}"), i * 16 + (b0 // 2 + 1) * 16)
                        eng.copy(rq[:, slot * M:(slot + 1) * M], pt[slot][:, 0:M]).then_inc(s("memrow_ready"), 1)

            def norm_squares(n):
                with eng.Fori(0, KD // 2) as i:
                    for a in range(2):
                        eng.wait_ge(s("sq_used"), i * 2 + (n * KD + a + 1))
                        act(sq[:, a, :], xT[:, i * 2 + a, :], ACT.Square).then_inc(s("sq_ready"), 1)
                eng.wait_ge(s("sq_used"), 2 + (n + 1) * KD)
                act(rstdB[:, :, :], pt4[:, 0:2, 0:HALF], ACT.Sqrt, bias=epsT[:, :], scale=1.0 / D).then_inc(s("norm_root"), 1)

            eng.wait_ge(s("turn_read"), 28)
            norm_squares(0)
            with eng.Fori(0, 4) as i:
                for a in range(2):
                    eng.wait_ge(s("product_read"), i * 2 + (in0 + a + 3))
                    act(mT[:, i * 2 + a, :], mT[:, i * 2 + a, :], ACT.Gelu_apprx_tanh).then_inc(s("u_acted"), 1)

            def value_rows(i, a, first, rows, srows):
                eng.wait_ge(s("val_turned"), i * 2 + (first + a + 3))
                at = bass.ds((i * 2 + a) * P, P)
                eng.copy(rows[:, :, at], pt[a].rearrange("p (r c) -> p r c", r=NT))
                eng.copy(srows[:, at], pt[2 + a][0:TS, 0:P]).then_inc(s("val_read"), 1)

            with eng.Fori(0, 4) as i:
                for a in range(2):
                    eng.wait_ge(s("product_read"), i * 2 + (in0 + 8 + a + 3))
                    act(stg[:, a, :], stg[:, a, :], ACT.Gelu_apprx_tanh).then_inc(s("val_staged"), 1)
                for a in range(2):
                    value_rows(i, a, 0, varow, vas)
            with eng.Fori(0, 4) as i:
                for a in range(2):
                    value_rows(i, a, 8, vrow, vbs)
            with eng.Fori(0, 4) as i:
                for a in range(2):
                    eng.wait_ge(s("product_read"), i * 2 + (in0 + 32 + a + 3))
                    m = mT[:, i * 2 + (AH + a), :]
                    act(m, m, ACT.Silu).then_inc(s("r_acted"), 1)
            eng.wait_ge(s("va_squared"), NT + 1)
            act(vss[:, :, :], vss[:, :, :], ACT.Sqrt, bias=epsT[:, :], scale=1.0 / P).then_inc(s("va_root"), 1)
            eng.wait_ge(s("gate_read"), BH)
            act(gates_tmp, rq[:, 2 * BH * T:3 * BH * T], ACT.Abs).then_inc(s("gate_ln"), 1)
            eng.wait_ge(s("gate_ln"), 1)
            act(gates_tmp, gates_tmp, ACT.Exp, scale=-1.0).then_inc(s("gate_ln"), 1)
            eng.wait_ge(s("gate_ln"), 2)
            act(gates_tmp, gates_tmp, ACT.Ln, bias=1.0).then_inc(s("gate_ln"), 1)

            with eng.Fori(0, BH) as j:
                st = ch.enter(j, 1)
                eng.wait_ge(s("diffs_ready"), j * 6 + 6)
                act(factors, factors, ACT.Exp).then_inc(s("exps_ready"), 1)
                act(qd, G[:, j, 0:TP], ACT.Exp).then_inc(s("exps_ready"), 1)
                act(glast, G[:, j, 0:TP].rearrange("p (r t) -> p r t", r=NT)[:, :, P - 1], ACT.Exp).then_inc(s("exps_ready"), 1)
                eng.wait_ge(s("kd_turned"), j + 1)
                eng.copy(kds, pt[0].rearrange("p (r d) -> p r d", r=NT)).then_inc(s("kds_ready"), 1)
                eng.wait_ge(s("o_done"), j + 1)
                for r in range(NT):
                    ins = act(on[:, r, :], pt[2 + r // 2][:, (r % 2) * BV:(r % 2 + 1) * BV], ACT.Square,
                              accum_out=ss[:, r:r + 1])
                ch.link(ins)
                act(ss[:, 0:NT], ss[:, 0:NT], ACT.Sqrt, bias=epsT[:, :], scale=1.0 / BV).then_inc(s("o_root"), 1)
            ch.leave(st, BH)

            act(ea, G[:, :, TP:T], ACT.Exp).then_inc(s("ks_ready"), 1)
            eng.wait_ge(s("ks_turned"), 1)
            eng.copy(kss, pt[0][0:TS, 0:BH * P]).then_inc(s("ks_ready"), 1)
            with eng.Fori(0, TS) as b:
                eng.wait_ge(s("os_done"), b + 3)
                eng.copy(oS[:, :, :, b], pt[3][:, 0:BH * NV].rearrange("p (h v) -> p h v", h=BH)).then_inc(s("os_read"), 1)
            eng.wait_ge(s("os_read"), TS + 1)
            act(oSq, oS, ACT.Square).then_inc(s("os_squared"), 1)
            eng.wait_ge(s("os_summed"), 1)
            act(roS, pt[0][:, 0:BH * TS].rearrange("p (h b) -> p h b", h=BH), ACT.Sqrt, bias=epsT[:, :], scale=1.0 / BV
                ).then_inc(s("os_root"), 1)

            eng.wait_ge(s("product_read"), 2 + xq0)
            norm_squares(1)

            def p_exp(u):
                a = u % 2
                eng.wait_ge(s("p_max"), u + 1)
                if u >= 2:
                    eng.wait_ge(s("p_turned"), u - 1)
                act(stg[:, a, 0:M], pt[a][:, 0:M], ACT.Exp, bias=ss[:, 6 + a:7 + a], accum_out=ss[:, 8 + a:9 + a]
                    ).then_inc(s("p_exp"), 1)

            def p_rows(u):
                h, r = divmod(u, NT)
                eng.wait_ge(s("p_turned"), u + 1)
                if h >= 2 and r == 0:
                    eng.wait_ge(s("xo_done"), XK * (h - 1))
                eng.copy(pT[h % 2][:, :, r * P:(r + 1) * P], pt[2 + u % 2][:, 0:2 * P].rearrange("p (m t) -> p m t", m=2)
                         ).then_inc(s("pT_ready"), 1)

            def out_rows(h):
                for k in range(XK):
                    n = h * XK + k
                    eng.wait_ge(s("xo_done"), n + 1)
                    eng.copy(hT[:, n, 0:TP], pg[(n % 4) // 2][:, n % 2, :]).then_inc(s("xo_read"), 1)

            for u in range(XH * NT + 1):
                if u < XH * NT:
                    p_exp(u)
                if u >= 1:
                    p_rows(u - 1)
                if u >= 2 and (u - 2) % NT == NT - 1:
                    out_rows((u - 2) // NT)
            out_rows(XH - 1)

            eng.wait_ge(s("qs_turned"), 1)
            eng.copy(srow[0:TS, 0:D].rearrange("p (a d) -> p a d", a=4), pt4[0:TS]).then_inc(s("qs_copied"), 1)
            NS = XH * TS
            eng.wait_ge(s("p_max"), XH * NT + 1)
            act(pS, pt[0][0:NS, 0:M], ACT.Exp, bias=ss[0:NS, 6:7], accum_out=ss[0:NS, 8:9]).then_inc(s("pS_exp"), 1)
            eng.wait_ge(s("pS_turned"), 1)
            eng.copy(pST, pt[1][:, 0:2 * NS]).then_inc(s("pST_ready"), 1)
            eng.wait_ge(s("vcache_used"), 2 * TS)
            for a in range(2):
                ins = eng.copy(srow[0:TS, a * 1024:(a + 1) * 1024].rearrange("p (c d) -> p c d", c=2), pg[a][0:TS])
            ins.then_inc(s("oxs_copied"), 1)
            eng.wait_ge(s("oxs_turned"), 1)
            eng.copy(hT[:, :, TP:T], pt[2][:, 0:KD * TS].rearrange("p (k b) -> p k b", k=KD)).then_inc(s("oxs_read"), 1)

            eng.wait_ge(s("product_read"), 2 + pq0)
            norm_squares(2)
            for n in range(4 * NT + 4):
                rows = P if n // 4 < NT else TS
                eng.wait_ge(s("xrow_turned"), n + 1)
                if n >= 2:
                    eng.wait_ge(s(f"x_stored{n % 2}"), 16 * (n // 2))
                eng.copy(xst[n % 2][0:rows], pt[2 + n % 2][0:rows]).then_inc(s("xrow_staged"), 1)
            for n in range(4):
                eng.wait_ge(s("keys_turned"), n + 1)
                eng.copy(skT[:, 4 * n:4 * n + 4, :], pt[2 + n % 2].rearrange("p (n c) -> p n c", n=4)).then_inc(s("keys_read"), 1)

            def copy_scores(r, h):
                for c in range(2):
                    ins = eng.copy(qs[:, c * P:(c + 1) * P], mflat[:, bass.ds(r * P + h * (2 * T) + c * T, P)])
                ins.then_inc(s("qs_ready"), 1)
                eng.wait_ge(s("sc_done"), r * PH + h + 1)
                eng.wait_ge(s("head_selected"), r * PH + h + 1)
                eng.copy(sc, pt[0][:, 0:2 * P]).then_inc(s("sc_copied"), 1)

            def top_exp(r, h):
                eng.wait_ge(s("top_ready"), r * PH + h + 1)
                act(ex, ts, ACT.Exp, bias=ntop, accum_out=esum).then_inc(s("top_exp"), 1)

            def row_root(r, p):
                eng.wait_ge(s("xrow_loaded"), r * 16 + 16)
                ch.link(act(hrow[p], xrow, ACT.Square, accum_out=ss[:, 0:1]))
                act(ss[:, 0:1], ss[:, 0:1], ACT.Sqrt, bias=epsT[:, :], scale=1.0 / D).then_inc(s("xrow_root"), 1)

            def y_root(n, r, p):
                eng.wait_ge(s("v_used"), r * E + (E + 4) if n == P else NT * E + TS + 4)
                for a in range(2):
                    ins = act(hrow[p][0:n, a * 1024:(a + 1) * 1024].rearrange("p (c d) -> p c d", c=2), pg[a][0:n], ACT.Square,
                              accum_out=ss[0:n, 1 + a:2 + a])
                ins.then_inc(s("y_squared"), 1)
                eng.wait_ge(s("y_summed"), r + 1)
                act(ss[0:n, 3:4], ss[0:n, 3:4], ACT.Sqrt, bias=epsT[0:n], scale=1.0 / D).then_inc(s("y_root"), 1)

            with eng.Fori(0, PH) as h:
                eng.wait_ge(s("product_read"), h * 2 + (pq0 + 4))
                copy_scores(0, h)
                top_exp(0, h)
            row_root(0, 0)

            def tile(r, p):
                with eng.Fori(0, PH) as h:
                    sh = ch.enter(h, 2 * TOPK)
                    copy_scores(r + 1, h)
                    for c16 in range(TOPK):
                        c, n = c16 % 4, r * E + h * TOPK
                        eng.wait_ge(s("u_used"), n + (c16 + 5))
                        act(g4[:, c:c + 1], act4[:, c:c + 1], ACT.Gelu_apprx_tanh).then_inc(s("act_read"), 1)
                        eng.wait_ge(s("act_read"), n + (c16 + 5))
                        ch.link(act(w4[:, c:c + 1], gate_all[p][:, bass.ds(h * TOPK + c16, 1)], ACT.Copy,
                                    scale=g4[:, c:c + 1]))
                        eng.wait_ge(s("v_used"), n + (c16 + 1))
                        ch.link(act(diag[c], ident[:, :], ACT.Copy, scale=w4[:, c:c + 1]))
                        eng.sem_inc(s("diag_ready"), 1)
                    top_exp(r + 1, h)
                ch.leave(sh, PH)
                row_root(r + 1, 1 - p)
                y_root(P, r, p)

            with eng.Fori(0, NT // 2) as i:
                sr = ch.enter(i, 2 * (1 + 2 * E))
                for p in range(2):
                    tile(i * 2 + p, p)
            ch.leave(sr, NT // 2)
            eng.wait_ge(s("picks_ready"), 1)
            for t in range(TS):
                c = t % 4
                eng.wait_ge(s("u_used"), NT * E + t + 5)
                act(g4[:, c:c + 1], act4[:, c:c + 1], ACT.Gelu_apprx_tanh).then_inc(s("act_read"), 1)
                eng.wait_ge(s("act_read"), NT * E + t + 5)
                ch.link(act(w4[:, c:c + 1], gateS[:, t:t + 1], ACT.Copy, scale=g4[:, c:c + 1]))
                eng.wait_ge(s("v_used"), NT * E + t + 1)
                act(wmask[c], e8[:, t, :], ACT.Copy, scale=w4[:, c:c + 1]).then_inc(s("diag_ready"), 1)
            y_root(TS, NT, 0)


_INS = ["x_prompt", "x_sample", "mem_prompt", "cache_mem_k", "cache_mem_v", "state_gla", "g_mix", "w_in", "w_alpha",
        "b_alpha", "w_s", "b_s", "g_sgu", "g_gla", "w_out", "g_mem", "w_xk", "w_xv", "g_xq", "w_xq", "w_xo", "g_ffn",
        "w_pq", "sub_keys", "u_emb", "v_emb", "g_final"]
_OUTS = [(1, 512, 2048), (8, 1, 2048), (1, 1, 256, 4, 512), (1, 1, 256, 4, 512), (1, 1, 4, 128, 256),
         (1, 8, 4, 128, 256), (1, 1, 128, 8, 128), (1, 8, 1, 8, 128)]


def kernel(**inputs):
    import concourse.bacc as _bacc
    from concourse.bass_utils import run_bass_kernel_spmd as _run

    nc = _bacc.Bacc("TRN2", target_bir_lowering=False, num_devices=1)
    arrays, args = {}, []
    for name in _INS:
        a = np.ascontiguousarray(inputs[name])
        arrays[f"in_{name}_dram"] = a
        args.append(nc.dram_tensor(f"in_{name}_dram", a.shape, mybir.dt.from_np(a.dtype), kind="ExternalInput").ap())
    for i, shape in enumerate(_OUTS):
        args.append(nc.dram_tensor(f"out_{i}_dram", shape, F32, kind="ExternalOutput").ap())
    program(nc, *args)
    r = _run(nc, [arrays], core_ids=[0])
    return tuple(r.results[0][f"out_{i}_dram"] for i in range(len(_OUTS)))
```

```python
from contextlib import ExitStack

import numpy as np

import concourse.bass as bass
from concourse import mybir

F32 = mybir.dt.float32
U32 = mybir.dt.uint32
ALU = mybir.AluOpType
ACT = mybir.ActivationFunctionType
AX = mybir.AxisListType.X

P = 128
EPS = 1e-6
TAU = 16.0
SUB = 32
REF = 15
NEG = -3.0e38


class Chain:

    def __init__(self, eng, sem):
        self.eng, self.sem, self.base, self.local = eng, sem, 0, 0

    def link(self, ins):
        ins.then_inc(self.sem, 1)
        self.local += 1
        self.eng.wait_ge(self.sem, self.base + self.local)

    def enter(self, i, per):
        state = (self.base, self.local, per)
        self.base, self.local = i * per + (self.base + self.local), 0
        return state

    def leave(self, state, count):
        assert self.local == state[2], (self.local, state[2])
        self.base, self.local = state[0], state[1] + count * state[2]


def program(nc, x_prompt, x_sample, mem_prompt, cache_mem_k, cache_mem_v, state_gla, g_mix, w_in, w_alpha,
            b_alpha, w_s, b_s, g_sgu, g_gla, w_out, g_mem, w_xk, w_xv, g_xq, w_xq, w_xo, g_ffn, w_pq,
            sub_keys, u_emb, v_emb, g_final,
            y_prompt, y_sample, mem_k_out, mem_v_out, state_p_out, state_s_out, chunk_p_out, chunk_s_out):
    D = x_prompt.shape[2]
    TP = x_prompt.shape[1]
    TS = x_sample.shape[0]
    T = TP + TS
    HALF = T // 2
    KD = D // P
    NT = TP // P
    M = mem_prompt.shape[1]
    AH = w_s.shape[1]
    BH = state_gla.shape[2]
    BV = state_gla.shape[4]
    NV = BV // P
    XH = cache_mem_k.shape[3]
    XD = cache_mem_k.shape[4]
    XK = XD // P
    PH = sub_keys.shape[1]
    TOPK = 16
    E = PH * TOPK
    RANK = w_alpha.shape[1]
    NSUB = P // SUB
    EH, EJ = PH - 1, 8
    LATE = EH * EJ - EJ
    KF = sum(NT * SUB * (i + 1) for i in range(NSUB))
    assert NT == 4 and KD == 16 and TS == 8 and E == P and T % 2 == 0

    with ExitStack() as ctx:
        def sb(name, shape, dt=F32):
            return ctx.enter_context(nc.sbuf_tensor(name, shape, dt))

        def sem(name):
            return ctx.enter_context(nc.semaphore(name))

        xh = sb("xh", [P, 2, KD, T])
        xT, hT = xh[:, 0], xh[:, 1]
        mflat = sb("mT", [P, KD * T + (NT + 1) * P - T])
        mT = mflat[:, 0:KD * T].rearrange("p (k t) -> p k t", k=KD)
        m2 = mT[:, :, :].rearrange("p k (a t) -> p k a t", a=2)
        x2 = xh[:, 0].rearrange("p k (a t) -> p k a t", a=2)
        hflat = xh[:, 1].rearrange("p k t -> p (k t)")
        ra = sb("ra", [P, 8192])
        rowbuf = ra[:, :].rearrange("p (s d) -> p s d", s=4)
        varow = ra[:, 0:4096].rearrange("p (r c) -> p r c", r=NT)
        vrow = ra[:, 4096:8192].rearrange("p (r c) -> p r c", r=NT)
        kTm = ra[:, 0:4096].rearrange("p (k m) -> p k m", k=KD)
        vmr = ra[:, 4096:8192].rearrange("p (a d) -> p a d", a=2)
        srow = sb("srow", [TS, 2048 + 512])
        vas, vbs, kss = srow[:, 0:1024], srow[:, 1024:2048], srow[:, 2048:2560]
        rq = sb("rq", [P, 3 * BH * T])
        qT = rq[:, 0:BH * T].rearrange("p (h t) -> p h t", h=BH)
        kT = rq[:, BH * T:2 * BH * T].rearrange("p (h t) -> p h t", h=BH)
        G = rq[:, 2 * BH * T:3 * BH * T].rearrange("p (h t) -> p h t", h=BH)
        memT = mT[:, :, 0:M]
        wring = sb("wring", [P, 2, KD, P])
        stg = sb("stg", [P, 2, T])
        rstdB = sb("rstdB", [P, 2, HALF])
        sq = sb("sq", [P, 2, T])
        sqsum = stg[:, 0, :]
        ident = sb("ident", [P, P])
        ones = sb("ones", [P, P])
        tri = sb("tri", [P, P])
        wsT = sb("wsT", [P, AH, P])
        bsB = sb("bsB", [P, AH, P])
        gsguB = sb("gsguB", [P, AH * P])
        NG = 4 * KD + BH + BH * NV
        gcol = sb("gcol", [P, NG])
        col_mix, col_mem, col_xq, col_ffn = (gcol[:, a * KD:(a + 1) * KD] for a in range(4))
        col_ba = gcol[:, 4 * KD:4 * KD + BH]
        col_gla = gcol[:, 4 * KD + BH:NG]
        w00B = sb("w00B", [P, AH])
        e8 = sb("e8", [P, TS, TS])
        epsT = sb("epsT", [P, 1])
        ss = sb("ss", [P, 16])
        rs = sb("rs", [P, 16])
        wg = sb("wg", [P, KD, RANK])
        primer = sb("primer", [1, 5 * 16])
        vss = sb("vss", [P, NT + 1, AH])
        zgT = sq[0:RANK, 0, :]
        walpha = sq[0:RANK, 1, 0:BH * P]

        gates_tmp = [sq[:, :, :], stg[:, :, :]]
        sgu_tmp = rq[:, 2 * BH * T:2 * BH * T + AH * P]
        KF0 = BH * T
        kf = hflat[:, KF0:KF0 + KF]
        qf = hflat[:, KF0 + KF:KF0 + KF + TP]
        kd = hflat[:, KF0 + KF + TP:KF0 + KF + 2 * TP]
        qd = hflat[:, KF0 + KF + 2 * TP:KF0 + KF + 3 * TP]
        factors = hflat[:, KF0:KF0 + KF + 2 * TP]
        smix = sgu_tmp[0:TS]
        stin = [(ra if b < TS // 2 else hflat)[:, b % (TS // 2) * BH * BV:(b % (TS // 2) + 1) * BH * BV].rearrange("p (h v) -> p h v", h=BH)
                for b in range(TS)]
        kf_i, at = [], 0
        for i in range(NSUB):
            kf_i.append(kf[:, at:at + NT * SUB * (i + 1)].rearrange("p (r c) -> p r c", r=NT))
            at += NT * SUB * (i + 1)
        SC0 = KF0 + KF + 3 * TP
        scT = hflat[:, SC0:SC0 + TP].rearrange("p (r t) -> p r t", r=NT)
        kds = hflat[:, SC0 + TP:SC0 + 2 * TP].rearrange("p (r d) -> p r d", r=NT)
        GS0 = SC0 + 2 * TP
        gstate = hflat[:, GS0:GS0 + BV]
        on = hflat[:, GS0 + BV:GS0 + BV + NT * BV].rearrange("p (r v) -> p r v", r=NT)
        SM0 = GS0 + BV + NT * BV
        glast = hflat[:, SM0:SM0 + NT]
        gated = rq[:, 2 * BH * T + AH * P:2 * BH * T + AH * P + TP].rearrange("p (r t) -> p r t", r=NT)
        SN0 = SM0 + 4
        oS = hflat[:, SN0:SN0 + 64].rearrange("p (h v b) -> p h v b", h=BH, v=NV)
        oSq = hflat[:, SN0 + 64:SN0 + 128].rearrange("p (h v b) -> p h v b", h=BH, v=NV)
        ea = hflat[:, SN0 + 128:SN0 + 160].rearrange("p (h b) -> p h b", h=BH)
        roS = hflat[:, SN0 + 160:SN0 + 192].rearrange("p (h b) -> p h b", h=BH)
        km = [hflat[0:TS, GS0 + BV + a * BH * P:GS0 + BV + (a + 1) * BH * P] for a in range(2)]
        assert SN0 + 192 <= KD * T
        pT = [rq[:, 4096 + a * 1024:4096 + (a + 1) * 1024].rearrange("p (m t) -> p m t", m=2) for a in range(2)]
        k_ring = [rq[:, a * D:(a + 1) * D] for a in range(2)]
        v_ring = [ra[:, a * D:(a + 1) * D] for a in range(4)]
        wsf = wsT[:, :, :].rearrange("p h c -> p (h c)")
        sS = wsf[:, 0:64].rearrange("p (m h b) -> p m h b", m=2, h=XH)
        pS = wsf[0:XH * TS, 128:128 + M]
        pST = wsf[:, 384:448]
        pM = wsf[:, 512:1024].rearrange("p (m h b c) -> p m h b c", m=2, h=XH, b=TS)
        xhf = xh[:, :, :, :].rearrange("p a k t -> p (a k t)")
        urow = [xhf[:, c * D:(c + 1) * D] for c in range(4)]
        vexp = [xhf[:, (4 + c) * D:(5 + c) * D] for c in range(4)]
        skT = ra[:, 0:D].rearrange("p (n c) -> p n c", n=2 * PH)
        xrow, ystage = ra[:, D:2 * D], ra[:, 2 * D:3 * D]
        hrow = [ra[:, 3 * D:4 * D], rq[:, 2 * D:3 * D]]
        skr = ra[:, 3 * D:4 * D].rearrange("p (n c) -> p n c", n=2 * PH)
        xst = [ra[:, D + a * 512:D + (a + 1) * 512] for a in range(4)]
        gffnB, gfinB = rq[:, 0:D], rq[:, D:2 * D]
        pools = [[gsguB[:, :], AH * P], [bsB[:, :, :].rearrange("p h c -> p (h c)"), AH * P], [wsf, AH * P],
                 [stg[:, :, :].rearrange("p a t -> p (a t)"), 2 * T]]

        def work(n, dt=F32):
            pool = next(p for p in pools if p[1] >= n)
            pool[1] -= n
            ap = pool[0][:, pool[1]:pool[1] + n]
            return ap if dt == F32 else ap.bitcast(dt)
        diag = [work(P) for _ in range(4)]
        idx_all, gate_all = [work(E, U32) for _ in range(2)], [work(E) for _ in range(2)]
        idx8, idxS = work(8, U32), work(TS, U32)
        idxf, gateS = work(E), work(TS)
        sc, sc2, cand, cand2 = work(2 * P), work(2 * P), work(2 * P), work(2 * P)
        onehot = work(2 * P)
        qs = work(2 * P)
        sv, si, sif = work(32), work(32, U32), work(32)
        ts, pos, posi, posj = work(TOPK), work(TOPK, U32), work(TOPK, U32), work(TOPK, U32)
        pif, pjf, pa, pb = work(TOPK), work(TOPK), work(TOPK), work(TOPK)
        ex, jota, jint = work(TOPK), work(TOPK), work(TOPK, mybir.dt.int32)
        act4, g4, w4 = work(4), work(4), work(4)
        early_w = work(EH * EJ)
        ntop, esum, erec = work(1), work(1), work(1)
        wmask = [work(TS) for _ in range(4)]

        pg = [ctx.enter_context(nc.psum_tensor(f"pg{i}", [P, 2, 512], F32)) for i in range(2)]
        pt4 = ctx.enter_context(nc.psum_tensor("pt4", [P, 4, 512], F32))
        pt = [pt4[:, i] for i in range(4)]

        def query_bank(b, h):
            return pt[h] if b % 2 == 0 else pg[h // 2][:, h % 2, :]

        kT_scr = nc.dram_tensor("kT_scratch", [KD, P, M], F32, kind="Internal").ap()
        x_scr = nc.dram_tensor("x_scratch", [T, D], F32, kind="Internal").ap()

        S = {}

        def s(name):
            if name not in S:
                S[name] = sem(name)
            return S[name]

        block = ctx.enter_context(nc.Block())

        xk0, xv0, in0, out0, xq0, xo0, pq0 = 0, 16, 32, 72, 88, 104, 120
        stages = [(w_xk, xk0, 16), (w_xv, xv0, 16), (w_in, in0, 40), (w_out, out0, 16), (w_xq, xq0, 16),
                  (w_xo, xo0, 16), (w_pq, pq0, 16)]

        def pe_product(eng, i, slot, b0, moving, width, operand=None):
            eng.wait_ge(s(f"w_loaded{slot}"), i * 16 + (b0 // 2 + 1) * 16)
            eng.wait_ge(s("product_read"), i * 2 + (b0 + slot + 1))
            for k in range(KD):
                if operand is not None:
                    eng.wait_ge(s("ht_ready"), operand + k + 1)
                if width == T:
                    for a in range(2):
                        mm = eng.matmul(pg[slot][:, a, 0:HALF], wring[:, slot, k], moving[:, k, a * HALF:(a + 1) * HALF],
                                        start=(k == 0), stop=(k == KD - 1))
                else:
                    mm = eng.matmul(pg[slot][:, 0, 0:width], wring[:, slot, k], moving[:, k, 0:width],
                                    start=(k == 0), stop=(k == KD - 1))
            mm.then_inc(s("product_done"), 1)

        def await_product(eng, i, slot, b0):
            eng.wait_ge(s("product_done"), i * 2 + (b0 + slot + 1))

        def u_index(r, h, j, late):
            return h * (TOPK - EJ) + (LATE + j) if late else r * E + h * TOPK + j

        def u_arrived(r, h, j, late):
            per = (TOPK - EJ if late else TOPK) // 4 * 16
            return h * per + (((LATE if late else r * E) + j) // 4 + 1) * 16

        item_rows = [P, P, P, P, P, P, TS]

        @block.sync
        def _(eng):
            def load_rows(item):
                if item >= 4:
                    eng.wait_ge(s("turned"), 3 + 4 * (item - 3))
                src = (mem_prompt[0, item * P:(item + 1) * P, :] if item < 2 else
                       x_prompt[0, (item - 2) * P:(item - 1) * P, :] if item < 6 else x_sample[:, 0, :])
                eng.dma_start(rowbuf[0:item_rows[item], item % 4, :], src).then_inc(s(f"rows_loaded{item % 4}"), 16)

            def load_weights(w, b0, count, first):
                wv = w[0, :, 0:count * P].rearrange("(k p) (n c) -> n p k c", p=P, c=P)
                start = 0
                if first:
                    start = 1
                    for slot in range(2):
                        eng.dma_start(wring[:, slot], wv[slot]).then_inc(s(f"w_loaded{slot}"), 16)
                    for item in range(4, 7):
                        load_rows(item)
                with eng.Fori(start, count // 2) as i:
                    for slot in range(2):
                        eng.wait_ge(s("product_done"), i * 2 + (b0 + slot - 1))
                        eng.dma_start(wring[:, slot], wv[i * 2 + slot]).then_inc(s(f"w_loaded{slot}"), 16)

            for a, g in enumerate((g_mix, g_mem, g_xq, g_ffn)):
                eng.dma_start(stg[a * KD:(a + 1) * KD, 0, 0:P], g[0].rearrange("(k p) -> k p", p=P)).then_inc(s("gains_loaded"), 16)
            eng.dma_start(stg[4 * KD:4 * KD + BH, 0, 0:P], b_alpha[0].rearrange("(k p) -> k p", p=P)).then_inc(s("gains_loaded"), 16)
            eng.dma_start(stg[4 * KD + BH:NG, 0, 0:P], g_gla[0].rearrange("h (v p) -> (h v) p", p=P)).then_inc(s("gains_loaded"), 16)
            for item in range(4):
                load_rows(item)
            first = True
            for n, (w, b0, count) in enumerate(stages):
                load_weights(w, b0, count, first)
                first = False

            eng.sem_inc(s("y_stored"), 16)
            def load_xrow(r):
                n = P if r < NT else TS
                eng.dma_start(xrow[0:n], x_scr[r * P:r * P + n, :]).then_inc(s("xrow_loaded"), 16)

            for r in range(NT + 1):
                if r < NT:
                    eng.wait_ge(s("acc_started"), 4 * (r + 1))
                    eng.wait_ge(s("hrow_ready"), r + 1)
                    load_xrow(r + 1)
                eng.wait_ge(s("y_ready"), r + 2)
                dst = y_prompt[0, r * P:(r + 1) * P, :] if r < NT else y_sample[:, 0, :]
                eng.dma_start(dst, ystage[0:(P if r < NT else TS)]).then_inc(s("y_stored"), 16)
            eng.wait_ge(s("y_stored"), 16 * (NT + 2))

        @block.gpsimd
        def _(eng):
            def passed():
                eng.sem_inc(s("pool_passed"), 1)

            eng.dma_start(hflat[:, 0:AH * P].rearrange("p (h c) -> p h c", h=AH),
                          w_s[0].rearrange("h t s -> t h s")).then_inc(s("ws_loaded"), 16)
            eng.memset(ident[:, :], 0.0).then_inc(s("pool_set"), 1)
            eng.memset(tri[:, :], 1.0).then_inc(s("pool_set"), 1)
            eng.memset(e8[:, :, :], 0.0).then_inc(s("pool_set"), 1)
            eng.memset(mflat[:, KD * T:], 0.0)
            eng.wait_ge(s("pool_set"), 3)
            eng.affine_select(out=ident[:, :], in_=ident[:, :], compare_op=ALU.not_equal, fill=1.0, base=0,
                              pattern=[[-1, P]], channel_multiplier=1).then_inc(s("masks_ready"), 1)
            eng.affine_select(out=tri[:, :], in_=tri[:, :], compare_op=ALU.is_ge, fill=0.0, base=0,
                              pattern=[[1, P]], channel_multiplier=-1).then_inc(s("masks_ready"), 1)
            eng.affine_select(out=e8[:, :, :], in_=e8[:, :, :], compare_op=ALU.not_equal, fill=1.0, base=0,
                              pattern=[[1, TS], [-1, TS]], channel_multiplier=0).then_inc(s("masks_ready"), 1)
            eng.wait_ge(s("ws_loaded"), 16)
            wsrow = hflat[:, 0:AH * P].rearrange("p (h c) -> p h c", h=AH)
            eng.affine_select(out=wsrow, in_=wsrow, compare_op=ALU.is_ge, fill=0.0, base=0,
                              pattern=[[0, AH], [-1, P]], channel_multiplier=1).then_inc(s("ws_masked"), 1)
            eng.dma_start(bsB[:, :, :].rearrange("p h c -> p (h c)"),
                          b_s[0].rearrange("h c -> (h c)").partition_broadcast(P)).then_inc(s("consts_loaded"), 16)
            eng.dma_start(gsguB[:, :], g_sgu[0].rearrange("h c -> (h c)").partition_broadcast(P)).then_inc(s("consts_loaded"), 16)
            eng.dma_start(w00B[0:TS, :], w_s[0, :, 0, 0:1].rearrange("h c -> (h c)").partition_broadcast(TS),
                          allow_slow_non_contiguous=True).then_inc(s("consts_loaded"), 16)
            eng.dma_start(wg[:, :, :], w_in[0, :, 40 * P:40 * P + RANK].rearrange("(k p) c -> p k c", p=P)).then_inc(s("wg_loaded"), 16)
            for n, name in enumerate(("kT_stored0", "kT_stored1", "memrow_stored0", "memrow_stored1", "state_stored")):
                eng.dma_start(primer[:, n * 16:(n + 1) * 16], g_final[0:16].partition_broadcast(1)).then_inc(s(name), 16)

            for kv, dst in enumerate((mem_k_out, mem_v_out)):
                rows = dst[0, 0].rearrange("(a m) h d -> m a (h d)", a=2).rearrange("m a (n c) -> n m a c", c=P)
                with eng.Fori(0, KD // 2) as i:
                    for slot in range(2):
                        if kv == 0:
                            eng.wait_ge(s("product_read"), i * 2 + (xk0 + slot + 3))
                            passed()
                            eng.dma_start(kT_scr[i * 2 + slot], stg[:, slot, 0:M]).then_inc(s(f"kT_stored{slot}"), 16)
                        eng.wait_ge(s("memrow_ready"), i * 2 + (kv * KD + slot + 3))
                        passed()
                        eng.dma_start(rows[i * 2 + slot], rq[:, slot * M:(slot + 1) * M].rearrange("p (a c) -> p a c", a=2)
                                      ).then_inc(s(f"memrow_stored{slot}"), 16)

            eng.wait_ge(s("sq_used"), 2 + KD)
            eng.dma_start(walpha, w_alpha[0]).then_inc(s("walpha_loaded"), 16)
            eng.wait_ge(s("va_normed"), NT + 1)
            eng.dma_start(chunk_p_out[0, 0].rearrange("t h c -> t (h c)"), varow[:, NT - 1, :]).then_inc(s("chunk_stored"), 16)
            eng.dma_start(chunk_s_out[0, :, 0].rearrange("t h c -> t (h c)"), vas).then_inc(s("chunk_stored"), 16)

            eng.wait_ge(s("chunk_stored"), 32)
            eng.wait_ge(s("sgu_done"), AH)

            def load_states(half):
                for b in range(half * TS // 2, (half + 1) * TS // 2):
                    eng.dma_start(stin[b], state_gla[0][b].rearrange("h d v -> d h v")).then_inc(s(f"sstate_loaded{half}"), 16)
            load_states(0)
            with eng.Fori(0, BH) as j:
                eng.wait_ge(s("state_ready"), j * NT + NT)
                passed()
                eng.dma_start(state_p_out[0, 0][j], hflat[:, GS0:GS0 + BV]).then_inc(s("state_stored"), 16)
            eng.wait_ge(s("head_out"), 2 + 2 * BH)
            load_states(1)
            for b in range(TS):
                eng.wait_ge(s("sstate_read"), b + 1)
                eng.dma_start(state_s_out[0][b].rearrange("h d v -> d h v"), stin[b]).then_inc(s("sstate_stored"), 16)

            eng.wait_ge(s("gla_sample_done"), 1)
            for slot in range(2):
                eng.wait_ge(s(f"kT_stored{slot}"), 16 * (KD // 2 + 1))
                eng.wait_ge(s(f"memrow_stored{slot}"), 16 * (KD + 1))
            eng.wait_ge(s("sstate_stored"), 16 * TS)
            eng.dma_start(kTm, kT_scr.rearrange("k p m -> p k m")).then_inc(s("attn_loaded"), 16)
            eng.dma_start(vmr, mem_v_out[0, 0].rearrange("(a m) h d -> m a (h d)", a=2)).then_inc(s("attn_loaded"), 16)
            cv = cache_mem_k[0].rearrange("b (a m) h d -> b a m (h d)", a=2)
            with eng.Fori(0, TS) as b:
                for a in range(2):
                    eng.wait_ge(s(f"cache_used{a}"), b + 1)
                    passed()
                    eng.dma_start(k_ring[a], cv[b, a]).then_inc(s(f"cache_loaded{a}"), 16)
            cv = cache_mem_v[0].rearrange("b (a m) h d -> b a m (h d)", a=2)
            eng.wait_ge(s("xo_done"), KD)
            for b in range(TS):
                for a in range(2):
                    n = b * 2 + a
                    if n >= 4:
                        eng.wait_ge(s("vcache_used"), n - 3)
                    eng.dma_start(v_ring[n % 4], cv[b, a]).then_inc(s(f"vcache_loaded{n % 4}"), 16)

            eng.wait_ge(s("oxs_read"), 1)
            eng.dma_start(gffnB, g_ffn[0].partition_broadcast(P)).then_inc(s("peer_consts"), 16)
            eng.dma_start(gfinB, g_final.partition_broadcast(P)).then_inc(s("peer_consts"), 16)
            for h in range(0, 16, 4):
                eng.dma_start(skr[:, h:h + 4, :], sub_keys[0].rearrange("h c n d -> n (h c) d")[:, h:h + 4, :]).then_inc(s("keys_loaded"), 16)
            eng.iota(jint, pattern=[[1, TOPK]], base=0, channel_multiplier=0
                     ).then_inc(s("iota_made"), 1)
            def copy_picks(p, h, j0, count):
                eng.tensor_copy(idx8[:, j0 % 8:j0 % 8 + 4], idx_all[p][:, bass.ds(h * TOPK + j0, 4)]).then_inc(s("idx_copied"), 1)
                eng.wait_ge(s("idx_copied"), count)

            def gather(rows, name, table, slot, used, n):
                eng.wait_ge(s(used), n + 1)
                passed()
                eng.indirect_dma_start(rows[slot % 4], None, table[0], bass.IndirectOffsetOnAxis(ap=idx8[:, slot % 8:slot % 8 + 1], axis=0)
                                       ).then_inc(s(f"{name}{slot % 4}"), 16)

            eng.wait_ge(s("ht_ready"), 3 * KD)
            eng.wait_ge(s("norm_root"), 3)
            eng.wait_ge(s("xrow_staged"), 4 * NT + 4)
            with eng.Fori(0, EH) as h:
                eng.wait_ge(s("head_selected"), h + 2)
                for j0 in range(0, EJ, 4):
                    eng.wait_ge(s("u_used"), h * EJ + (j0 + 1))
                    copy_picks(0, h, j0, h * (EJ // 4) + (j0 // 4 + 1))
                    for j in range(j0, j0 + 4):
                        gather(urow, "u_loaded", u_emb, j, "u_used", h * EJ + j)

            def gather_head(r, p, h, late):
                for j0 in range(0, TOPK, 4):
                    v_only = late and j0 < EJ
                    eng.wait_ge(s("v_used"), r * E + h * TOPK + (j0 + 1))
                    eng.wait_ge(s("u_used"), h * EJ + (EH * EJ + j0) if v_only else u_index(r, h, j0, late) + 1)
                    copy_picks(p, h, j0, r * (E // 4) + h * (TOPK // 4) + (EH * EJ // 4 + j0 // 4 + 1))
                    for j in range(j0, j0 + 4):
                        if not v_only:
                            gather(urow, "u_loaded", u_emb, j, "u_used", u_index(r, h, j, late))
                        gather(vexp, "v_loaded", v_emb, j, "v_used", r * E + h * TOPK + j)

            eng.wait_ge(s("product_read"), 2 + pq0 + 16)
            for r in range(NT):
                if r:
                    eng.wait_ge(s("head_selected"), r * PH + (PH + 1))
                with eng.Fori(0, PH if r else EH) as h:
                    gather_head(r, r % 2, h, r == 0)
                if r == 0:
                    eng.wait_ge(s("head_selected"), PH + 1)
                    gather_head(0, 0, PH - 1, False)
            eng.wait_ge(s("picks_ready"), 1)
            for t in range(TS):
                c = t % 4
                eng.wait_ge(s("u_used"), NT * E + t + 1)
                eng.indirect_dma_start(urow[c], None, u_emb[0], bass.IndirectOffsetOnAxis(ap=idxS[:, t:t + 1], axis=0)
                                       ).then_inc(s(f"u_loaded{c}"), 16)
                eng.wait_ge(s("v_used"), NT * E + t + 1)
                eng.indirect_dma_start(vexp[c], None, v_emb[0], bass.IndirectOffsetOnAxis(ap=idxS[:, t:t + 1], axis=0)
                                       ).then_inc(s(f"v_loaded{c}"), 16)
            eng.wait_ge(s("state_stored"), 16 * (BH + 1))
            eng.wait_ge(s("sstate_stored"), 16 * TS)

        @block.tensor
        def _(eng):
            def turn(out, src, n):
                return eng.transpose(out, src, ident[0:n, 0:n])

            def norm_sum(n):
                eng.wait_ge(s("sq_added"), n + 1)
                for c in range(2):
                    mm = eng.matmul(pt[c][:, 0:HALF], ones[:, :], sqsum[:, c * HALF:(c + 1) * HALF], start=True, stop=True)
                mm.then_inc(s("norm_summed"), 1)

            def gate_columns():
                eng.wait_ge(s("wg_loaded"), 16)
                for c in range(2):
                    for k in range(KD):
                        mm = eng.matmul(pt[2 + c][0:RANK, 0:HALF], wg[:, k], hT[:, k, c * HALF:(c + 1) * HALF],
                                        start=(k == 0), stop=(k == KD - 1))
                mm.then_inc(s("zg_done"), 1)

            def product_loop(b0, count, moving, width, after=None, norm=None):
                if norm is not None:
                    for slot in range(2):
                        pe_product(eng, 0, slot, b0, moving, width, norm * KD if slot == 0 else None)
                    norm_sum(norm)
                    if norm == 0:
                        gate_columns()
                with eng.Fori(0 if norm is None else 1, count // 2) as i:
                    for slot in range(2):
                        pe_product(eng, i, slot, b0, moving, width)
                    if after:
                        after(i)

            eng.sem_inc(s("mem_turned"), 2)
            eng.sem_inc(s("val_turned"), 2)
            eng.sem_inc(s("v_used"), 4)

            unit = 0

            def turn_unit(pieces):
                nonlocal unit
                if unit >= 4:
                    eng.wait_ge(s("turn_read"), unit - 3)
                for dst, src, n in pieces:
                    mm = turn(dst, src, n)
                mm.then_inc(s("turned"), 1)
                unit += 1

            eng.wait_ge(s("masks_ready"), 1)
            eng.wait_ge(s("gains_loaded"), 96)
            turn_unit([(pt[0][:, 0:NG], stg[0:NG, 0, 0:P], NG)])
            eng.wait_ge(s("ws_masked"), 1)
            for u in range(2):
                turn_unit([(pt[unit % 4][:, a * P:(a + 1) * P], hflat[:, (4 * u + a) * P:(4 * u + a + 1) * P], P)
                           for a in range(4)])
            for item in range(7):
                if item < 2:
                    eng.wait_ge(s("mem_scaled"), item + 1)
                else:
                    eng.wait_ge(s(f"rows_loaded{item % 4}"), 16 * (item // 4 + 1))
                if item < 6:
                    for g in range(4):
                        turn_unit([(pt[unit % 4][:, a * P:(a + 1) * P],
                                    rowbuf[:, item % 4, (4 * g + a) * P:(4 * g + a + 1) * P], P) for a in range(4)])
                else:
                    turn_unit([(pt[unit % 4][:, k * TS:(k + 1) * TS], rowbuf[0:TS, item % 4, k * P:(k + 1) * P], TS)
                               for k in range(KD)])

            eng.wait_ge(s("turn_read"), unit)
            for b0 in (xk0, xv0):
                def mem_rows(i):
                    for slot in range(2):
                        eng.wait_ge(s("product_read"), i * 2 + (b0 + slot + 3))
                        eng.wait_ge(s("memrow_ready"), i * 2 + (b0 + slot + 1))
                        for a in range(2):
                            mm = turn(pt[slot][:, a * P:(a + 1) * P], stg[:, slot, a * P:(a + 1) * P], P)
                        mm.then_inc(s("mem_turned"), 1)
                product_loop(b0, 16, memT, M, mem_rows)

            eng.wait_ge(s("memrow_ready"), 2 + 2 * KD)
            product_loop(in0, 8, hT, T, norm=0)
            eng.wait_ge(s("zg_read"), 1)

            def value_rows(first):
                def after(i):
                    for slot in range(2):
                        if first == 0:
                            eng.wait_ge(s("val_staged"), i * 2 + (slot + 1))
                        else:
                            eng.wait_ge(s("product_read"), i * 2 + (in0 + 24 + slot + 3))
                        eng.wait_ge(s("val_read"), i * 2 + (first + slot + 1))
                        for r in range(NT):
                            turn(pt[slot][:, r * P:(r + 1) * P], stg[:, slot, r * P:(r + 1) * P], P)
                        turn(pt[2 + slot][0:TS, 0:P], stg[:, slot, TP:T], P).then_inc(s("val_turned"), 1)
                return after
            eng.wait_ge(s("norm_root"), 1)
            product_loop(in0 + 8, 8, hT, T, value_rows(0))
            product_loop(in0 + 16, 8, hT, T)
            product_loop(in0 + 24, 8, hT, T, value_rows(8))
            for h in range(AH):
                if h < NT:
                    eng.wait_ge(s("va_normed"), NT + 1)
                    eng.wait_ge(s("val_read"), 2 + 16)
                else:
                    eng.wait_ge(s("sgu_read"), h - 3)
                for r in range(NT):
                    mm = eng.matmul(pt[h % 4][:, r * P:(r + 1) * P], varow[:, r, h * P:(h + 1) * P], wsT[:, h],
                                    start=True, stop=True)
                mm.then_inc(s("sgu_done"), 1)
            eng.wait_ge(s("sgu_read"), AH)
            eng.wait_ge(s("sgu_sample"), 1)
            for h in range(AH):
                mm = turn(pt[0][:, h * TS:(h + 1) * TS], smix[:, h * P:(h + 1) * P], TS)
            mm.then_inc(s("sgu_done"), 1)

            eng.wait_ge(s("sgu_read"), AH + 1)
            eng.wait_ge(s("walpha_loaded"), 16)
            for j in range(BH):
                eng.wait_ge(s("product_read"), 2 + in0 + 32)
                if j >= 2:
                    eng.wait_ge(s("gate_read"), j - 1)
                for c in range(2):
                    mm = eng.matmul(pg[j % 2][:, c, 0:HALF], walpha[:, j * P:(j + 1) * P],
                                    zgT[:, c * HALF:(c + 1) * HALF], start=True, stop=True)
                mm.then_inc(s("gate_done"), 1)

            eng.wait_ge(s("gate_read"), BH)
            product_loop(in0 + 32, 8, hT, T)

            eng.wait_ge(s("product_read"), 2 + out0)
            with eng.Fori(0, BH) as j:
                eng.wait_ge(s("factors_ready"), j * 7 + 7)
                for r in range(NT):
                    mm = turn(pt[0][:, r * P:(r + 1) * P], kd[:, r * P:(r + 1) * P], P)
                mm.then_inc(s("kd_turned"), 1)
                for r in range(NT):
                    for a in range(NSUB):
                        mm = eng.matmul(pt[1][0:SUB * (a + 1), r * P + a * SUB:r * P + (a + 1) * SUB],
                                        kf_i[a][:, r, :], qf[:, r * P + a * SUB:r * P + (a + 1) * SUB],
                                        start=True, stop=True)
                mm.then_inc(s("scores_done"), 1)
                eng.wait_ge(s("scores_masked"), j * NSUB + NSUB)
                eng.wait_ge(s("kds_ready"), j + 1)
                for r in range(NT):
                    v = vrow[:, r, bass.ds(j * BV, BV)]
                    if r >= 2:
                        eng.wait_ge(s("state_ready"), j * NT + (r - 1))
                    eng.matmul(pg[0][:, r % 2, 0:BV], kds[:, r, :], v, start=True, stop=True).then_inc(s("state_part"), 1)
                    out = pt[2 + r // 2][:, (r % 2) * BV:(r % 2 + 1) * BV]
                    mm = eng.matmul(out, scT[:, r, :], v, start=True, stop=(r == 0))
                    if r >= 1:
                        eng.wait_ge(s("state_ready"), j * NT + r)
                        mm = eng.matmul(out, qd[:, r * P:(r + 1) * P], gstate, start=False, stop=True)
                        if r < NT - 1:
                            mm.then_inc(s("state_used"), 1)
                mm.then_inc(s("o_done"), 1)
                eng.wait_ge(s("o_normed"), j * NT + NT)
                eng.wait_ge(s("head_out"), j * 2 + 2)
                for v in range(NV):
                    for r in range(NT):
                        mm = turn(pg[1][:, v, r * P:(r + 1) * P], on[:, r, v * P:(v + 1) * P], P)
                mm.then_inc(s("o_turned"), 1)

            eng.wait_ge(s("head_out"), 2 + 2 * BH)
            for j in range(BH):
                mm = turn(pt[0][0:TS, j * P:(j + 1) * P], kT[:, j, TP:T], P)
            mm.then_inc(s("ks_turned"), 1)

            def outer(b):
                eng.wait_ge(s("km_ready"), b + 1)
                if b >= 2:
                    eng.wait_ge(s("sstate_read"), b - 1)
                for j in range(BH):
                    mm = eng.matmul(pg[j // 2][:, b % 2, (j % 2) * BV:(j % 2 + 1) * BV], km[b % 2][:, j * P:(j + 1) * P],
                                    vbs[:, j * BV:(j + 1) * BV], start=True, stop=True)
                mm.then_inc(s("outer_done"), 1)

            outer(0)
            for b in range(TS):
                if b + 1 < TS:
                    outer(b + 1)
                eng.wait_ge(s("sstate_read"), b + 1)
                for j in range(BH):
                    for v in range(NV):
                        n = (b * BH + j) * NV + v
                        mm = eng.matmul(pt[3][:, n:n + 1], stin[b][:, j, v * P:(v + 1) * P], qT[:, j, TP + b:TP + b + 1],
                                        start=True, stop=True)
            mm.then_inc(s("os_done"), 1)
            eng.wait_ge(s("os_squared"), 1)
            for v in range(NV):
                mm = eng.matmul(pt[0][:, 0:BH * TS], ones[:, :], oSq[:, :, v, :], start=(v == 0), stop=(v == NV - 1))
            mm.then_inc(s("os_summed"), 1)

            eng.wait_ge(s("gla_sample_done"), 1)
            product_loop(out0, 16, mT, T)
            eng.wait_ge(s("product_read"), 2 + xq0)
            product_loop(xq0, 16, hT, T, norm=1)
            eng.wait_ge(s("product_read"), 2 + xo0)
            eng.wait_ge(s("attn_loaded"), 32)
            eng.wait_ge(s("norm_root"), 2)

            units = [(h, r) for h in range(XH) for r in range(NT)]

            def scores(u):
                h, r = units[u]
                if u >= 2:
                    eng.wait_ge(s("p_exp"), u - 1)
                for k in range(XK):
                    mm = eng.matmul(pt[u % 2][:, 0:M], mT[:, h * XK + k, r * P:(r + 1) * P], kTm[:, h * XK + k, :],
                                    start=(k == 0), stop=(k == XK - 1))
                mm.then_inc(s("xscores_done"), 1)

            def turn_p(u):
                eng.wait_ge(s("p_ready"), u + 1)
                if u >= 2:
                    eng.wait_ge(s("pT_ready"), u - 1)
                for a in range(2):
                    mm = turn(pt[2 + u % 2][:, a * P:(a + 1) * P], stg[:, u % 2, a * P:(a + 1) * P], P)
                mm.then_inc(s("p_turned"), 1)

            def values(h):
                eng.wait_ge(s("pT_ready"), NT * (h + 1))
                for k in range(XK):
                    n = h * XK + k
                    if n >= 4:
                        eng.wait_ge(s("xo_read"), n - 3)
                    bank = pg[(n % 4) // 2][:, n % 2, :]
                    for a in range(2):
                        mm = eng.matmul(bank, vmr[:, a, n * P:(n + 1) * P], pT[h % 2][:, a, :], start=(a == 0), stop=(a == 1))
                    mm.then_inc(s("xo_done"), 1)

            for u in range(len(units) + 1):
                if u < len(units):
                    scores(u)
                if u >= 1:
                    turn_p(u - 1)
                if u >= 2 and (u - 2) % NT == NT - 1:
                    values((u - 2) // NT)
            values(XH - 1)

            eng.wait_ge(s("pT_ready"), len(units))
            for k in range(KD):
                mm = turn(pt[k // 4][0:TS, (k % 4) * P:(k % 4 + 1) * P], mT[:, k, TP:T], P)
            mm.then_inc(s("qs_turned"), 1)
            eng.wait_ge(s("qs_copied"), 1)
            eng.wait_ge(s("xo_read"), KD)
            for b in range(TS):
                if b >= 2:
                    eng.wait_ge(s("cache_used1"), b)
                for c in range(XH):
                    mm = eng.matmul(query_bank(b, c), ident[0:TS, b:b + 1].broadcast_to([TS, P]),
                                    srow[0:TS, c * XD:(c + 1) * XD], start=True, stop=True)
                mm.then_inc(s("qB_done"), 1)
            eng.wait_ge(s("cache_used1"), TS + 1)
            for a in range(2):
                mm = turn(pt[0][0:XH * TS, a * P:(a + 1) * P], wsf[:, a * 32:(a + 1) * 32], P)
            mm.then_inc(s("ss_turned"), 1)
            eng.wait_ge(s("pS_ready"), 1)
            for a in range(2):
                mm = turn(pt[1][:, a * 32:(a + 1) * 32], pS[:, a * P:(a + 1) * P], XH * TS)
            mm.then_inc(s("pS_turned"), 1)
            eng.wait_ge(s("pM_ready"), 1)
            for b in range(TS):
                for a in range(2):
                    n = b * 2 + a
                    eng.wait_ge(s(f"vcache_loaded{n % 4}"), 16 * (n // 4 + 1))
                    for h in range(XH):
                        mm = eng.matmul(pg[h // 2][0:TS, h % 2, :], pM[:, a, h, b, :], v_ring[n % 4][:, h * XD:(h + 1) * XD],
                                        start=(n == 0), stop=(n == 2 * TS - 1), skip_group_check=True)
                    mm.then_inc(s("vcache_used"), 1)
            eng.wait_ge(s("oxs_copied"), 1)
            for k in range(KD):
                mm = turn(pt[2][:, k * TS:(k + 1) * TS], srow[0:TS, k * P:(k + 1) * P], TS)
            mm.then_inc(s("oxs_turned"), 1)
            eng.wait_ge(s("oxs_read"), 1)
            product_loop(xo0, 16, hT, T)
            eng.wait_ge(s("product_read"), 2 + pq0)
            for n in range(4 * NT + 4):
                r, c = divmod(n, 4)
                if n >= 2:
                    eng.wait_ge(s("xrow_staged"), n - 1)
                for a in range(4):
                    k = 4 * c + a
                    src = xT[:, k, r * P:(r + 1) * P] if r < NT else xT[:, k, TP:T]
                    mm = turn(pt[2 + n % 2][0:(P if r < NT else TS), a * P:(a + 1) * P], src, P)
                mm.then_inc(s("xrow_turned"), 1)
            eng.wait_ge(s("xrow_staged"), 4 * NT + 4)
            for n in range(4):
                eng.wait_ge(s("keys_loaded"), 64)
                if n >= 2:
                    eng.wait_ge(s("keys_read"), n - 1)
                for a in range(4):
                    mm = turn(pt[2 + n % 2][:, a * P:(a + 1) * P], skr[:, 4 * n + a, :], P)
                mm.then_inc(s("keys_turned"), 1)
            eng.wait_ge(s("keys_read"), 4)

            def key_scores(r, h):
                eng.wait_ge(s("qs_ready"), r * PH + h + 1)
                eng.wait_ge(s("sc_copied"), r * PH + h + 1)
                for c in range(2):
                    mm = eng.matmul(pt[0][:, c * P:(c + 1) * P], qs[:, c * P:(c + 1) * P], skT[:, h * 2 + c, :],
                                    start=True, stop=True)
                mm.then_inc(s("sc_done"), 1)

            for slot in range(2):
                pe_product(eng, 0, slot, pq0, hT, T, 2 * KD if slot == 0 else None)
            norm_sum(2)
            with eng.Fori(0, PH - 1) as h:
                pe_product(eng, h + 1, 0, pq0, hT, T)
                key_scores(0, h)
                pe_product(eng, h + 1, 1, pq0, hT, T)
            key_scores(0, PH - 1)
            eng.wait_ge(s("product_read"), 2 + pq0 + 16)

            def acc(c):
                return pg[c // 2][:, c % 2, :]

            def tile_sum(r):
                eng.wait_ge(s("xrow_loaded"), r * 16 + 16)
                eng.wait_ge(s("y_ready"), r + 1)
                for c in range(4):
                    eng.matmul(acc(c), ident[:, :], xrow[:, c * 512:(c + 1) * 512], start=True, stop=True
                               ).then_inc(s("acc_started"), 1)
                with eng.Fori(0, PH) as h:
                    key_scores(r + 1, h)
                    with eng.Fori(0, TOPK // 4) as g:
                        for c in range(4):
                            eng.wait_ge(s("diag_ready"), r * E + h * TOPK + g * 4 + (c + 1))
                            eng.wait_ge(s(f"v_loaded{c}"), (r * (E // 4) + h * (TOPK // 4) + g) * 16 + 16)
                            for d in range(4):
                                mm = eng.matmul(acc(d), diag[c], vexp[c][:, d * 512:(d + 1) * 512], start=False, stop=True,
                                                skip_group_check=True)
                            mm.then_inc(s("v_used"), 1)

            with eng.Fori(0, NT // 2) as i:
                for p in range(2):
                    tile_sum(i * 2 + p)
            eng.wait_ge(s("picks_made"), 1)
            turn(pt[1][:, 0:TS], idxf[0:TS, :], TS)
            turn(pt[1][:, TS:2 * TS], gate_all[0][0:TS, :], TS).then_inc(s("picks_turned"), 1)
            eng.wait_ge(s("xrow_loaded"), (NT + 1) * 16)
            eng.wait_ge(s("y_ready"), NT + 1)
            eng.wait_ge(s("picks_ready"), 1)
            for c in range(4):
                eng.matmul(acc(c)[0:TS], ident[0:TS, 0:TS], xrow[0:TS, c * 512:(c + 1) * 512], start=True, stop=True
                           ).then_inc(s("acc_started"), 1)

            def spread(t):
                eng.wait_ge(s("u_used"), NT * E + t + 4)
                for c in range(4):
                    mm = eng.matmul(pt[c][:, :], ident[0:TS, t:t + 1].broadcast_to([TS, P]),
                                    hrow[0][0:TS, c * 512:(c + 1) * 512], start=True, stop=True)
                mm.then_inc(s("hB_done"), 1)

            spread(0)
            for t in range(TS):
                if t + 1 < TS:
                    spread(t + 1)
                c = t % 4
                eng.wait_ge(s("diag_ready"), NT * E + t + 1)
                eng.wait_ge(s(f"v_loaded{c}"), (NT * E // 4 + t // 4 + 1) * 16)
                for d in range(4):
                    mm = eng.matmul(acc(d)[0:TS], wmask[c], vexp[c][:, d * 512:(d + 1) * 512], start=False, stop=True,
                                    skip_group_check=True)
                mm.then_inc(s("v_used"), 1)

        @block.vector
        def _(eng):
            ch = Chain(eng, s("dve_chain"))
            for name, n in (("product_read", 2), ("sq_used", 2), ("head_out", 2), ("cache_used0", 1),
                            ("cache_used1", 1), ("u_used", 4), ("y_ready", 1), ("head_selected", 1)):
                eng.sem_inc(s(name), n)
            eng.memset(ones[:, :], 1.0).then_inc(s("ones_ready"), 1)
            eng.memset(epsT[:, :], EPS).then_inc(s("ones_ready"), 1)
            eng.memset(vss[:, :, :], 1.0).then_inc(s("ones_ready"), 1)
            eng.wait_ge(s("ones_ready"), 3)

            for item in range(2):
                eng.wait_ge(s("mem_root"), item + 1)
                ch.link(eng.reciprocal(rs[:, item:item + 1], ss[:, item:item + 1]))
                eng.tensor_scalar(rowbuf[:, item, :], rowbuf[:, item, :], rs[:, item:item + 1], None, ALU.mult
                                  ).then_inc(s("mem_scaled"), 1)
            unit = 0

            def take(ins_of):
                nonlocal unit
                eng.wait_ge(s("turned"), unit + 1)
                ins_of(pt[unit % 4]).then_inc(s("turn_read"), 1)
                unit += 1

            take(lambda t: eng.tensor_copy(gcol[:, :], t[:, 0:NG]))
            for u in range(2):
                take(lambda t: eng.tensor_copy(wsT[:, 4 * u:4 * u + 4, :], t.rearrange("p (h c) -> p h c", h=4)))
            eng.wait_ge(s("turn_read"), 1)
            for item in range(2):
                for g in range(4):
                    take(lambda t: eng.tensor_tensor(
                        memT[:, 4 * g:4 * g + 4, item * P:(item + 1) * P], t.rearrange("p (k c) -> p k c", k=4),
                        col_mem[:, 4 * g:4 * g + 4].unsqueeze(2).broadcast_to([P, 4, P]), ALU.mult))
            for r in range(NT):
                for g in range(4):
                    take(lambda t: eng.tensor_copy(xT[:, 4 * g:4 * g + 4, r * P:(r + 1) * P],
                                                   t.rearrange("p (k c) -> p k c", k=4)))
            take(lambda t: eng.tensor_copy(xT[:, :, TP:T], t[:, 0:P].rearrange("p (k c) -> p k c", k=KD)))

            for kv, b0 in enumerate((xk0, xv0)):
                if kv:
                    for slot in range(2):
                        eng.wait_ge(s(f"kT_stored{slot}"), 16 * (KD // 2 + 1))
                with eng.Fori(0, KD // 2) as i:
                    for slot in range(2):
                        await_product(eng, i, slot, b0)
                        eng.wait_ge(s("mem_turned"), i * 2 + (b0 + slot + 1))
                        if not kv:
                            eng.wait_ge(s(f"kT_stored{slot}"), i * 16 + 16)
                        eng.tensor_copy(stg[:, slot, 0:M], pg[slot][:, 0, 0:M]).then_inc(s("product_read"), 1)

            def norm_operand(n, col):
                with eng.Fori(0, KD // 2) as i:
                    for a in range(2):
                        eng.tensor_scalar(hT[:, i * 2 + a, :], xT[:, i * 2 + a, :], col[:, bass.ds(i * 2 + a, 1)], None,
                                          ALU.mult).then_inc(s("ht_ready"), 1)
                eng.wait_ge(s("sq_ready"), n * KD + 2)
                ch.link(eng.tensor_tensor(sqsum, sq[:, 0, :], sq[:, 1, :], ALU.add))
                eng.sem_inc(s("sq_used"), 2)
                with eng.Fori(1, KD // 2) as i:
                    st = ch.enter(i + (-1), 2)
                    for a in range(2):
                        eng.wait_ge(s("sq_ready"), i * 2 + (n * KD + a + 1))
                        ch.link(eng.tensor_tensor(sqsum, sqsum, sq[:, a, :], ALU.add))
                        eng.sem_inc(s("sq_used"), 1)
                ch.leave(st, KD // 2 - 1)
                eng.sem_inc(s("sq_added"), 1)
                eng.wait_ge(s("norm_root"), n + 1)
                ch.link(eng.reciprocal(rstdB[:, :, :], rstdB[:, :, :]))

            def read_loop(b0, count, ins_of, before=None):
                with eng.Fori(0, count // 2) as i:
                    for slot in range(2):
                        await_product(eng, i, slot, b0)
                        if before:
                            before(i, slot)
                        ins_of(i * 2 + slot, slot).then_inc(s("product_read"), 1)

            def halves(ap):
                return ap.rearrange("p (a t) -> p a t", a=2)

            eng.wait_ge(s("turn_read"), unit)
            eng.wait_ge(s("mem_turned"), 2 + 2 * KD)
            norm_operand(0, col_mix)
            eng.wait_ge(s("zg_done"), 1)
            eng.tensor_tensor(halves(zgT), pt4[0:RANK, 2:4, 0:HALF], rstdB[0:RANK], ALU.mult).then_inc(s("zg_read"), 1)
            prod = [pg[a][:, :, 0:HALF] for a in range(2)]
            read_loop(in0, 8, lambda n, a: eng.tensor_tensor(m2[:, n], prod[a], rstdB[:, :, :], ALU.mult))
            eng.wait_ge(s("mem_turned"), 2 + 2 * KD)
            read_loop(in0 + 8, 8, lambda n, a: eng.tensor_tensor(halves(stg[:, a, :]), prod[a], rstdB[:, :, :], ALU.mult),
                      lambda i, a: eng.wait_ge(s("val_turned"), i * 2 + (a + 1)))
            for slot in range(2):
                eng.wait_ge(s(f"memrow_stored{slot}"), 16 * (KD + 1))
            read_loop(in0 + 16, 4, lambda n, a: eng.scalar_tensor_tensor(
                halves(qT[:, n, :]), prod[a], float(P) ** -0.5, rstdB[:, :, :], ALU.mult, ALU.mult))

            eng.wait_ge(s("val_read"), 2 + 8)
            eng.wait_ge(s("consts_loaded"), 48)

            def va_rows(r):
                return (varow[:, r, :], P) if r < NT else (vas, TS)
            for r in range(NT + 1):
                v, n = va_rows(r)
                ch.link(eng.tensor_tensor(sgu_tmp[0:n], v, v, ALU.mult))
                eng.tensor_reduce(vss[0:n, r, :], sgu_tmp[0:n].rearrange("p (h c) -> p h c", h=AH), AX, ALU.add
                                  ).then_inc(s("va_squared"), 1)
                eng.wait_ge(s("va_squared"), r + 1)
            read_loop(in0 + 20, 4, lambda n, a: eng.tensor_tensor(halves(kT[:, n, :]), prod[a], rstdB[:, :, :], ALU.mult))
            eng.wait_ge(s("va_root"), 1)
            ch.link(eng.reciprocal(vss[:, :, :], vss[:, :, :]))
            for r in range(NT + 1):
                v, n = va_rows(r)
                v3 = v.rearrange("p (h c) -> p h c", h=AH)
                ch.link(eng.tensor_tensor(v3, v3, vss[0:n, r, :].unsqueeze(2).broadcast_to([n, AH, P]), ALU.mult))
                eng.tensor_tensor(v, v, gsguB[0:n], ALU.mult).then_inc(s("va_normed"), 1)
            eng.wait_ge(s("va_normed"), NT + 1)
            s3 = smix.rearrange("p (h c) -> p h c", h=AH)
            ch.link(eng.tensor_tensor(s3, vas.rearrange("p (h c) -> p h c", h=AH),
                                      w00B[0:TS].unsqueeze(2).broadcast_to([TS, AH, P]), ALU.mult))
            eng.tensor_tensor(s3, s3, bsB[0:TS, :, 0:1].broadcast_to([TS, AH, P]), ALU.add).then_inc(s("sgu_sample"), 1)
            read_loop(in0 + 24, 8, lambda n, a: eng.tensor_tensor(halves(stg[:, a, :]), prod[a], rstdB[:, :, :], ALU.mult),
                      lambda i, a: eng.wait_ge(s("val_turned"), i * 2 + (8 + a + 1)))

            for h in range(AH):
                eng.wait_ge(s("sgu_done"), h + 1)
                eng.tensor_tensor(gated, pt[h % 4].rearrange("p (r t) -> p r t", r=NT),
                                  bsB[:, h, :].unsqueeze(1).broadcast_to([P, NT, P]), ALU.add).then_inc(s("sgu_read"), 1)
                eng.wait_ge(s("sgu_read"), h + 1)
                if h == 0:
                    eng.wait_ge(s("u_acted"), 8)
                ch.link(eng.tensor_tensor(mT[:, h, 0:TP].rearrange("p (r t) -> p r t", r=NT),
                                          mT[:, h, 0:TP].rearrange("p (r t) -> p r t", r=NT), gated, ALU.mult))
            eng.wait_ge(s("sgu_done"), AH + 1)
            eng.tensor_tensor(mT[:, 0:AH, TP:T], mT[:, 0:AH, TP:T], pt[0][:, 0:AH * TS].rearrange("p (h c) -> p h c", h=AH),
                              ALU.mult).then_inc(s("sgu_read"), 1)

            for j in range(BH):
                eng.wait_ge(s("gate_done"), j + 1)
                eng.tensor_scalar(halves(G[:, j, :]), prod[j % 2], col_ba[:, j:j + 1], None, ALU.add
                                  ).then_inc(s("gate_read"), 1)
            read_loop(in0 + 32, 4, lambda n, a: eng.tensor_tensor(m2[:, n + 8], prod[a], rstdB[:, :, :], ALU.mult))
            Gf = rq[:, 2 * BH * T:3 * BH * T]
            eng.wait_ge(s("gate_ln"), 4)
            ch.link(eng.tensor_scalar(Gf, Gf, 0.0, None, ALU.min))
            for x in range(2):
                lg, G2 = gates_tmp[x], G[:, 2 * x:2 * x + 2, :]
                eng.wait_ge(s("gate_ln"), 3 * x + 3)
                ch.link(eng.tensor_tensor(G2, G2, lg, ALU.subtract))
                ch.link(eng.tensor_scalar(lg, G2, 1.0 / TAU, None, ALU.mult))
                for j in range(2):
                    for r in range(NT):
                        eng.tensor_tensor_scan(G2[:, j, r * P:(r + 1) * P], ones[:, :], lg[:, j, r * P:(r + 1) * P], 0.0,
                                               ALU.mult, ALU.add)
                ch.link(eng.tensor_copy(G2[:, :, TP:T], lg[:, :, TP:T]))
            read_loop(in0 + 36, 4, lambda n, a: eng.tensor_tensor(m2[:, n + 12], prod[a], rstdB[:, :, :], ALU.mult))
            ch.link(eng.memset(scT, 0.0))

            eng.wait_ge(s("r_acted"), 8)
            def by_chunk(x, j):
                return x[:, j, 0:TP].rearrange("p (r t) -> p r t", r=NT)

            def diffs(j):
                Gr = by_chunk(G, j)
                Gs = G[:, j, 0:TP].rearrange("p (a t) -> p a t", t=SUB)
                eng.tensor_tensor(qf.rearrange("p (a t) -> p a t", t=SUB), Gs,
                                  Gs[:, :, REF:REF + 1].broadcast_to([P, NT * NSUB, SUB]), ALU.subtract
                                  ).then_inc(s("diffs_ready"), 1)
                for a in range(NSUB):
                    n = SUB * (a + 1)
                    eng.tensor_tensor(kf_i[a], Gr[:, :, a * SUB + REF:a * SUB + REF + 1].broadcast_to([P, NT, n]),
                                      Gr[:, :, 0:n], ALU.subtract).then_inc(s("diffs_ready"), 1)
                kd3 = kd.rearrange("p (r t) -> p r t", r=NT)
                eng.tensor_tensor(kd3, Gr[:, :, P - 1:P].broadcast_to([P, NT, P]), Gr, ALU.subtract
                                  ).then_inc(s("diffs_ready"), 1)

            def factors_of(j):
                kr = by_chunk(kT, j)
                eng.wait_ge(s("exps_ready"), j * 3 + 3)
                eng.tensor_tensor(kd, kd, kT[:, j, 0:TP], ALU.mult).then_inc(s("factors_ready"), 1)
                eng.tensor_tensor(qf, qf, qT[:, j, 0:TP], ALU.mult).then_inc(s("factors_ready"), 1)
                for a in range(NSUB):
                    eng.tensor_tensor(kf_i[a], kf_i[a], kr[:, :, 0:SUB * (a + 1)], ALU.mult).then_inc(s("factors_ready"), 1)
                eng.tensor_tensor(qd, qd, qT[:, j, 0:TP], ALU.mult).then_inc(s("factors_ready"), 1)

            def gla_head(j, last):
                eng.wait_ge(s("scores_done"), j + 1)
                for a in range(NSUB):
                    n, c = SUB * (a + 1), a * SUB
                    eng.tensor_tensor(scT[0:n, :, c:c + SUB], pt[1][0:n].rearrange("p (r t) -> p r t", r=NT)[:, :, c:c + SUB],
                                      tri[0:n, c:c + SUB].unsqueeze(1).broadcast_to([n, NT, SUB]), ALU.mult
                                      ).then_inc(s("scores_masked"), 1)
                eng.wait_ge(s("state_stored"), j * 16 + 16)
                for r in range(NT):
                    eng.wait_ge(s("state_part"), j * NT + (r + 1))
                    part = pg[0][:, r % 2, 0:BV]
                    if r == 0:
                        eng.tensor_copy(gstate, part).then_inc(s("state_ready"), 1)
                        continue
                    if r < NT - 1:
                        eng.wait_ge(s("state_used"), j * (NT - 2) + r)
                    else:
                        eng.wait_ge(s("o_done"), j + 1)
                    eng.wait_ge(s("state_ready"), j * NT + r)
                    eng.scalar_tensor_tensor(gstate, gstate, glast[:, r:r + 1], part, ALU.mult, ALU.add
                                             ).then_inc(s("state_ready"), 1)
                if not last:
                    diffs(j + 1)
                eng.wait_ge(s("o_root"), j + 1)
                ch.link(eng.reciprocal(rs[:, 0:NT], ss[:, 0:NT]))
                for r in range(NT):
                    eng.tensor_scalar(on[:, r, :], pt[2 + r // 2][:, (r % 2) * BV:(r % 2 + 1) * BV], rs[:, r:r + 1], None,
                                      ALU.mult).then_inc(s("o_normed"), 1)
                if not last:
                    factors_of(j + 1)
                eng.wait_ge(s("o_turned"), j + 1)
                for v in range(NV):
                    m = mT[:, j * NV + (AH + v), 0:TP]
                    eng.scalar_tensor_tensor(m, pg[1][:, v, :], col_gla[:, bass.ds(j * NV + v, 1)], m, ALU.mult, ALU.mult
                                             ).then_inc(s("head_out"), 1)

            diffs(0)
            factors_of(0)
            with eng.Fori(0, BH - 1) as j:
                st = ch.enter(j, 1)
                gla_head(j, False)
            ch.leave(st, BH - 1)
            gla_head(BH - 1, True)

            eng.wait_ge(s("ks_ready"), 2)

            def mask_keys(b):
                if b >= 2:
                    eng.wait_ge(s("outer_done"), b - 1)
                eng.tensor_scalar(km[b % 2], kss, ident[0:TS, b:b + 1], None, ALU.mult).then_inc(s("km_ready"), 1)

            for b in range(2):
                mask_keys(b)
            for b in range(TS):
                eng.wait_ge(s("outer_done"), b + 1)
                eng.wait_ge(s(f"sstate_loaded{b // (TS // 2)}"), 16 * (TS // 2))
                for h in range(BH):
                    ins = eng.scalar_tensor_tensor(stin[b][:, h, :], stin[b][:, h, :], ea[:, h, b:b + 1],
                                                   pg[h // 2][:, b % 2, (h % 2) * BV:(h % 2 + 1) * BV], ALU.mult, ALU.add)
                ins.then_inc(s("sstate_read"), 1)
                if b + 2 < TS:
                    mask_keys(b + 2)
            eng.wait_ge(s("os_root"), 1)
            ch.link(eng.reciprocal(roS, roS))
            for v in range(NV):
                ch.link(eng.tensor_tensor(oS[:, :, v, :], oS[:, :, v, :], roS, ALU.mult))
            for h in range(BH):
                for v in range(NV):
                    m = mT[:, AH + h * NV + v, TP:T]
                    ins = eng.scalar_tensor_tensor(m, oS[:, h, v, :], col_gla[:, h * NV + v:h * NV + v + 1], m, ALU.mult, ALU.mult)
            ins.then_inc(s("gla_sample_done"), 1)

            read_loop(out0, 16, lambda n, a: eng.tensor_tensor(x2[:, n], x2[:, n], prod[a], ALU.add))
            eng.wait_ge(s("sstate_stored"), 16 * TS)
            eng.wait_ge(s("state_stored"), 16 * (BH + 1))
            eng.wait_ge(s("product_read"), 2 + xq0)
            norm_operand(1, col_xq)
            read_loop(xq0, 16, lambda n, a: eng.scalar_tensor_tensor(
                m2[:, n], prod[a], float(XD) ** -0.5, rstdB[:, :, :], ALU.mult, ALU.mult))

            for u in range(XH * NT):
                a = u % 2
                eng.wait_ge(s("xscores_done"), u + 1)
                ch.link(eng.tensor_reduce(ss[:, 4 + a:5 + a], pt[a][:, 0:M], AX, ALU.max))
                eng.tensor_scalar(ss[:, 6 + a:7 + a], ss[:, 4 + a:5 + a], -1.0, None, ALU.mult).then_inc(s("p_max"), 1)
                eng.wait_ge(s("p_exp"), u + 1)
                ch.link(eng.reciprocal(rs[:, 4 + a:5 + a], ss[:, 8 + a:9 + a]))
                eng.tensor_scalar(stg[:, a, 0:M], stg[:, a, 0:M], rs[:, 4 + a:5 + a], None, ALU.mult).then_inc(s("p_ready"), 1)

            for b in range(TS):
                eng.wait_ge(s("qB_done"), b + 1)
                for a in range(2):
                    eng.wait_ge(s(f"cache_loaded{a}"), b * 16 + 16)
                    for h in range(XH):
                        keys = k_ring[a][:, h * XD:(h + 1) * XD]
                        ins = eng.tensor_tensor_reduce(keys, keys, query_bank(b, h), 1.0, 0.0, ALU.mult, ALU.add,
                                                       sS[:, a, h, b:b + 1])
                    ins.then_inc(s(f"cache_used{a}"), 1)
            NS = XH * TS
            eng.wait_ge(s("ss_turned"), 1)
            ch.link(eng.tensor_reduce(ss[0:NS, 4:5], pt[0][0:NS, 0:M], AX, ALU.max))
            eng.tensor_scalar(ss[0:NS, 6:7], ss[0:NS, 4:5], -1.0, None, ALU.mult).then_inc(s("p_max"), 1)
            eng.wait_ge(s("pS_exp"), 1)
            ch.link(eng.reciprocal(rs[0:NS, 4:5], ss[0:NS, 8:9]))
            eng.tensor_scalar(pS, pS, rs[0:NS, 4:5], None, ALU.mult).then_inc(s("pS_ready"), 1)
            eng.wait_ge(s("pST_ready"), 1)
            eng.tensor_tensor(pM.rearrange("p m h b c -> p (m h) b c"),
                              pST.rearrange("p (n b) -> p n b", b=TS).unsqueeze(3).broadcast_to([P, 2 * XH, TS, TS]),
                              e8[:, :, :].unsqueeze(1).broadcast_to([P, 2 * XH, TS, TS]), ALU.mult).then_inc(s("pM_ready"), 1)

            read_loop(xo0, 16, lambda n, a: eng.tensor_tensor(x2[:, n], x2[:, n], prod[a], ALU.add))
            eng.wait_ge(s("product_read"), 2 + pq0)
            norm_operand(2, col_ffn)

            eng.wait_ge(s("iota_made"), 1)
            ch.link(eng.tensor_copy(jota, jint))

            def passed():
                eng.sem_inc(s("dve_passed"), 1)

            def top16(vals, idx, table, rest):
                passed()
                ch.link(eng.max(vals[:, 0:8], table))
                passed()
                eng.max_index(idx[:, 0:8], vals[:, 0:8], table)
                ch.link(eng.match_replace(rest, vals[:, 0:8], table, NEG))
                passed()
                ch.link(eng.max(vals[:, 8:16], rest))
                passed()
                ch.link(eng.max_index(idx[:, 8:16], vals[:, 8:16], rest))

            c3, o3 = (x.rearrange("p (i j) -> p i j", i=TOPK) for x in (cand, onehot))
            pairs = [P, TOPK, TOPK]

            def top_half(r, h, c):
                eng.wait_ge(s("sc_copied"), r * PH + h + 2)
                top16(sv[:, c * 16:c * 16 + 16], si[:, c * 16:c * 16 + 16], sc[:, c * P:(c + 1) * P], sc2[:, c * P:(c + 1) * P])

            def top_pairs():
                eng.tensor_copy(sif, si)
                ch.link(eng.tensor_tensor(c3, sv[:, 0:16].unsqueeze(2).broadcast_to(pairs),
                                          sv[:, 16:32].unsqueeze(1).broadcast_to(pairs), ALU.add))
                top16(ts, pos, cand, cand2)
                eng.tensor_scalar(ntop, ts[:, 0:1], -1.0, None, ALU.mult).then_inc(s("top_ready"), 1)

            def keep_picks(r, h, p):
                eng.tensor_scalar(posi, pos, 4, None, ALU.logical_shift_right)
                ch.link(eng.tensor_scalar(posj, pos, 15, None, ALU.bitwise_and))
                eng.tensor_copy(pif, posi)
                ch.link(eng.tensor_copy(pjf, posj))
                for c, (pf, out) in enumerate(((pif, pa), (pjf, pb))):
                    ch.link(eng.tensor_tensor(o3, jota.unsqueeze(1).broadcast_to(pairs),
                                              pf.unsqueeze(2).broadcast_to(pairs), ALU.is_equal))
                    ch.link(eng.tensor_tensor(o3, o3, sif[:, c * 16:c * 16 + 16].unsqueeze(1).broadcast_to(pairs), ALU.mult))
                    ch.link(eng.tensor_reduce(out, o3, AX, ALU.add))
                at = bass.ds(h * TOPK, TOPK)
                ch.link(eng.scalar_tensor_tensor(pa, pa, float(P), pb, ALU.mult, ALU.add))
                eng.tensor_copy(idx_all[p][:, at], pa)
                eng.wait_ge(s("top_exp"), r * PH + h + 1)
                ch.link(eng.reciprocal(erec, esum))
                eng.tensor_scalar(gate_all[p][:, at], ex, erec, None, ALU.mult).then_inc(s("head_selected"), 1)

            def select_head(r, h, p):
                for c in range(2):
                    top_half(r, h, c)
                top_pairs()
                keep_picks(r, h, p)

            def norm_rows(r, p):
                eng.wait_ge(s("xrow_root"), r + 1)
                ch.link(eng.reciprocal(rs[:, 0:1], ss[:, 0:1]))
                eng.scalar_tensor_tensor(hrow[p], xrow, rs[:, 0:1], gffnB, ALU.mult, ALU.mult).then_inc(s("hrow_ready"), 1)
                eng.wait_ge(s("hrow_ready"), r + 1)
                passed()

            def finish(n, r):
                eng.wait_ge(s("y_root"), r + 1)
                ch.link(eng.reciprocal(rs[0:n, 1:2], ss[0:n, 3:4]))
                eng.wait_ge(s("y_stored"), r * 16 + 16)
                for a in range(2):
                    ins = eng.scalar_tensor_tensor(ystage[0:n, a * 1024:(a + 1) * 1024].rearrange("p (c d) -> p c d", c=2),
                                                   pg[a][0:n], rs[0:n, 1:2],
                                                   gfinB[0:n, a * 1024:(a + 1) * 1024].rearrange("p (c d) -> p c d", c=2),
                                                   ALU.mult, ALU.mult)
                ins.then_inc(s("y_ready"), 1)

            SEL = 23

            def query_block(i, slot):
                await_product(eng, i, slot, pq0)
                eng.tensor_tensor(m2[:, i * 2 + slot], prod[slot], rstdB[:, :, :], ALU.mult).then_inc(s("product_read"), 1)

            for slot in range(2):
                query_block(0, slot)
            def dot(j, p, loaded, n):
                eng.wait_ge(s(f"u_loaded{j % 4}"), loaded)
                eng.wait_ge(s("act_read"), n + 1)
                eng.tensor_tensor_reduce(urow[j % 4], urow[j % 4], hrow[p], 1.0, 0.0, ALU.mult, ALU.add, act4[:, j % 4:j % 4 + 1]
                                         ).then_inc(s("u_used"), 1)

            def early_dots(h, half):
                for j in range(half * EJ // 2, (half + 1) * EJ // 2):
                    dot(j, 0, h * (EJ // 4 * 16) + (j // 4 + 1) * 16, h * EJ + j)

            query_block(1, 0)
            select_head(0, 0, 0)
            query_block(1, 1)
            eng.wait_ge(s("peer_consts"), 32)
            norm_rows(0, 0)
            with eng.Fori(0, PH - 2) as h:
                sh = ch.enter(h, SEL)
                query_block(h + 2, 0)
                early_dots(h, 0)
                for c in range(2):
                    top_half(0, h + 1, c)
                query_block(h + 2, 1)
                top_pairs()
                keep_picks(0, h + 1, 0)
                early_dots(h, 1)
            ch.leave(sh, PH - 2)
            early_dots(PH - 2, 0)
            select_head(0, PH - 1, 0)
            early_dots(PH - 2, 1)

            def head(r, p, h, late):
                for g in range(TOPK // 4):
                    for j in range(4 * g, 4 * g + 4):
                        if not late or j >= EJ:
                            dot(j, p, u_arrived(r, h, j, late), u_index(r, h, j, late))
                    if g < 2:
                        top_half(r + 1, h, g)
                    elif g == 2:
                        top_pairs()
                    else:
                        keep_picks(r + 1, h, 1 - p)

            for r in range(NT):
                p, heads = r % 2, PH if r else EH
                with eng.Fori(0, heads) as h:
                    sh = ch.enter(h, SEL)
                    head(r, p, h, r == 0)
                ch.leave(sh, heads)
                if r == 0:
                    head(0, 0, PH - 1, False)
                norm_rows(r + 1, 1 - p)
                eng.wait_ge(s("y_squared"), r + 1)
                ch.link(eng.tensor_tensor(ss[:, 3:4], ss[:, 1:2], ss[:, 2:3], ALU.add))
                eng.sem_inc(s("y_summed"), 1)
                finish(P, r)

            ch.link(eng.tensor_copy(idxf, idx_all[0]))
            eng.sem_inc(s("picks_made"), 1)
            eng.wait_ge(s("picks_turned"), 1)
            eng.tensor_copy(idxS, pt[1][:, 0:TS])
            eng.tensor_copy(gateS, pt[1][:, TS:2 * TS]).then_inc(s("picks_ready"), 1)
            for t in range(TS):
                c = t % 4
                eng.wait_ge(s("hB_done"), t + 1)
                eng.wait_ge(s(f"u_loaded{c}"), (NT * E // 4 + t // 4 + 1) * 16)
                eng.wait_ge(s("act_read"), NT * E + t + 1)
                eng.tensor_tensor_reduce(urow[c], urow[c], pt4[:, :, :].rearrange("p a d -> p (a d)"), 1.0, 0.0, ALU.mult,
                                         ALU.add, act4[:, c:c + 1]).then_inc(s("u_used"), 1)
            eng.wait_ge(s("y_squared"), NT + 1)
            ch.link(eng.tensor_tensor(ss[0:TS, 3:4], ss[0:TS, 1:2], ss[0:TS, 2:3], ALU.add))
            eng.sem_inc(s("y_summed"), 1)
            finish(TS, NT)

        @block.scalar
        def _(eng):
            ch = Chain(eng, s("act_chain"))
            act = eng.activation
            for name, n in (("memrow_ready", 2), ("val_read", 2), ("sc_copied", 1), ("act_read", 4)):
                eng.sem_inc(s(name), n)
            eng.wait_ge(s("ones_ready"), 3)
            for item in range(2):
                eng.wait_ge(s(f"rows_loaded{item}"), 16)
                ch.link(act(hflat[:, 2048:4096], rowbuf[:, item, :], ACT.Square, accum_out=ss[:, item:item + 1]))
                act(ss[:, item:item + 1], ss[:, item:item + 1], ACT.Sqrt, bias=epsT[:, :], scale=1.0 / D).then_inc(s("mem_root"), 1)

            for b0 in (xk0, xv0):
                with eng.Fori(0, KD // 2) as i:
                    for slot in range(2):
                        eng.wait_ge(s("mem_turned"), i * 2 + (b0 + slot + 3))
                        eng.wait_ge(s(f"memrow_stored{slot}"), i * 16 + (b0 // 2 + 1) * 16)
                        eng.copy(rq[:, slot * M:(slot + 1) * M], pt[slot][:, 0:M]).then_inc(s("memrow_ready"), 1)

            def norm_squares(n):
                with eng.Fori(0, KD // 2) as i:
                    for a in range(2):
                        eng.wait_ge(s("sq_used"), i * 2 + (n * KD + a + 1))
                        act(sq[:, a, :], xT[:, i * 2 + a, :], ACT.Square).then_inc(s("sq_ready"), 1)

            def norm_root(n):
                eng.wait_ge(s("norm_summed"), n + 1)
                act(rstdB[:, :, :], pt4[:, 0:2, 0:HALF], ACT.Sqrt, bias=epsT[:, :], scale=1.0 / D).then_inc(s("norm_root"), 1)

            eng.wait_ge(s("turn_read"), 28)
            norm_squares(0)
            norm_root(0)
            with eng.Fori(0, 4) as i:
                for a in range(2):
                    eng.wait_ge(s("product_read"), i * 2 + (in0 + a + 3))
                    act(mT[:, i * 2 + a, :], mT[:, i * 2 + a, :], ACT.Gelu_apprx_tanh).then_inc(s("u_acted"), 1)

            def value_rows(i, a, first, rows, srows):
                eng.wait_ge(s("val_turned"), i * 2 + (first + a + 3))
                at = bass.ds((i * 2 + a) * P, P)
                eng.copy(rows[:, :, at], pt[a].rearrange("p (r c) -> p r c", r=NT))
                eng.copy(srows[:, at], pt[2 + a][0:TS, 0:P]).then_inc(s("val_read"), 1)

            with eng.Fori(0, 4) as i:
                for a in range(2):
                    eng.wait_ge(s("product_read"), i * 2 + (in0 + 8 + a + 3))
                    act(stg[:, a, :], stg[:, a, :], ACT.Gelu_apprx_tanh).then_inc(s("val_staged"), 1)
                for a in range(2):
                    value_rows(i, a, 0, varow, vas)
            eng.wait_ge(s("va_squared"), NT + 1)
            act(vss[:, :, :], vss[:, :, :], ACT.Sqrt, bias=epsT[:, :], scale=1.0 / P).then_inc(s("va_root"), 1)
            with eng.Fori(0, 4) as i:
                for a in range(2):
                    value_rows(i, a, 8, vrow, vbs)
            eng.wait_ge(s("gate_read"), BH)
            for x, g in enumerate(gates_tmp):
                act(g, G[:, 2 * x:2 * x + 2, :], ACT.Abs).then_inc(s("gate_ln"), 1)
                eng.wait_ge(s("gate_ln"), 3 * x + 1)
                act(g, g, ACT.Exp, scale=-1.0).then_inc(s("gate_ln"), 1)
                eng.wait_ge(s("gate_ln"), 3 * x + 2)
                act(g, g, ACT.Ln, bias=1.0).then_inc(s("gate_ln"), 1)
            with eng.Fori(0, 4) as i:
                for a in range(2):
                    eng.wait_ge(s("product_read"), i * 2 + (in0 + 32 + a + 3))
                    m = mT[:, i * 2 + (AH + a), :]
                    act(m, m, ACT.Silu).then_inc(s("r_acted"), 1)

            def factor_exps(j):
                eng.wait_ge(s("diffs_ready"), j * 6 + 6)
                act(factors, factors, ACT.Exp).then_inc(s("exps_ready"), 1)
                act(qd, G[:, j, 0:TP], ACT.Exp).then_inc(s("exps_ready"), 1)
                act(glast, G[:, j, 0:TP].rearrange("p (r t) -> p r t", r=NT)[:, :, P - 1], ACT.Exp).then_inc(s("exps_ready"), 1)

            def gla_head(j, last):
                eng.wait_ge(s("kd_turned"), j + 1)
                eng.copy(kds, pt[0].rearrange("p (r d) -> p r d", r=NT)).then_inc(s("kds_ready"), 1)
                eng.wait_ge(s("o_done"), j + 1)
                for r in range(NT):
                    ins = act(on[:, r, :], pt[2 + r // 2][:, (r % 2) * BV:(r % 2 + 1) * BV], ACT.Square,
                              accum_out=ss[:, r:r + 1])
                ch.link(ins)
                act(ss[:, 0:NT], ss[:, 0:NT], ACT.Sqrt, bias=epsT[:, :], scale=1.0 / BV).then_inc(s("o_root"), 1)
                if not last:
                    factor_exps(j + 1)

            factor_exps(0)
            with eng.Fori(0, BH - 1) as j:
                st = ch.enter(j, 1)
                gla_head(j, False)
            ch.leave(st, BH - 1)
            gla_head(BH - 1, True)

            act(ea, G[:, :, TP:T], ACT.Exp).then_inc(s("ks_ready"), 1)
            eng.wait_ge(s("ks_turned"), 1)
            eng.copy(kss, pt[0][0:TS, 0:BH * P]).then_inc(s("ks_ready"), 1)
            eng.wait_ge(s("os_done"), 1)
            eng.copy(oS.rearrange("p h v b -> p (h v) b"), pt[3][:, 0:TS * BH * NV].rearrange("p (b n) -> p n b", b=TS)
                     ).then_inc(s("os_read"), 1)
            eng.wait_ge(s("os_read"), 1)
            act(oSq, oS, ACT.Square).then_inc(s("os_squared"), 1)
            eng.wait_ge(s("os_summed"), 1)
            act(roS, pt[0][:, 0:BH * TS].rearrange("p (h b) -> p h b", h=BH), ACT.Sqrt, bias=epsT[:, :], scale=1.0 / BV
                ).then_inc(s("os_root"), 1)

            eng.wait_ge(s("product_read"), 2 + xq0)
            norm_squares(1)
            norm_root(1)

            def p_exp(u):
                a = u % 2
                eng.wait_ge(s("p_max"), u + 1)
                if u >= 2:
                    eng.wait_ge(s("p_turned"), u - 1)
                act(stg[:, a, 0:M], pt[a][:, 0:M], ACT.Exp, bias=ss[:, 6 + a:7 + a], accum_out=ss[:, 8 + a:9 + a]
                    ).then_inc(s("p_exp"), 1)

            def p_rows(u):
                h, r = divmod(u, NT)
                eng.wait_ge(s("p_turned"), u + 1)
                if h >= 2 and r == 0:
                    eng.wait_ge(s("xo_done"), XK * (h - 1))
                eng.copy(pT[h % 2][:, :, r * P:(r + 1) * P], pt[2 + u % 2][:, 0:2 * P].rearrange("p (m t) -> p m t", m=2)
                         ).then_inc(s("pT_ready"), 1)

            def out_rows(h):
                for k in range(XK):
                    n = h * XK + k
                    eng.wait_ge(s("xo_done"), n + 1)
                    eng.copy(hT[:, n, 0:TP], pg[(n % 4) // 2][:, n % 2, :]).then_inc(s("xo_read"), 1)

            for u in range(XH * NT + 1):
                if u < XH * NT:
                    p_exp(u)
                if u >= 1:
                    p_rows(u - 1)
                if u >= 2 and (u - 2) % NT == NT - 1:
                    out_rows((u - 2) // NT)
            out_rows(XH - 1)

            eng.wait_ge(s("qs_turned"), 1)
            eng.copy(srow[0:TS, 0:D].rearrange("p (a d) -> p a d", a=4), pt4[0:TS]).then_inc(s("qs_copied"), 1)
            NS = XH * TS
            eng.wait_ge(s("p_max"), XH * NT + 1)
            act(pS, pt[0][0:NS, 0:M], ACT.Exp, bias=ss[0:NS, 6:7], accum_out=ss[0:NS, 8:9]).then_inc(s("pS_exp"), 1)
            eng.wait_ge(s("pS_turned"), 1)
            eng.copy(pST, pt[1][:, 0:2 * NS]).then_inc(s("pST_ready"), 1)
            eng.wait_ge(s("vcache_used"), 2 * TS)
            for a in range(2):
                ins = eng.copy(srow[0:TS, a * 1024:(a + 1) * 1024].rearrange("p (c d) -> p c d", c=2), pg[a][0:TS])
            ins.then_inc(s("oxs_copied"), 1)
            eng.wait_ge(s("oxs_turned"), 1)
            eng.copy(hT[:, :, TP:T], pt[2][:, 0:KD * TS].rearrange("p (k b) -> p k b", k=KD)).then_inc(s("oxs_read"), 1)

            eng.wait_ge(s("product_read"), 2 + pq0)
            for n in range(4 * NT + 4):
                rows = P if n // 4 < NT else TS
                eng.wait_ge(s("xrow_turned"), n + 1)
                if n >= 4:
                    eng.wait_ge(s(f"x_stored{n % 4}"), 16 * (n // 4))
                eng.copy(xst[n % 4][0:rows], pt[2 + n % 2][0:rows]).then_inc(s("xrow_staged"), 1)
                eng.wait_ge(s("xrow_staged"), n + 1)
                r, c = divmod(n, 4)
                eng.dma_start(x_scr[r * P:r * P + rows, c * 512:(c + 1) * 512],
                              xst[n % 4][0:rows]).then_inc(s(f"x_stored{n % 4}"), 16)
            for n in range(4):
                eng.wait_ge(s("keys_turned"), n + 1)
                eng.copy(skT[:, 4 * n:4 * n + 4, :], pt[2 + n % 2].rearrange("p (n c) -> p n c", n=4)).then_inc(s("keys_read"), 1)
            norm_squares(2)
            norm_root(2)
            for a in range(4):
                eng.wait_ge(s(f"x_stored{a}"), 16 * (NT + 1))
            eng.dma_start(xrow, x_scr[0:P, :]).then_inc(s("xrow_loaded"), 16)

            def copy_scores(r, h):
                for c in range(2):
                    ins = eng.copy(qs[:, c * P:(c + 1) * P], mflat[:, bass.ds(r * P + h * (2 * T) + c * T, P)])
                ins.then_inc(s("qs_ready"), 1)
                eng.wait_ge(s("sc_done"), r * PH + h + 1)
                eng.wait_ge(s("head_selected"), r * PH + h + 1)
                eng.copy(sc, pt[0][:, 0:2 * P]).then_inc(s("sc_copied"), 1)

            def top_exp(r, h):
                eng.wait_ge(s("top_ready"), r * PH + h + 1)
                act(ex, ts, ACT.Exp, bias=ntop, accum_out=esum).then_inc(s("top_exp"), 1)

            def row_root(r, p):
                eng.wait_ge(s("xrow_loaded"), r * 16 + 16)
                ch.link(act(hrow[p], xrow, ACT.Square, accum_out=ss[:, 0:1]))
                act(ss[:, 0:1], ss[:, 0:1], ACT.Sqrt, bias=epsT[:, :], scale=1.0 / D).then_inc(s("xrow_root"), 1)

            def y_root(n, r, p):
                eng.wait_ge(s("v_used"), r * E + (E + 4) if n == P else NT * E + TS + 4)
                for a in range(2):
                    ins = act(hrow[p][0:n, a * 1024:(a + 1) * 1024].rearrange("p (c d) -> p c d", c=2), pg[a][0:n], ACT.Square,
                              accum_out=ss[0:n, 1 + a:2 + a])
                ins.then_inc(s("y_squared"), 1)
                eng.wait_ge(s("y_summed"), r + 1)
                act(ss[0:n, 3:4], ss[0:n, 3:4], ACT.Sqrt, bias=epsT[0:n], scale=1.0 / D).then_inc(s("y_root"), 1)

            def gelu(j, n):
                c = j % 4
                eng.wait_ge(s("u_used"), n + 5)
                act(g4[:, c:c + 1], act4[:, c:c + 1], ACT.Gelu_apprx_tanh).then_inc(s("act_read"), 1)
                eng.wait_ge(s("act_read"), n + 5)

            def early_weights(h, half):
                eng.wait_ge(s("head_selected"), h + 2)
                for j in range(half * EJ // 2, (half + 1) * EJ // 2):
                    gelu(j, h * EJ + j)
                    ch.link(act(early_w[:, bass.ds(h * EJ + j, 1)], gate_all[0][:, bass.ds(h * TOPK + j, 1)], ACT.Copy,
                                scale=g4[:, j % 4:j % 4 + 1]))

            eng.wait_ge(s("product_read"), pq0 + 4)
            copy_scores(0, 0)
            top_exp(0, 0)
            row_root(0, 0)
            with eng.Fori(0, PH - 2) as h:
                sh = ch.enter(h, EJ)
                eng.wait_ge(s("product_read"), h * 2 + (pq0 + 6))
                copy_scores(0, h + 1)
                early_weights(h, 0)
                top_exp(0, h + 1)
                early_weights(h, 1)
            ch.leave(sh, PH - 2)
            eng.wait_ge(s("product_read"), pq0 + 2 + 2 * PH)
            copy_scores(0, PH - 1)
            early_weights(PH - 2, 0)
            top_exp(0, PH - 1)
            early_weights(PH - 2, 1)

            def head(r, p, h, late):
                copy_scores(r + 1, h)
                for j in range(TOPK):
                    c = j % 4
                    if late and j < EJ:
                        ch.link(act(w4[:, c:c + 1], early_w[:, bass.ds(h * EJ + j, 1)], ACT.Copy))
                    else:
                        gelu(j, u_index(r, h, j, late))
                        ch.link(act(w4[:, c:c + 1], gate_all[p][:, bass.ds(h * TOPK + j, 1)], ACT.Copy, scale=g4[:, c:c + 1]))
                    eng.wait_ge(s("v_used"), r * E + h * TOPK + (j + 1))
                    ch.link(act(diag[c], ident[:, :], ACT.Copy, scale=w4[:, c:c + 1]))
                    eng.sem_inc(s("diag_ready"), 1)
                top_exp(r + 1, h)

            for r in range(NT):
                p, heads = r % 2, PH if r else EH
                with eng.Fori(0, heads) as h:
                    sh = ch.enter(h, 2 * TOPK)
                    head(r, p, h, r == 0)
                ch.leave(sh, heads)
                if r == 0:
                    head(0, 0, PH - 1, False)
                row_root(r + 1, 1 - p)
                y_root(P, r, p)
            eng.wait_ge(s("picks_ready"), 1)
            for t in range(TS):
                c = t % 4
                eng.wait_ge(s("u_used"), NT * E + t + 5)
                act(g4[:, c:c + 1], act4[:, c:c + 1], ACT.Gelu_apprx_tanh).then_inc(s("act_read"), 1)
                eng.wait_ge(s("act_read"), NT * E + t + 5)
                ch.link(act(w4[:, c:c + 1], gateS[:, t:t + 1], ACT.Copy, scale=g4[:, c:c + 1]))
                eng.wait_ge(s("v_used"), NT * E + t + 1)
                act(wmask[c], e8[:, t, :], ACT.Copy, scale=w4[:, c:c + 1]).then_inc(s("diag_ready"), 1)
            y_root(TS, NT, 0)


_INS = ["x_prompt", "x_sample", "mem_prompt", "cache_mem_k", "cache_mem_v", "state_gla", "g_mix", "w_in", "w_alpha",
        "b_alpha", "w_s", "b_s", "g_sgu", "g_gla", "w_out", "g_mem", "w_xk", "w_xv", "g_xq", "w_xq", "w_xo", "g_ffn",
        "w_pq", "sub_keys", "u_emb", "v_emb", "g_final"]
_OUTS = [(1, 512, 2048), (8, 1, 2048), (1, 1, 256, 4, 512), (1, 1, 256, 4, 512), (1, 1, 4, 128, 256),
         (1, 8, 4, 128, 256), (1, 1, 128, 8, 128), (1, 8, 1, 8, 128)]


def kernel(**inputs):
    import concourse.bacc as _bacc
    from concourse.bass_utils import run_bass_kernel_spmd as _run

    nc = _bacc.Bacc("TRN2", target_bir_lowering=False, num_devices=1)
    arrays, args = {}, []
    for name in _INS:
        a = np.ascontiguousarray(inputs[name])
        arrays[f"in_{name}_dram"] = a
        args.append(nc.dram_tensor(f"in_{name}_dram", a.shape, mybir.dt.from_np(a.dtype), kind="ExternalInput").ap())
    for i, shape in enumerate(_OUTS):
        args.append(nc.dram_tensor(f"out_{i}_dram", shape, F32, kind="ExternalOutput").ap())
    program(nc, *args)
    r = _run(nc, [arrays], core_ids=[0])
    return tuple(r.results[0][f"out_{i}_dram"] for i in range(len(_OUTS)))
```
